# Optimizing a Trainium2 kernel written in Bass

```python
import math
import jax, jax.numpy as jnp
from jax import lax
import numpy as np

D_MODEL = 1024
BATCH = 1
SEQ = 256
DEPTH = 1

CHUNK = 64

HGRN_HEADS = 4
HGRN_DK = 128
HGRN_DV = 128
HGRN_WIDTH = HGRN_HEADS * HGRN_DK
HGRN_VWIDTH = HGRN_HEADS * HGRN_DV
HGRN_BLOCK = 16
HGRN_F_MIN = 1e-30

MLA_HEADS = 4
MLA_Q_RANK = 256
MLA_KV_RANK = 128
MLA_NOPE = 128
MLA_ROPE = 64
MLA_V = 128
MLA_QK = MLA_NOPE + MLA_ROPE
ROPE_THETA = 10000.0
Q_BLOCK = 128
MASK_VALUE = -1e30

S5_GROUPS = 32
S5_GROUP_CH = 16
S5_STATE = 64
S5_WIDTH = S5_GROUPS * S5_GROUP_CH
S5_DT_MIN = 0.001
S5_DT_MAX = 0.1

LRU_WIDTH = 512
LRU_BLOCKS = 8
LRU_BLOCK_W = LRU_WIDTH // LRU_BLOCKS
LRU_CONV = 4
LRU_C = 8.0

N_BRANCH = 4
BRANCH_WIDTH = 512

N_EXPERTS = 32
TOP_K = 4
EXPERT_FF = 1024
SWIGLU_ALPHA = 1.702
SWIGLU_LIMIT = 7.0
EXPERT_BLOCK = 256

DEEPNORM_ALPHA = (2.0 * DEPTH) ** 0.25
DEEPNORM_BETA = (8.0 * DEPTH) ** -0.25
LN_EPS = 1e-5
RMS_EPS = 1e-6

IN_SPLITS = (HGRN_WIDTH, HGRN_WIDTH, HGRN_VWIDTH, HGRN_VWIDTH,
             MLA_Q_RANK, MLA_KV_RANK + MLA_ROPE,
             S5_WIDTH,
             LRU_WIDTH, LRU_WIDTH,
             N_BRANCH * D_MODEL)
D_IN = sum(IN_SPLITS)
IN_OFFSETS = tuple(int(v) for v in np.cumsum(IN_SPLITS)[:-1])

kernel_name = 'hybrid_streaming_encoder_block'

def layer_norm(x, w, b):
    xf = x.astype(jnp.float32)
    xc = xf - jnp.mean(xf, axis=-1, keepdims=True)
    var = jnp.mean(xc * xc, axis=-1, keepdims=True)
    return (xc * lax.rsqrt(var + LN_EPS) * w + b).astype(x.dtype)

def rms_norm(x, w):
    xf = x.astype(jnp.float32)
    ms = jnp.mean(xf * xf, axis=-1, keepdims=True)
    return (xf * lax.rsqrt(ms + RMS_EPS) * w).astype(x.dtype)

def linear_recurrence_combine(left, right):
    a_l, b_l = left
    a_r, b_r = right
    return a_l * a_r, a_r * b_l + b_r

def hgrn2_mixer(q_raw, f_raw, i_raw, g_raw, lb, norm_w):
    bsz, seq, _ = q_raw.shape
    f32 = jnp.float32
    nb = seq // HGRN_BLOCK
    lb = lb.astype(f32)
    z = f_raw.astype(f32)
    q = jax.nn.silu(q_raw.astype(f32))
    log_f = jnp.log(jnp.maximum(lb + (1.0 - lb) * jax.nn.sigmoid(z), HGRN_F_MIN))
    k = (1.0 - lb) * jax.nn.sigmoid(-z)
    v = i_raw.astype(f32)

    def to_blocks(t, d):
        return t.reshape(bsz, nb, HGRN_BLOCK, HGRN_HEADS, d).transpose(1, 0, 3, 2, 4)

    q, k, log_f = to_blocks(q, HGRN_DK), to_blocks(k, HGRN_DK), to_blocks(log_f, HGRN_DK)
    v = to_blocks(v, HGRN_DV)
    b = jnp.cumsum(log_f, axis=3)
    b_last = b[..., HGRN_BLOCK - 1:HGRN_BLOCK, :]
    q_inter = q * jnp.exp(b)
    k_state = k * jnp.exp(b_last - b)
    decay = jnp.exp(b_last[..., 0, :])
    causal = jnp.tril(jnp.ones((HGRN_BLOCK, HGRN_BLOCK), dtype=bool))[:, :, None]

    def block_step(state, xs):
        q_c, k_c, v_c, b_c, qi_c, ks_c, d_c = xs
        diff = b_c[:, :, :, None, :] - b_c[:, :, None, :, :]
        w = jnp.where(causal, jnp.exp(jnp.where(causal, diff, 0.0)), 0.0)
        scores = jnp.einsum('bhtd,bhsd,bhtsd->bhts', q_c, k_c, w)
        o_c = jnp.einsum('bhts,bhsv->bhtv', scores, v_c) + jnp.einsum('bhtd,bhdv->bhtv', qi_c, state)
        state = state * d_c[..., None] + jnp.einsum('bhsd,bhsv->bhdv', ks_c, v_c)
        return state, o_c

    state0 = jnp.zeros((bsz, HGRN_HEADS, HGRN_DK, HGRN_DV), f32)
    _, o = lax.scan(block_step, state0, (q, k, v, b, q_inter, k_state, decay))
    o = rms_norm(o, norm_w.astype(f32).reshape(HGRN_HEADS, 1, HGRN_DV))
    o = o.transpose(1, 0, 3, 2, 4).reshape(bsz, seq, HGRN_VWIDTH)
    return (o * jax.nn.silu(g_raw.astype(f32))).astype(q_raw.dtype)

def rope_cos_sin(positions):
    inv_freq = ROPE_THETA ** (-jnp.arange(0, MLA_ROPE, 2, dtype=jnp.float32) / MLA_ROPE)
    ang = positions.astype(jnp.float32)[..., None] * inv_freq
    return jnp.cos(ang), jnp.sin(ang)

def apply_rope(x, cos, sin):
    x1, x2 = jnp.split(x.astype(jnp.float32), 2, axis=-1)
    return jnp.concatenate([x1 * cos - x2 * sin, x2 * cos + x1 * sin], axis=-1).astype(x.dtype)

def mla_mixer(cq_raw, ckv_raw, positions, q_norm_w, wq_b, kv_norm_w, wkv_b):
    bsz, seq, _ = cq_raw.shape
    q = (rms_norm(cq_raw, q_norm_w) @ wq_b).reshape(bsz, seq, MLA_HEADS, MLA_QK)
    c_kv = rms_norm(ckv_raw[..., :MLA_KV_RANK], kv_norm_w)
    kv = (c_kv @ wkv_b).reshape(bsz, seq, MLA_HEADS, MLA_NOPE + MLA_V)
    k_nope, v = kv[..., :MLA_NOPE], kv[..., MLA_NOPE:]
    cos, sin = rope_cos_sin(positions)
    q_pe = apply_rope(q[..., MLA_NOPE:], cos[:, :, None, :], sin[:, :, None, :])
    k_pe = apply_rope(ckv_raw[..., MLA_KV_RANK:], cos, sin)
    q = jnp.concatenate([q[..., :MLA_NOPE], q_pe], axis=-1)
    k = jnp.concatenate([k_nope, jnp.broadcast_to(k_pe[:, :, None, :], (bsz, seq, MLA_HEADS, MLA_ROPE))], axis=-1)
    nqb = seq // Q_BLOCK
    q_blocks = q.reshape(bsz, nqb, Q_BLOCK, MLA_HEADS, MLA_QK).transpose(1, 0, 2, 3, 4)
    key_chunk = jnp.arange(seq) // CHUNK
    scale = MLA_QK ** -0.5

    def attend_block(args):
        q_blk, blk = args
        q_chunk = (blk * Q_BLOCK + jnp.arange(Q_BLOCK)) // CHUNK
        s = jnp.einsum('bqhd,bkhd->bhqk', q_blk, k).astype(jnp.float32) * scale
        s = jnp.where(key_chunk[None, :] <= q_chunk[:, None], s, MASK_VALUE)
        p = jax.nn.softmax(s, axis=-1).astype(v.dtype)
        return jnp.einsum('bhqk,bkhv->bqhv', p, v)

    o = lax.map(attend_block, (q_blocks, jnp.arange(nqb)))
    return o.transpose(1, 0, 2, 3, 4).reshape(bsz, seq, MLA_HEADS * MLA_V)

def s5_mixer(u_raw, a_re, a_im, log_dt, b_re, b_im, c_re, c_im, d_skip, w_glu, b_glu):
    bsz, seq, _ = u_raw.shape
    f32 = jnp.float32
    u = u_raw.astype(f32).reshape(bsz, seq, S5_GROUPS, S5_GROUP_CH)
    lam = lax.complex(a_re.astype(f32), a_im.astype(f32))
    dt = jnp.exp(log_dt.astype(f32))[:, None]
    lam_bar = jnp.exp(lam * dt)
    b_bar = ((lam_bar - 1.0) / lam)[..., None] * lax.complex(b_re.astype(f32), b_im.astype(f32))
    c_mat = lax.complex(c_re.astype(f32), c_im.astype(f32))
    bu = jnp.einsum('gnc,bsgc->bsgn', b_bar, u.astype(jnp.complex64))
    a_seq = jnp.broadcast_to(lam_bar[None, None], (1, seq, S5_GROUPS, S5_STATE))
    _, states = lax.associative_scan(linear_recurrence_combine, (a_seq, bu), axis=1)
    y = jnp.einsum('gcn,bsgn->bsgc', c_mat, states).real + d_skip.astype(f32) * u
    y = jax.nn.gelu(y.reshape(bsz, seq, S5_WIDTH))
    y = y * jax.nn.sigmoid(y @ w_glu.astype(f32) + b_glu.astype(f32))
    return y.astype(u_raw.dtype)

def rglru_mixer(x_raw, gate_raw, conv_w, conv_b, wa, ba, wx, bx, a_param):
    bsz, seq, width = x_raw.shape
    f32 = jnp.float32
    xc = lax.conv_general_dilated(x_raw, conv_w.astype(x_raw.dtype)[:, None, :], window_strides=(1,),
                                  padding=[(LRU_CONV - 1, 0)], dimension_numbers=('NWC', 'WIO', 'NWC'),
                                  feature_group_count=width) + conv_b
    xb = xc.reshape(bsz, seq, LRU_BLOCKS, LRU_BLOCK_W)
    r = jax.nn.sigmoid(jnp.einsum('bshi,hij->bshj', xb, wa).reshape(bsz, seq, width).astype(f32) + ba)
    i = jax.nn.sigmoid(jnp.einsum('bshi,hij->bshj', xb, wx).reshape(bsz, seq, width).astype(f32) + bx)
    log_a = -LRU_C * r * jax.nn.softplus(a_param.astype(f32))
    a = jnp.exp(log_a)
    b = jnp.sqrt(jnp.maximum(-jnp.expm1(2.0 * log_a), 0.0)) * (i * xc.astype(f32))
    _, h = lax.associative_scan(linear_recurrence_combine, (a, b), axis=1)
    return (h * jax.nn.gelu(gate_raw.astype(f32))).astype(x_raw.dtype)

def clamped_swiglu(h):
    glu, lin = jnp.split(h, 2, axis=-1)
    glu = jnp.minimum(glu, SWIGLU_LIMIT)
    lin = jnp.clip(lin, -SWIGLU_LIMIT, SWIGLU_LIMIT)
    return glu * jax.nn.sigmoid(SWIGLU_ALPHA * glu) * (lin + 1.0)

def moe_ffn(x, router_w, router_b, w1, b1, w2, b2):
    bsz, seq, d = x.shape
    n = bsz * seq
    xt = x.reshape(n, d)
    logits = (xt @ router_w + router_b).astype(jnp.float32)
    top_val, top_idx = lax.top_k(logits, TOP_K)
    top_w = jax.nn.softmax(top_val, axis=-1)
    nk = n * TOP_K
    expert_flat = top_idx.reshape(nk)
    token_flat = jnp.arange(nk, dtype=jnp.int32) // TOP_K
    weight_flat = top_w.reshape(nk)
    counts = jnp.bincount(expert_flat, length=N_EXPERTS)
    padded = ((counts + EXPERT_BLOCK - 1) // EXPERT_BLOCK) * EXPERT_BLOCK
    p_end = jnp.cumsum(padded)
    p_start = p_end - padded
    u_start = jnp.cumsum(counts) - counts
    order = jnp.argsort(expert_flat)
    e_sorted = expert_flat[order]
    dest = p_start[e_sorted] + (jnp.arange(nk, dtype=jnp.int32) - u_start[e_sorted])
    n_slots = nk + N_EXPERTS * EXPERT_BLOCK
    n_blocks = n_slots // EXPERT_BLOCK
    slot_token = jnp.full((n_slots,), n, dtype=jnp.int32).at[dest].set(token_flat[order])
    slot_w = jnp.zeros((n_slots,), jnp.float32).at[dest].set(weight_flat[order])
    block_expert = jnp.minimum(
        jnp.searchsorted(p_end, jnp.arange(n_blocks, dtype=jnp.int32) * EXPERT_BLOCK, side='right'),
        N_EXPERTS - 1)
    x_pad = jnp.concatenate([xt, jnp.zeros((1, d), xt.dtype)], axis=0)
    x_slots = x_pad[slot_token].reshape(n_blocks, EXPERT_BLOCK, d)

    def expert_block(args):
        xb, e = args
        return clamped_swiglu(xb @ w1[e] + b1[e]) @ w2[e] + b2[e]

    y_slots = lax.map(expert_block, (x_slots, block_expert)).reshape(n_slots, d)
    out = jnp.zeros((n + 1, d), jnp.float32).at[slot_token].add(y_slots.astype(jnp.float32) * slot_w[:, None])
    return out[:n].reshape(bsz, seq, d).astype(x.dtype)

def hybrid_layer(x, positions, lb, w_in, b_gate, hgrn_norm_w,
                 mla_q_norm_w, mla_wq_b, mla_kv_norm_w, mla_wkv_b,
                 s5_a_re, s5_a_im, s5_log_dt, s5_b_re, s5_b_im, s5_c_re, s5_c_im, s5_d, s5_w_glu, s5_b_glu,
                 lru_conv_w, lru_conv_b, lru_wa, lru_ba, lru_wx, lru_bx, lru_a_param,
                 w_branch, w_out, ln1_w, ln1_b, ln2_w, ln2_b,
                 router_w, router_b, moe_w1, moe_b1, moe_w2, moe_b2):
    bsz, seq, _ = x.shape
    proj = x @ w_in
    hq, hf, hi, hg, cq, ckv, su, lx, lg, gl = jnp.split(proj, IN_OFFSETS, axis=-1)
    y_a = hgrn2_mixer(hq, hf, hi, hg, lb, hgrn_norm_w)
    y_b = mla_mixer(cq, ckv, positions, mla_q_norm_w, mla_wq_b, mla_kv_norm_w, mla_wkv_b)
    y_c = s5_mixer(su, s5_a_re, s5_a_im, s5_log_dt, s5_b_re, s5_b_im, s5_c_re, s5_c_im, s5_d, s5_w_glu, s5_b_glu)
    y_d = rglru_mixer(lx, lg, lru_conv_w, lru_conv_b, lru_wa, lru_ba, lru_wx, lru_bx, lru_a_param)
    branches = jnp.stack([y_a.astype(x.dtype), y_b.astype(x.dtype), y_c.astype(x.dtype), y_d.astype(x.dtype)], axis=2)
    branch_out = jnp.einsum('bsnw,nwd->bsnd', branches, w_branch)
    gates = jax.nn.sigmoid(gl.reshape(bsz, seq, N_BRANCH, D_MODEL) + b_gate)
    mix = jnp.sum(gates * branch_out, axis=2) @ w_out
    h = layer_norm(DEEPNORM_ALPHA * x + mix, ln1_w, ln1_b)
    ffn = moe_ffn(h, router_w, router_b, moe_w1, moe_b1, moe_w2, moe_b2)
    return layer_norm(DEEPNORM_ALPHA * h + ffn, ln2_w, ln2_b)

def setup_inputs(seed: int = 0) -> dict:
    key = jax.random.key(seed)
    ks = jax.random.split(key, 40)
    f32 = jnp.float32
    L = DEPTH

    def nrm(k, shape, scale):
        return jax.random.normal(k, shape, f32) * scale

    x = nrm(ks[0], (BATCH, SEQ, D_MODEL), 1.0)
    offsets = jax.random.randint(ks[1], (BATCH, 1), 0, 4 * SEQ, dtype=jnp.int32)
    positions = offsets + jnp.arange(SEQ, dtype=jnp.int32)[None, :]
    u_a = jax.random.uniform(ks[26], (L, LRU_WIDTH), f32, 0.9, 0.999)
    return {
        'x': x,
        'positions': positions,
        'w_in': nrm(ks[2], (L, D_MODEL, D_IN), D_MODEL ** -0.5),
        'b_gate': nrm(ks[3], (L, N_BRANCH, D_MODEL), 0.02),
        'hgrn_lb_logits': 1.0 + nrm(ks[4], (L, HGRN_WIDTH), 0.1),
        'hgrn_norm_w': 1.0 + nrm(ks[5], (L, HGRN_VWIDTH), 0.02),
        'mla_q_norm_w': 1.0 + nrm(ks[6], (L, MLA_Q_RANK), 0.02),
        'mla_wq_b': nrm(ks[7], (L, MLA_Q_RANK, MLA_HEADS * MLA_QK), MLA_Q_RANK ** -0.5),
        'mla_kv_norm_w': 1.0 + nrm(ks[8], (L, MLA_KV_RANK), 0.02),
        'mla_wkv_b': nrm(ks[9], (L, MLA_KV_RANK, MLA_HEADS * (MLA_NOPE + MLA_V)), MLA_KV_RANK ** -0.5),
        's5_a_re': -0.5 + nrm(ks[10], (L, S5_GROUPS, S5_STATE), 0.01),
        's5_a_im': jnp.tile(jnp.pi * jnp.arange(S5_STATE, dtype=f32), (L, S5_GROUPS, 1)),
        's5_log_dt': jax.random.uniform(ks[11], (L, S5_GROUPS), f32, math.log(S5_DT_MIN), math.log(S5_DT_MAX)),
        's5_b_re': nrm(ks[12], (L, S5_GROUPS, S5_STATE, S5_GROUP_CH), (2.0 * S5_GROUP_CH) ** -0.5),
        's5_b_im': nrm(ks[13], (L, S5_GROUPS, S5_STATE, S5_GROUP_CH), (2.0 * S5_GROUP_CH) ** -0.5),
        's5_c_re': nrm(ks[14], (L, S5_GROUPS, S5_GROUP_CH, S5_STATE), (2.0 * S5_STATE) ** -0.5),
        's5_c_im': nrm(ks[15], (L, S5_GROUPS, S5_GROUP_CH, S5_STATE), (2.0 * S5_STATE) ** -0.5),
        's5_d': nrm(ks[16], (L, S5_GROUPS, S5_GROUP_CH), 1.0),
        's5_w_glu': nrm(ks[17], (L, S5_WIDTH, S5_WIDTH), S5_WIDTH ** -0.5),
        's5_b_glu': nrm(ks[18], (L, S5_WIDTH), 0.02),
        'lru_conv_w': nrm(ks[19], (L, LRU_CONV, LRU_WIDTH), LRU_CONV ** -0.5),
        'lru_conv_b': nrm(ks[20], (L, LRU_WIDTH), 0.02),
        'lru_wa': nrm(ks[21], (L, LRU_BLOCKS, LRU_BLOCK_W, LRU_BLOCK_W), LRU_BLOCK_W ** -0.5),
        'lru_ba': nrm(ks[22], (L, LRU_WIDTH), 0.02),
        'lru_wx': nrm(ks[23], (L, LRU_BLOCKS, LRU_BLOCK_W, LRU_BLOCK_W), LRU_BLOCK_W ** -0.5),
        'lru_bx': nrm(ks[24], (L, LRU_WIDTH), 0.02),
        'lru_a_param': jnp.log(jnp.expm1(-jnp.log(u_a) / LRU_C)),
        'w_branch': nrm(ks[25], (L, N_BRANCH, BRANCH_WIDTH, D_MODEL), DEEPNORM_BETA * BRANCH_WIDTH ** -0.5),
        'w_out': nrm(ks[27], (L, D_MODEL, D_MODEL), DEEPNORM_BETA * D_MODEL ** -0.5),
        'ln1_w': 1.0 + nrm(ks[28], (L, D_MODEL), 0.02),
        'ln1_b': nrm(ks[29], (L, D_MODEL), 0.02),
        'ln2_w': 1.0 + nrm(ks[30], (L, D_MODEL), 0.02),
        'ln2_b': nrm(ks[31], (L, D_MODEL), 0.02),
        'router_w': nrm(ks[32], (L, D_MODEL, N_EXPERTS), D_MODEL ** -0.5),
        'router_b': nrm(ks[33], (L, N_EXPERTS), 0.01),
        'moe_w1': nrm(ks[34], (L, N_EXPERTS, D_MODEL, 2 * EXPERT_FF), DEEPNORM_BETA * D_MODEL ** -0.5),
        'moe_b1': nrm(ks[35], (L, N_EXPERTS, 2 * EXPERT_FF), 0.01),
        'moe_w2': nrm(ks[36], (L, N_EXPERTS, EXPERT_FF, D_MODEL), DEEPNORM_BETA * EXPERT_FF ** -0.5),
        'moe_b2': nrm(ks[37], (L, N_EXPERTS, D_MODEL), 0.01),
    }

def reference(x, positions, w_in, b_gate, hgrn_lb_logits, hgrn_norm_w,
              mla_q_norm_w, mla_wq_b, mla_kv_norm_w, mla_wkv_b,
              s5_a_re, s5_a_im, s5_log_dt, s5_b_re, s5_b_im, s5_c_re, s5_c_im, s5_d, s5_w_glu, s5_b_glu,
              lru_conv_w, lru_conv_b, lru_wa, lru_ba, lru_wx, lru_bx, lru_a_param,
              w_branch, w_out, ln1_w, ln1_b, ln2_w, ln2_b,
              router_w, router_b, moe_w1, moe_b1, moe_w2, moe_b2):
    probs = jax.nn.softmax(hgrn_lb_logits.astype(jnp.float32), axis=0)
    lower_bounds = jnp.cumsum(probs, axis=0) - probs[0:1]
    for l in range(DEPTH):
        x = hybrid_layer(x, positions, lower_bounds[l], w_in[l], b_gate[l], hgrn_norm_w[l],
                         mla_q_norm_w[l], mla_wq_b[l], mla_kv_norm_w[l], mla_wkv_b[l],
                         s5_a_re[l], s5_a_im[l], s5_log_dt[l], s5_b_re[l], s5_b_im[l], s5_c_re[l], s5_c_im[l],
                         s5_d[l], s5_w_glu[l], s5_b_glu[l],
                         lru_conv_w[l], lru_conv_b[l], lru_wa[l], lru_ba[l], lru_wx[l], lru_bx[l], lru_a_param[l],
                         w_branch[l], w_out[l], ln1_w[l], ln1_b[l], ln2_w[l], ln2_b[l],
                         router_w[l], router_b[l], moe_w1[l], moe_b1[l], moe_w2[l], moe_b2[l])
    return x


_drawn_inputs = setup_inputs


def setup_inputs(seed=0):
    import zlib

    import numpy as np

    out = dict(_drawn_inputs(seed))
    spreads = {}
    factors = {'b_gate': 8.0,
     'hgrn_norm_w': 36.135,
     'mla_q_norm_w': 8.0,
     'mla_kv_norm_w': 8.0,
     's5_a_re': 64.0,
     's5_a_im': 64.0,
     's5_log_dt': 64.0,
     's5_b_re': 64.0,
     's5_b_im': 64.0,
     's5_c_re': 64.0,
     's5_c_im': 64.0,
     's5_w_glu': 17.733,
     's5_b_glu': 200.0,
     'lru_conv_b': 50.512,
     'lru_wa': 23.096,
     'lru_ba': 64.0,
     'lru_bx': 64.0,
     'lru_a_param': 24.472,
     'ln1_b': 2.808,
     'ln2_w': 21.094,
     'ln2_b': 22.159,
     'router_b': 8.0,
     'moe_b1': 26.695,
     'moe_b2': 8.0,
     'lru_conv_w': 8.0,
     'lru_wx': 8.0,
     's5_d': 3.059}
    for name, (base, spread) in spreads.items():
        noise = np.random.default_rng([zlib.crc32(name.encode()), seed]).standard_normal(out[name].shape)
        drawn = base * np.exp(spread * noise) if base else spread * noise
        out[name] = __import__('jax').numpy.asarray(drawn.astype(out[name].dtype))
    for name, factor in factors.items():
        out[name] = (out[name] * factor).astype(out[name].dtype)
    return out
```

```python
from contextlib import ExitStack

import numpy as np

import concourse.bass as bass
from concourse import mybir

ALU = mybir.AluOpType
ACT = mybir.ActivationFunctionType
F32 = mybir.dt.float32
I32 = mybir.dt.int32
U32 = mybir.dt.uint32
X = mybir.AxisListType.X

P = 128
SEQ = 256
D = 1024
KD = D // P
TH = SEQ // P
HEADS = 4
BLK = 16
NBLK = SEQ // BLK
HB = HEADS * NBLK
Q_RANK, KV_RANK, NOPE, ROPE, VD = 256, 128, 128, 64, 128
QK = NOPE + ROPE
R2 = ROPE // 2
CHUNK = 64
MASK_VALUE = -1e30
SM = float(QK) ** -0.5
S5T = 16
NBR = 4
BW = 512
NE = 32
TOPK = 4
FF = 1024
CAP = 64
NITEM = SEQ * TOPK // CAP
ALPHA = 2.0 ** 0.25
LN_EPS, RMS_EPS = 1e-5, 1e-6
F_MIN = 1e-30
LIMIT, SWA = 7.0, 1.702
TWO_PI = 2.0 * np.pi
INV2PI = float(np.float32(1.0 / TWO_PI))
MAGIC = 12582912.0
C1 = 6.28125
C2 = float(np.float32(TWO_PI - C1))
C3 = float(TWO_PI - C1 - np.float64(np.float32(TWO_PI - C1)))
PI_LOW = 3.1415925
TWO_PI_LOW = 6.2831850

HQ, HF, HI, HG, CQ, CKV, SU, LX, LG, GL = 0, 512, 1024, 1536, 2048, 2304, 2496, 3008, 3520, 4032
CW = 256
SLOT = 2048
R1 = 8
R2S = 12

VR = {}
_at = 0
for _name, _n in (("a_re", 16), ("a_im", 16), ("hnorm", 4), ("qnorm", 2), ("kvnorm", 1), ("dskip", 4), ("bglu", 4),
                  ("convw", 16), ("convb", 4), ("ba", 4), ("bx", 4), ("apar", 4), ("lb", 4), ("bgate", 32)):
    VR[_name] = _at
    _at += _n
NVEC = _at


def weight_stream():
    s = [("lx", 0), ("lx", 1), ("su", 0), ("su", 1), ("lg", 0), ("lg", 1), ("cq", 0)]
    for h in range(8):
        s += [("gl", 2 * h), ("gl", 2 * h + 1)]
    s += [("wglu", 0), ("ckv", 0), ("wq", 0), ("wkv", 0)]
    s += [("hf", 0), ("hf", 1), ("hq", 0), ("hq", 1)]
    s += [("wb", 3, 0), ("wb", 3, 1), ("wb", 2, 0), ("wb", 2, 1)]
    s += [("hi", 0), ("hi", 1), ("hg", 0), ("hg", 1)]
    s += [("wb", 1, 0), ("wb", 1, 1), ("wb", 0, 0), ("wb", 0, 1)]
    s += [("wo", i) for i in range(4)]
    return s


COL = {"lx": LX, "lg": LG, "su": SU, "cq": CQ, "ckv": CKV, "gl": GL, "hf": HF, "hq": HQ, "hi": HI, "hg": HG}
STREAM = weight_stream()
PROJ = [c for c in STREAM if c[0] in COL]
NPAIR = NE // 2


def encoder_layer(nc, A, out, dbg=None):
    with ExitStack() as ctx:
        def sb(name, shape, dt=F32):
            return ctx.enter_context(nc.sbuf_tensor(name, shape, dt))

        def sem(name):
            return ctx.enter_context(nc.semaphore(name))

        banks = ctx.enter_context(nc.psum_tensor("banks", [P, 8, 512], F32))
        bank = [banks[:, i, :] for i in range(8)]

        ring = sb("ring", [P, R2S * SLOT])
        merge_gate = ring[:, R1 * SLOT:].rearrange("p (c t) -> p c t", t=SEQ)
        ident = sb("ident", [P, P])
        ones = sb("ones", [P, P])
        ones_128 = sb("ones_128", [P, P])
        ones_256 = sb("ones_256", [P, P])
        earlier = sb("earlier", [P, P])
        blockmask = sb("blockmask", [P, 8])
        headmask = sb("headmask", [P, HEADS])
        oddmask = sb("oddmask", [P, 2])
        half_pi = sb("half_pi", [P, 1])
        iota_i = sb("iota_i", [P, SEQ], I32)
        iota = sb("iota", [P, SEQ])
        vec = sb("vec", [P, NVEC])
        small = sb("small", [P, 512])
        acc = sb("acc", [P, KD, SEQ])
        yT = sb("yT", [P, NBR, HEADS, SEQ])
        xT = sb("xT", [P, KD, SEQ])
        ARENA = 16912
        arena = sb("arena", [P, ARENA])

        def at(off, *shape):
            n = int(np.prod(shape))
            assert off + n <= ARENA, (off, shape, ARENA)
            v = arena[:, off:off + n]
            if len(shape) == 1:
                return v
            names = "abcd"[:len(shape)]
            return v.rearrange(f"p ({' '.join(names)}) -> p {' '.join(names)}", **dict(zip(names[1:], shape[1:])))

        class At:
            def __init__(self, base):
                self.o = base

            def __call__(self, *shape):
                v = at(self.o, *shape)
                self.o += int(np.prod(shape))
                return v

        m = At(0)
        su = m(4, SEQ)
        s_raw = m(4, 256)
        b_exp = m(2, 16, 32)
        c_exp = m(2, 4, 128)
        bT = m(2, 4, 128)
        cT = m(2, 4, 128)
        sinT, cosT = [None, None], [None, None]
        for i in range(2):
            sinT[i], cosT[i] = m(4, SEQ), m(4, SEQ)
        t1, t2 = m(2, SEQ), m(2, SEQ)
        s5_end = m.o
        xr = [at(1024, 2, SEQ), at(2048, 2, SEQ)]
        xi = [at(1536, 2, SEQ), at(2560, 2, SEQ)]
        zr, zi = at(3072, 2, SEQ), at(3584, 2, SEQ)
        s_out = yT[:, 1]
        lx = m(4, SEQ + 4)
        xc = m(4, SEQ)
        lr_r = m(4, SEQ)
        lr_i = m(4, SEQ)
        lr_t = m(4, SEQ)
        lr_g = yT[:, 3]
        cq_s = m(2, SEQ)
        m = At(0)
        hg_f, hg_q, hg_k = m(4 * SEQ), m(4 * SEQ), m(4 * SEQ)
        grow = m(HB, BLK)
        decay = m(HB, 1)
        prod = [m(HB, BLK), m(HB, BLK)]
        q_inter = m(4 * SEQ)
        hg_kT = hg_f.rearrange("p (a b) -> p a b", a=8)
        hg_bd = hg_q.rearrange("p (a b) -> p a b", a=8)
        second = m.o
        hg_v, hg_g = m(2, 512), m(4 * SEQ)
        v_exp = [m(8, P), m(8, P)]
        state = m(NBLK, P)
        hg_o, hg_sq, hg_rs = m(SEQ), m(SEQ), m(SEQ)
        hg_end = m.o
        m = At(second)
        cq = m(2, SEQ)
        ckv = m(SEQ)
        sq = m(3, SEQ)
        rst = m(2, SEQ)
        qn = m(4, SEQ)
        kn = m(4, SEQ)
        vv = m(2, 512)
        rp1, rp2 = m(2, SEQ), m(2, SEQ)
        tA, tB = m(2, SEQ), m(2, SEQ)
        m_tmp = at(max(m.o, hg_end), 512)
        wa = sb("wa", [P, 4, P])
        wx = sb("wx", [P, 4, P])
        cos_p, sin_p = wa[:, 0:2, :].rearrange("p a b -> p (a b)"), wa[:, 2:4, :].rearrange("p a b -> p (a b)")
        ang = wx[:, 0:2, :].rearrange("p a b -> p (a b)")
        ang2 = wx[:, 2:4, :].rearrange("p a b -> p (a b)")
        qm1 = acc[:, 0:4, :]
        qm2 = acc[:, 4:8, :]
        probs = [rst[:, i, :] for i in range(2)]
        probsT = [sq.rearrange("p a b -> p (a b)")[:, i * SEQ:(i + 1) * SEQ].rearrange("p (a b) -> p a b", a=2) for i in range(2)]
        rows = sb("rows", [P, P])
        inv_freq = sb("inv_freq", [P, 1])
        pos_i = iota_i
        x_tok = acc[:, :, :].rearrange("p (h k) t -> p h (k t)", h=2)
        m = At(0)
        h_tok = m(2, D)
        y_acc = m(2, D)
        ln_w, ln_b = m(D), m(D)
        b1_all = m(2 * FF)
        xg = m(KD, CAP)
        g1, g2, g3 = m(512), m(512), m(512)
        actT = m(4, P)
        y_pair = m(D)
        wselT = m(2, P)
        hT = xT
        sel = m(2, CAP)
        wsel = m(2, P)
        esel = m(CAP)
        logits = m(2, NE)
        wfull, rank = m(2, NE + 1), m(2, NE + 1)
        member = m(2, NE)
        oneh = m(NE)
        top = m(2, 8)
        b2_all = m(D)
        wTd = m(2, P)
        rb = m(NE)
        rw = m(KD, NE)
        cmp = m(NITEM, 96)
        item_off = m(NITEM)
        item_ef = m(NITEM)
        cand = m(3, 96)
        top_i = sb("top_i", [P, 2, 8], U32)
        item_e = sb("item_e", [1, 32], I32)
        x_res = y_acc

        landed = [sem(f"landed{i}") for i in range(R2S)]
        names = """chunk_used const_ready iota_ready iota_read x_in vec_in dt_in s5_in lru_in pos_in xT_psum xT_vec xT_act vec_psum vec_ready
            dt_rows dt_exp s5_small s5_mag s5_theta s5_trig0 exp_ready prep_psum prep_evac f_ready trig_ready bu_psum bu_free x_ready x_used
            y_evac gelu_ready glu_psum glu_gate yC_ready proj_evac xc_ready gate_psum gate_act absa_ready expa_ready sp_ready
            lru_exp lru_b2 lru_sqrt yD_ready cos_req cos_ready sq_ready ss_psum norm_ready mla_psum mla_evac mla_masked
            s_psum smax_ready sexp_ready p_norm pT_psum pT_ready o_psum o_evac lbe_req lbe_ready g_ready p_ready p_used hgT_psum kT_ready bd_ready
            vx_ready u_psum u_used st_ready ho_psum ho_evac hss_psum yA_ready merge_psum merge_used merge_done xres_in ln_in h_ready
            hT_psum hT_act rw_in logit_psum rs_req rs_ready rb_in b_in b_clear topexp_req topexp_ready route_ready rank_psum wT_psum wT_ready b2_psum b2_used
            sel_ready xg_psum xg_ready expert_chunk_used gmin_ready sig_ready act_ready at_psum at_ready ypair_vec ypair_act
            wselT_psum wselT_ready comb_psum comb_used ln2_in out_ready out_sent v_chain f_chain a_chain g_chain items_ready
            """.split()
        S = {n: sem(n) for n in names}

        def v_(name, i=0, n=1):
            return vec[:, VR[name] + i:VR[name] + i + n]

        slot_of = {c: i % R1 for i, c in enumerate(STREAM)}
        uses = [0] * R2S
        need = {}
        for i, c in enumerate(STREAM):
            uses[i % R1] += 1
            need[c] = 16 * uses[i % R1]
        last_in_slot = [max(i for i in range(len(STREAM)) if i % R1 == s) for s in range(R1)]

        def slot(s, *shape):
            n = int(np.prod(shape))
            v = ring[:, s * SLOT:s * SLOT + n]
            names = "abcd"[:len(shape)]
            return v.rearrange(f"p ({' '.join(names)}) -> p {' '.join(names)}", **dict(zip(names[1:], shape[1:])))

        w_in = A["w_in"].rearrange("(k p) n -> p k n", p=P)
        w1 = A["moe_w1"]
        w2 = A["moe_w2"]

        def chunk_source(c):
            if c[0] in COL:
                lo = COL[c[0]] + CW * c[1]
                w = 192 if c[0] == "ckv" else CW
                return (KD, w), w_in[:, :, lo:lo + w]
            if c[0] == "wglu":
                return (4, 512), A["s5_w_glu"].rearrange("(k p) n -> p k n", p=P)
            if c[0] == "wq":
                return (2, 768), A["mla_wq_b"].rearrange("(k p) n -> p k n", p=P)
            if c[0] == "wkv":
                return (1, 1024), A["mla_wkv_b"].rearrange("(k p) n -> p k n", p=P)
            if c[0] == "wb":
                return (4, 512), A["w_branch"][c[1]].rearrange("(k p) n -> p k n", p=P)[:, :, 512 * c[2]:512 * c[2] + 512]
            return (2, D), A["w_out"][256 * c[1]:256 * c[1] + 256, :].rearrange("(k p) n -> p k n", p=P)

        block = ctx.enter_context(nc.Block())

        def expert_source(e, c):
            if c < 8:
                return w1[e, P * c:P * c + P, :]
            return w2[e, 256 * (c - 8):256 * (c - 8) + 256, :].rearrange("(k p) n -> p k n", p=P)

        def expert_slot(c):
            return slot(c, SLOT) if c < 8 else slot(c, 2, D)

        @block.sync
        def _(sp):
            for i, c in enumerate(STREAM):
                if i >= R1:
                    sp.wait_ge(S["chunk_used"], i - R1 + 1)
                shape, src = chunk_source(c)
                sp.dma_start(slot(i % R1, *shape), src).then_inc(landed[i % R1], 16)
            for c in range(R2S):
                if c < R1:
                    sp.wait_ge(S["chunk_used"], last_in_slot[c] + 1)
                elif c == R1:
                    sp.wait_ge(S["merge_done"], 4)
                sp.dma_start(expert_slot(c), expert_source(0, c)).then_inc(landed[c], 16)
            with sp.Fori(1, NE) as e:
                for c in range(R2S):
                    sp.wait_ge(S["expert_chunk_used"], (e - 1) * R2S + c + 1)
                    sp.dma_start(expert_slot(c), expert_source(e, c)).then_inc(landed[c], 16)
            sp.wait_ge(S["items_ready"], 1)
            n_items = sp.value_load(item_e[0:1, NITEM:NITEM + 1], min_val=0, max_val=NITEM)
            with sp.If(n_items > 0):
                with sp.Fori(0, n_items) as j:
                    e = sp.value_load(item_e[0:1, bass.ds(j, 1)], min_val=0, max_val=NE - 1)
                    for c in range(R2S):
                        sp.wait_ge(S["expert_chunk_used"], (j + NE - 1) * R2S + c + 1)
                        sp.dma_start(expert_slot(c), expert_source(e, c)).then_inc(landed[c], 16)
            sp.wait_ge(S["out_ready"], 1)
            sp.dma_start(out[0].rearrange("(h p) n -> p h n", p=P), y_acc).then_inc(S["out_sent"], 16)
            sp.wait_ge(S["out_sent"], 16)

        @block.gpsimd
        def _(pool):
            g = [0]

            def link(ins):
                g[0] += 1
                ins.then_inc(S["g_chain"], 1)
                pool.wait_ge(S["g_chain"], g[0])

            link(nc.gpsimd.memset(ident[:, :], 0.0))
            link(nc.gpsimd.affine_select(out=ident[:, :], in_=ident[:, :], compare_op=ALU.not_equal, fill=1.0,
                                         base=0, pattern=[[-1, P]], channel_multiplier=1))
            nc.gpsimd.memset(ones[:, :], 1.0).then_inc(S["const_ready"], 1)
            nc.gpsimd.memset(ones_128[:, :], 1.0 / 128).then_inc(S["const_ready"], 1)
            nc.gpsimd.memset(ones_256[:, :], 1.0 / 256).then_inc(S["const_ready"], 1)
            nc.gpsimd.memset(half_pi[:, :], float(np.pi / 2)).then_inc(S["const_ready"], 1)
            nc.gpsimd.memset(rows[:, :], 0.0).then_inc(S["const_ready"], 1)
            nc.gpsimd.iota(iota_i[:, :], pattern=[[1, SEQ]], base=0, channel_multiplier=0).then_inc(S["iota_ready"], 1)
            nc.gpsimd.memset(wa[:, :, :], 0.0).then_inc(S["const_ready"], 1)
            nc.gpsimd.memset(wx[:, :, :], 0.0).then_inc(S["const_ready"], 1)
            link(nc.gpsimd.memset(blockmask[:, :], 1.0))
            link(nc.gpsimd.affine_select(out=blockmask[:, :], in_=blockmask[:, :], compare_op=ALU.is_ge, fill=0.0,
                                         base=0, pattern=[[-16, 8]], channel_multiplier=1))
            link(nc.gpsimd.affine_select(out=blockmask[:, :], in_=blockmask[:, :], compare_op=ALU.is_ge, fill=0.0,
                                         base=15, pattern=[[16, 8]], channel_multiplier=-1))
            link(nc.gpsimd.memset(headmask[:, :], 1.0))
            link(nc.gpsimd.affine_select(out=headmask[:, :], in_=headmask[:, :], compare_op=ALU.is_ge, fill=0.0,
                                         base=0, pattern=[[-32, HEADS]], channel_multiplier=1))
            link(nc.gpsimd.affine_select(out=headmask[:, :], in_=headmask[:, :], compare_op=ALU.is_ge, fill=0.0,
                                         base=31, pattern=[[32, HEADS]], channel_multiplier=-1))
            link(nc.gpsimd.memset(earlier[:, :], 1.0))
            nc.gpsimd.affine_select(out=earlier[:, :], in_=earlier[:, :], compare_op=ALU.is_gt, fill=0.0,
                                    base=0, pattern=[[1, P]], channel_multiplier=-1).then_inc(S["const_ready"], 1)
            pool.wait_ge(S["proj_evac"], PROJ.index(("hi", 1)) + 1)
            for n in range(8):
                h, half = n // 2, n % 2
                if n >= 2:
                    pool.wait_ge(S["u_psum"], 2 * (n - 1))
                nc.gpsimd.tensor_tensor(v_exp[n % 2], hg_v[:, half, h * P:h * P + P].unsqueeze(1).to_broadcast([P, 8, P]),
                                        blockmask[:, :].unsqueeze(2).to_broadcast([P, 8, P]), ALU.mult).then_inc(S["vx_ready"], 1)

        NCONST = 8

        @block.scalar
        def _(act):
            ac = [0]

            def link(ins):
                ac[0] += 1
                ins.then_inc(S["a_chain"], 1)
                act.wait_ge(S["a_chain"], ac[0])

            act.dma_start(x_tok, A["x"][0].rearrange("(h p) n -> p h n", p=P)).then_inc(S["x_in"], 16)
            act.wait_ge(S["const_ready"], 7)
            nvec = 0
            for name, src in (("a_re", "s5_a_re"), ("a_im", "s5_a_im"), ("hnorm", "hgrn_norm_w"), ("qnorm", "mla_q_norm_w"),
                              ("kvnorm", "mla_kv_norm_w"), ("dskip", "s5_d"), ("bglu", "s5_b_glu"), ("convw", "lru_conv_w"),
                              ("convb", "lru_conv_b"), ("ba", "lru_ba"), ("bx", "lru_bx"), ("apar", "lru_a_param"),
                              ("lb", "hgrn_lb_logits"), ("bgate", "b_gate")):
                n = A[src].shape[0]
                act.dma_start(rows[VR[name]:VR[name] + n, :], A[src]).then_inc(S["vec_in"], 16)
                nvec += 1
            assert nvec == 14
            act.dma_start(inv_freq[:, :], A["inv_freq"]).then_inc(S["pos_in"], 16)
            act.dma_start(small[0:S5T, 0:2], A["s5_log_dt"]).then_inc(S["dt_in"], 16)
            for i in range(4):
                for half in range(2):
                    p0 = 64 * half
                    act.dma_start(wa[p0:p0 + 64, i, p0:p0 + 64], A["lru_wa"][2 * i + half]).then_inc(S["lru_in"], 16)
                    act.dma_start(wx[p0:p0 + 64, i, p0:p0 + 64], A["lru_wx"][2 * i + half]).then_inc(S["lru_in"], 16)
            act.dma_start(s_raw[:, 0, :].rearrange("p (a b) -> p a b", a=16), A["s5_b_re"].rearrange("(j q) c -> q j c", q=P)).then_inc(S["s5_in"], 16)
            act.dma_start(s_raw[:, 1, :].rearrange("p (a b) -> p a b", a=16), A["s5_b_im"].rearrange("(j q) c -> q j c", q=P)).then_inc(S["s5_in"], 16)
            act.dma_start(s_raw[:, 2, :].rearrange("p (a b) -> p a b", a=4), A["s5_c_re"].rearrange("(j q) c -> q j c", q=P)).then_inc(S["s5_in"], 16)
            act.dma_start(s_raw[:, 3, :].rearrange("p (a b) -> p a b", a=4), A["s5_c_im"].rearrange("(j q) c -> q j c", q=P)).then_inc(S["s5_in"], 16)

            act.wait_ge(S["iota_read"], 1)
            act.dma_start(pos_i[:, :], A["positions"].to_broadcast([P, SEQ])).then_inc(S["pos_in"], 16)
            proj_n = [0]

            def projected(c):
                i = proj_n[0]
                assert PROJ[i] == c, (PROJ[i], c)
                proj_n[0] += 1
                act.wait_ge(S["chunk_used"], STREAM.index(c) + 1)
                return bank[i % 2]

            def evac_gate(n):
                b = projected(("gl", n))
                for j in range(2):
                    ins = nc.scalar.activation(merge_gate[:, 2 * n + j, :], b[:, j * SEQ:(j + 1) * SEQ], ACT.Sigmoid,
                                               bias=v_("bgate", 2 * n + j))
                ins.then_inc(S["proj_evac"], 1)

            for r in (1, 3):
                act.wait_ge(S["xT_psum"], r + 1)
                nc.scalar.activation(xT[:, 2 * r:2 * r + 2, :].rearrange("p a b -> p (a b)"), bank[3 + r][:, :], ACT.Copy).then_inc(S["xT_act"], 1)
            act.wait_ge(S["vec_ready"], 1)
            for i in range(2):
                b = projected(("lx", i))
                nc.scalar.activation(lx[:, 2 * i:2 * i + 2, 3:3 + SEQ], b[:, :].rearrange("p (a b) -> p a b", a=2), ACT.Copy)\
                    .then_inc(S["proj_evac"], 1)
            act.wait_ge(S["dt_exp"], 1)
            nc.scalar.activation(small[:, 32:48], small[:, 16:32], ACT.Exp).then_inc(S["s5_small"], 1)
            act.wait_ge(S["s5_mag"], 1)
            nc.scalar.activation(small[:, 80:96], small[:, 48:64], ACT.Exp).then_inc(S["s5_small"], 1)
            act.wait_ge(S["absa_ready"], 1)
            nc.scalar.activation(small[:, 364:368], small[:, 360:364], ACT.Exp, scale=-1.0).then_inc(S["expa_ready"], 1)
            act.wait_ge(S["lbe_req"], 1)
            nc.scalar.activation(small[:, 404:408], small[:, 400:404], ACT.Exp).then_inc(S["lbe_ready"], 1)
            act.wait_ge(S["s5_theta"], 1)
            nc.scalar.activation(small[:, 112:144], small[:, 144:176], ACT.Sin).then_inc(S["s5_trig0"], 1)
            for i in range(2):
                b = projected(("su", i))
                nc.scalar.activation(su[:, 2 * i:2 * i + 2, :].rearrange("p a b -> p (a b)"), b[:, :], ACT.Copy).then_inc(S["proj_evac"], 1)
            for i in range(4):
                act.wait_ge(S["gate_psum"], i + 1)
                nc.scalar.activation(lr_r[:, i, :], bank[3 + i][:, 0:SEQ], ACT.Sigmoid, bias=v_("ba", i)).then_inc(S["gate_act"], 1)
                nc.scalar.activation(lr_i[:, i, :], bank[3 + i][:, SEQ:], ACT.Sigmoid, bias=v_("bx", i)).then_inc(S["gate_act"], 1)
            for i in range(2):
                b = projected(("lg", i))
                nc.scalar.activation(lr_g[:, 2 * i:2 * i + 2, :].rearrange("p a b -> p (a b)"), b[:, :], ACT.Gelu_apprx_tanh).then_inc(S["proj_evac"], 1)
            b = projected(("cq", 0))
            nc.scalar.activation(cq_s.rearrange("p a b -> p (a b)"), b[:, :], ACT.Copy).then_inc(S["proj_evac"], 1)
            for i in range(4):
                act.wait_ge(S["prep_psum"], i + 1)
                dst = (bT[:, 0], bT[:, 1], cT[:, 0], cT[:, 1])[i]
                nc.scalar.activation(dst.rearrange("p a b -> p (a b)"), bank[3 + i][:, :], ACT.Copy, scale=-1.0 if i == 3 else 1.0)\
                    .then_inc(S["prep_evac"], 1)

            def trig(q):
                act.wait_ge(S["f_ready"], q + 1)
                s, c = sinT[q % 2].rearrange("p a b -> p (a b)"), cosT[q % 2].rearrange("p a b -> p (a b)")
                nc.scalar.activation(s, s, ACT.Sin, scale=TWO_PI_LOW).then_inc(S["trig_ready"], 1)
                nc.scalar.activation(c, c, ACT.Sin, scale=-TWO_PI_LOW, bias=half_pi[:, 0:1]).then_inc(S["trig_ready"], 1)

            trig(0)
            trig(1)
            act.wait_ge(S["sp_ready"], 1)
            act.wait_ge(S["gate_act"], 8)
            for i in range(4):
                nc.scalar.activation(lr_t[:, i, :], lr_r[:, i, :], ACT.Tanh, scale=small[:, 380 + i:381 + i]).then_inc(S["lru_exp"], 1)
                nc.scalar.activation(lx[:, i, 0:SEQ], lr_r[:, i, :], ACT.Exp, scale=small[:, 384 + i:385 + i]).then_inc(S["lru_exp"], 1)
            act.wait_ge(S["lru_exp"], 8)
            for i in range(4):
                nc.scalar.activation(lr_r[:, i, :], lr_r[:, i, :], ACT.Exp, scale=small[:, 376 + i:377 + i]).then_inc(S["lru_exp"], 1)
            act.wait_ge(S["lru_b2"], 1)
            nc.scalar.activation(lr_t.rearrange("p a b -> p (a b)"), lr_t.rearrange("p a b -> p (a b)"), ACT.Sqrt).then_inc(S["lru_sqrt"], 1)
            for h in range(8):
                if h in (4, 6):
                    trig(h // 2)
                evac_gate(2 * h)
                evac_gate(2 * h + 1)
            act.wait_ge(S["cos_req"], 1)
            nc.scalar.activation(sin_p, ang, ACT.Sin).then_inc(S["cos_ready"], 1)
            nc.scalar.activation(cos_p, ang2, ACT.Sin).then_inc(S["cos_ready"], 1)
            def root(v, nth):
                act.wait_ge(S["rs_req"], nth)
                nc.scalar.activation(v, v, ACT.Sqrt).then_inc(S["rs_ready"], 1)

            act.wait_ge(S["y_evac"], 4)
            act.wait_ge(S["x_used"], 8)
            nc.scalar.activation(s_out.rearrange("p a b -> p (a b)"), s_out.rearrange("p a b -> p (a b)"), ACT.Gelu_apprx_tanh).then_inc(S["gelu_ready"], 1)
            for i in range(4):
                if i == 0:
                    act.wait_ge(S["glu_psum"], 1)
                if i == 2:
                    act.wait_ge(S["chunk_used"], STREAM.index(("wglu", 0)) + 1)
                nc.scalar.activation(yT[:, 2, i, :], bank[3 + i // 2][:, (i % 2) * SEQ:(i % 2 + 1) * SEQ], ACT.Sigmoid, bias=v_("bglu", i))\
                    .then_inc(S["glu_gate"], 1)
            b = projected(("ckv", 0))
            act.wait_ge(S["yD_ready"], 1)
            act.wait_ge(S["yC_ready"], 1)
            nc.scalar.activation(ckv, b[:, 0:SEQ], ACT.Copy).then_inc(S["proj_evac"], 1)
            root(rst.rearrange("p a b -> p (a b)"), 1)
            for n in range(6):
                if n < 5:
                    act.wait_ge(S["mla_psum"], n + 1)
                else:
                    act.wait_ge(S["chunk_used"], STREAM.index(("wkv", 0)) + 1)
                dst = (qn[:, 0:2], qn[:, 2:4], kn[:, 0:2], kn[:, 2:4], vv[:, 0], vv[:, 1])[n]
                if n < 4:
                    dst = dst.rearrange("p a b -> p (a b)")
                nc.scalar.activation(dst, bank[(6, 7, 5, 6, 7, 5)[n]][:, :], ACT.Copy).then_inc(S["mla_evac"], 1)

            for i in range(2):
                b = projected(("hf", i))
                nc.scalar.activation(hg_f[:, 512 * i:512 * i + 512], b[:, :], ACT.Sigmoid)
                nc.scalar.activation(hg_k[:, 512 * i:512 * i + 512], b[:, :], ACT.Sigmoid, scale=-1.0).then_inc(S["proj_evac"], 1)
            for i in range(2):
                b = projected(("hq", i))
                nc.scalar.activation(hg_q[:, 512 * i:512 * i + 512], b[:, :], ACT.Silu).then_inc(S["proj_evac"], 1)
            for n in range(8 + 2):
                if n < 8:
                    nk = P * (n % 2 + 1)
                    act.wait_ge(S["smax_ready"], n + 1)
                    if n >= 2:
                        act.wait_ge(S["pT_psum"], n - 1)
                    nc.scalar.activation(probs[n % 2][:, 0:nk], bank[3 + n % 2][:, 0:nk], ACT.Exp, bias=small[:, 192 + n:193 + n], scale=SM,
                                         accum_out=small[:, 200 + n:201 + n]).then_inc(S["sexp_ready"], 1)
                if n >= 1 and n - 1 < 8:
                    i = n - 1
                    act.wait_ge(S["pT_psum"], i + 1)
                    nk = i % 2 + 1
                    nc.scalar.activation(probsT[i % 2][:, 0:nk, :].rearrange("p a b -> p (a b)"), bank[5 + i % 2][:, 0:nk * P], ACT.Copy).then_inc(S["pT_ready"], 1)
                if n >= 2 and n % 2 == 1:
                    h = (n - 3) // 2
                    if h >= 0:
                        act.wait_ge(S["o_psum"], h + 1)
                        nc.scalar.activation(yT[:, 1, h, :], bank[7][:, 0:SEQ], ACT.Copy).then_inc(S["o_evac"], 1)
            act.wait_ge(S["o_evac"], 4)
            for i in range(2):
                b = projected(("hi", i))
                for half in range(2):
                    ins = nc.scalar.activation(hg_v[:, half, 256 * i:256 * i + 256], b[:, half * 256:half * 256 + 256], ACT.Copy)
                ins.then_inc(S["proj_evac"], 1)
            for i in range(2):
                b = projected(("hg", i))
                nc.scalar.activation(hg_g[:, 512 * i:512 * i + 512], b[:, :], ACT.Silu).then_inc(S["proj_evac"], 1)
            for i in range(2):
                act.wait_ge(S["hgT_psum"], i + 1)
                nc.scalar.activation(hg_kT[:, 4 * i:4 * i + 4, :].rearrange("p a b -> p (a b)"), bank[4 + i][:, :], ACT.Copy).then_inc(S["kT_ready"], 1)
            for h in range(HEADS):
                act.wait_ge(S["ho_psum"], h + 1)
                if h:
                    act.wait_ge(S["yA_ready"], h)
                nc.scalar.activation(hg_sq, bank[7][:, 0:SEQ], ACT.Square).then_inc(S["ho_evac"], 1)
                nc.scalar.activation(hg_o, bank[7][:, 0:SEQ], ACT.Copy).then_inc(S["ho_evac"], 1)
                root(hg_rs, 2 + h)
            assert proj_n[0] == len(PROJ)

            act.wait_ge(S["yA_ready"], HEADS)
            act.dma_start(x_res, A["x"][0].rearrange("(h p) n -> p h n", p=P)).then_inc(S["xres_in"], 16)
            act.dma_start(ln_w, A["ln1_w"].to_broadcast([P, D])).then_inc(S["ln_in"], 16)
            act.dma_start(ln_b, A["ln1_b"].to_broadcast([P, D])).then_inc(S["ln_in"], 16)
            act.dma_start(rb, A["router_b"].to_broadcast([P, NE])).then_inc(S["rb_in"], 16)
            act.dma_start(rw, A["router_w"].rearrange("(k p) n -> p k n", p=P)).then_inc(S["rw_in"], 16)
            act.wait_ge(S["b_clear"], 1)
            act.dma_start(b1_all[0:NE, :], A["moe_b1"]).then_inc(S["b_in"], 16)
            act.dma_start(b2_all[0:NE, :], A["moe_b2"]).then_inc(S["b_in"], 16)
            for half in range(2):
                root(small[:, 314:315], 6 + half)
            for r in range(4):
                act.wait_ge(S["hT_psum"], r + 1)
                nc.scalar.activation(hT[:, 2 * r:2 * r + 2, :].rearrange("p a b -> p (a b)"), bank[r][:, :], ACT.Copy).then_inc(S["hT_act"], 1)
            act.dma_start(ln_w, A["ln2_w"].to_broadcast([P, D])).then_inc(S["ln2_in"], 16)
            act.dma_start(ln_b, A["ln2_b"].to_broadcast([P, D])).then_inc(S["ln2_in"], 16)
            act.wait_ge(S["topexp_req"], 1)
            for half in range(2):
                nc.scalar.activation(small[:, 216 + 8 * half:220 + 8 * half], top[:, half, 0:TOPK], ACT.Exp, bias=small[:, 232 + half:233 + half],
                                     accum_out=small[:, 236 + half:237 + half]).then_inc(S["topexp_ready"], 1)
            act.wait_ge(S["wT_psum"], 1)
            nc.scalar.activation(wTd[0:NE].rearrange("p a b -> p (a b)"), bank[6][0:NE, 0:2 * P], ACT.Copy).then_inc(S["wT_ready"], 1)

            def gathered(g):
                act.wait_ge(S["xg_psum"], g + 1)
                nc.scalar.activation(xg.rearrange("p a b -> p (a b)"), bank[5][:, :], ACT.Copy).then_inc(S["xg_ready"], 1)

            def expert(n, u, gather_next=None):
                act.wait_ge(S["gmin_ready"], n + 1)
                nc.scalar.activation(g3, g1, ACT.Sigmoid, scale=SWA).then_inc(S["sig_ready"], 1)
                act.wait_ge(S["at_psum"], n + 1)
                nc.scalar.activation(actT.rearrange("p a b -> p (a b)"), bank[6][:, :], ACT.Copy).then_inc(S["at_ready"], 1)
                if gather_next is not None:
                    gathered(gather_next)
                act.wait_ge(S["expert_chunk_used"], n * R2S + R2S)
                nc.scalar.activation(y_pair[64 * u:64 * u + 64, 0:512], bank[4][0:64, :], ACT.Copy).then_inc(S["ypair_act"], 1)

            def weights(m_):
                act.wait_ge(S["wselT_psum"], m_ + 1)
                nc.scalar.activation(wselT.rearrange("p a b -> p (a b)"), bank[7][:, 0:256], ACT.Copy).then_inc(S["wselT_ready"], 1)

            gathered(0)
            with act.Fori(0, NPAIR) as p:
                expert(p * 2, 0, p * 2 + 1)
                weights(p)
                expert(p * 2 + 1, 1, p * 2 + 2)
            act.wait_ge(S["items_ready"], 1)
            n_items = act.value_load(item_e[0:1, NITEM:NITEM + 1], min_val=0, max_val=NITEM)
            with act.If(n_items > 0):
                with act.Fori(0, n_items) as j:
                    gathered(j + NE + 1)
                    weights(j + NPAIR)
                    expert(j + NE, 0)
            for half in range(2):
                root(small[:, 314:315], 8 + half)

        @block.tensor
        def _(pe):
            mm = nc.tensor.matmul
            st = [0]
            pj = [0]

            def chunk(c):
                i = st[0]
                assert STREAM[i] == c, (STREAM[i], c)
                st[0] += 1
                pe.wait_ge(landed[i % R1], need[c])
                shape, _ = chunk_source(c)
                return slot(i % R1, *shape)

            def proj(c):
                w = chunk(c)
                i = pj[0]
                pj[0] += 1
                if i >= 2:
                    pe.wait_ge(S["proj_evac"], i - 1)
                b = bank[i % 2]
                if c[0] == "hi":
                    for half in range(2):
                        for k in range(KD):
                            last = mm(b[:, half * CW:half * CW + CW], xT[:, k, half * P:half * P + P], w[:, k, :], start=k == 0, stop=k == KD - 1)
                elif c[0] == "ckv":
                    for k in range(KD):
                        last = mm(b[:, 0:SEQ], w[:, k, 0:P], xT[:, k, :], start=k == 0, stop=k == KD - 1)
                    pe.wait_ge(S["glu_gate"], 4)
                    for half in range(2):
                        for k in range(KD):
                            for h in range(HEADS):
                                last = mm(bank[3 + half][32 * h:32 * h + 32, SEQ:], w[:, k, P + R2 * half:P + R2 * half + R2], xT[:, k, :],
                                          start=k == 0, stop=k == KD - 1)
                else:
                    for j in range(2):
                        for k in range(KD):
                            last = mm(b[:, j * SEQ:(j + 1) * SEQ], w[:, k, j * P:j * P + P], xT[:, k, :], start=k == 0, stop=k == KD - 1)
                last.then_inc(S["chunk_used"], 1)

            def merge(br, n):
                for dh in range(2):
                    w = chunk(("wb", br, dh))
                    for j in range(2):
                        u = 4 * n + 2 * dh + j
                        if u:
                            pe.wait_ge(S["merge_used"], u)
                        for i in range(2):
                            for k in range(4):
                                last = mm(bank[2][:, i * SEQ:(i + 1) * SEQ], w[:, k, (2 * j + i) * P:(2 * j + i + 1) * P], yT[:, br, k, :],
                                          start=k == 0, stop=k == 3)
                        last.then_inc(S["merge_psum"] if j == 0 else S["chunk_used"], 1)

            pe.wait_ge(S["const_ready"], NCONST)
            pe.wait_ge(S["x_in"], 16)
            for r in range(4):
                for kk in range(2):
                    for half in range(2):
                        k = 2 * r + kk
                        last = nc.tensor.transpose(bank[3 + r][:, kk * SEQ + half * P:kk * SEQ + half * P + P], x_tok[:, half, k * P:k * P + P], ident[:, :])
                last.then_inc(S["xT_psum"], 1)
            pe.wait_ge(S["vec_in"], 16 * 14)
            nc.tensor.transpose(bank[7][:, 0:P], rows[:, :], ident[:, :])
            pe.wait_ge(S["dt_rows"], 1)
            nc.tensor.transpose(bank[7][:, P:P + S5T], small[0:S5T, 64:192], ident[0:S5T, 0:S5T]).then_inc(S["vec_psum"], 1)
            pe.wait_ge(S["xT_vec"], 2)
            pe.wait_ge(S["xT_act"], 2)
            proj(("lx", 0))
            proj(("lx", 1))
            proj(("su", 0))
            proj(("su", 1))
            pe.wait_ge(S["lru_in"], 16 * 16)
            for i in range(4):
                pe.wait_ge(S["xc_ready"], i + 1)
                mm(bank[3 + i][:, 0:SEQ], wa[:, i, :], xc[:, i, :], start=True, stop=True)
                mm(bank[3 + i][:, SEQ:], wx[:, i, :], xc[:, i, :], start=True, stop=True).then_inc(S["gate_psum"], 1)
            proj(("lg", 0))
            proj(("lg", 1))
            proj(("cq", 0))
            pe.wait_ge(S["exp_ready"], 1)
            pe.wait_ge(S["gate_act"], 8)
            for i in range(4):
                for q in range(4):
                    src = b_exp[:, i, 4 * q:4 * q + 4, :].rearrange("p a b -> p (a b)") if i < 2 else c_exp[:, i - 2, q, :]
                    last = nc.tensor.transpose(bank[3 + i][:, q * P:q * P + P], src, ident[:, :])
                last.then_inc(S["prep_psum"], 1)
            pe.wait_ge(S["prep_evac"], 4)
            pe.wait_ge(S["proj_evac"], 4)

            def drive(h):
                if h >= 2:
                    pe.wait_ge(S["bu_free"], h - 1)
                for i in range(2):
                    for j in (2 * h, 2 * h + 1):
                        q, r = j // 4, 32 * (j % 4)
                        last = mm(bank[3 + 2 * (h % 2) + j % 2][:, i * SEQ:(i + 1) * SEQ], bT[r:r + 32, i, q, :], su[r:r + 32, q, :],
                                  start=True, stop=True, tile_position=(r, 0))
                last.then_inc(S["bu_psum"], 1)

            def read_out(h):
                pe.wait_ge(S["x_ready"], h + 1)
                q = h // 2
                if h % 2 == 0 and q >= 1:
                    pe.wait_ge(S["y_evac"], q)
                for i, xs in ((0, xr), (1, xi)):
                    for j in (2 * h, 2 * h + 1):
                        r = 32 * (j % 4)
                        last = mm(bank[7][r:r + 32, 0:SEQ], cT[:, i, q, r:r + 32], xs[h % 2][:, j % 2, :], start=i == 0, stop=i == 1)
                last.then_inc(S["x_used"], 1)

            drive(0)
            for h in range(8):
                if h < 7:
                    drive(h + 1)
                proj(("gl", 2 * h))
                proj(("gl", 2 * h + 1))
                read_out(h)
            w = chunk(("wglu", 0))
            pe.wait_ge(S["gelu_ready"], 1)
            for j in range(4):
                for k in range(4):
                    last = mm(bank[3 + j // 2][:, (j % 2) * SEQ:(j % 2 + 1) * SEQ], w[:, k, j * P:j * P + P], s_out[:, k, :], start=k == 0, stop=k == 3)
                if j == 1:
                    last.then_inc(S["glu_psum"], 1)
            last.then_inc(S["chunk_used"], 1)
            proj(("ckv", 0))
            pe.wait_ge(S["sq_ready"], 1)
            mm(bank[5][:, 0:SEQ], ones_256[:, :], sq[:, 0, :], start=True, stop=False)
            mm(bank[5][:, 0:SEQ], ones_256[:, :], sq[:, 1, :], start=False, stop=True)
            mm(bank[5][:, SEQ:], ones_128[:, :], sq[:, 2, :], start=True, stop=True).then_inc(S["ss_psum"], 1)
            wq = chunk(("wq", 0))
            pe.wait_ge(S["norm_ready"], 1)
            for h in range(HEADS):
                for k in range(2):
                    last = mm(bank[6 + h // 2][:, (h % 2) * SEQ:(h % 2 + 1) * SEQ], wq[:, k, h * QK:h * QK + NOPE], cq[:, k, :], start=k == 0, stop=k == 1)
                if h % 2:
                    last.then_inc(S["mla_psum"], 1)
            for half in range(2):
                for h in range(HEADS):
                    for k in range(2):
                        lo = h * QK + NOPE + R2 * half
                        last = mm(bank[3 + half][32 * h:32 * h + 32, 0:SEQ], wq[:, k, lo:lo + R2], cq[:, k, :], start=k == 0, stop=k == 1)
            last.then_inc(S["chunk_used"], 1)
            wkv = chunk(("wkv", 0))
            for h in range(HEADS):
                if h == 2:
                    pe.wait_ge(S["mla_evac"], 1)
                last = mm(bank[5 + h // 2][:, (h % 2) * SEQ:(h % 2 + 1) * SEQ], wkv[:, 0, h * 256:h * 256 + NOPE], ckv, start=True, stop=True)
                if h % 2:
                    last.then_inc(S["mla_psum"], 1)
            wv = wkv[:, 0, :].rearrange("p (h c) -> p h c", h=HEADS)[:, :, NOPE:]
            for half in range(2):
                pe.wait_ge(S["mla_evac"], 2 + half)
                mm(bank[7 - 2 * half][:, :].rearrange("p (a b) -> p a b", a=HEADS), ckv[:, half * P:half * P + P], wv, start=True, stop=True)\
                    .then_inc(S["chunk_used"] if half else S["mla_psum"], 1)
            for c in (("hf", 0), ("hf", 1), ("hq", 0), ("hq", 1)):
                proj(c)
            pe.wait_ge(S["mla_evac"], 6)
            pe.wait_ge(S["mla_masked"], 1)
            for n in range(8 + 2):
                if n < 8:
                    h, qt = n // 2, n % 2
                    nk = P * (qt + 1)
                    if n >= 2:
                        pe.wait_ge(S["sexp_ready"], n - 1)
                    b = bank[3 + n % 2]
                    mm(b[:, 0:nk], qn[:, h, qt * P:qt * P + P], kn[:, h, 0:nk], start=True, stop=False)
                    mm(b[:, 0:nk], qm1[:, h, qt * P:qt * P + P], rp1[:, 1, 0:nk], start=False, stop=False)
                    mm(b[:, 0:nk], qm2[:, h, qt * P:qt * P + P], rp2[:, 1, 0:nk], start=False, stop=True).then_inc(S["s_psum"], 1)
                if 1 <= n <= 8:
                    i = n - 1
                    pe.wait_ge(S["p_norm"], i + 1)
                    if i >= 2:
                        pe.wait_ge(S["pT_ready"], i - 1)
                    for kt in range(i % 2 + 1):
                        last = nc.tensor.transpose(bank[5 + i % 2][:, kt * P:kt * P + P], probs[i % 2][:, kt * P:kt * P + P], ident[:, :])
                    last.then_inc(S["pT_psum"], 1)
                if n >= 2:
                    i = n - 2
                    h, qt = i // 2, i % 2
                    pe.wait_ge(S["pT_ready"], i + 1)
                    if qt == 0 and h >= 1:
                        pe.wait_ge(S["o_evac"], h)
                    for kt in range(qt + 1):
                        last = mm(bank[7][:, qt * P:qt * P + P], vv[:, kt, h * VD:h * VD + VD], probsT[i % 2][:, kt, :], start=kt == 0, stop=kt == qt)
                    if qt:
                        last.then_inc(S["o_psum"], 1)
            pe.wait_ge(S["yD_ready"], 1)
            merge(3, 0)
            pe.wait_ge(S["yC_ready"], 1)
            merge(2, 1)
            for c in (("hi", 0), ("hi", 1), ("hg", 0), ("hg", 1)):
                proj(c)
            for t in range(BLK):
                pe.wait_ge(S["p_ready"], t + 1)
                for n in range(8):
                    last = mm(bank[3][:, n * BLK + t:n * BLK + t + 1], prod[t % 2][:, 8 * n:8 * n + 8, :].rearrange("p a b -> p (a b)"), ones[:, 0:1], start=True, stop=True)
                last.then_inc(S["p_used"], 1)
            pe.wait_ge(S["g_ready"], 1)
            for n in range(8):
                last = nc.tensor.transpose(bank[4 + n // 4][:, (n % 4) * P:(n % 4 + 1) * P], grow[:, 8 * n:8 * n + 8, :].rearrange("p a b -> p (a b)"), ident[:, :])
                if n % 4 == 3:
                    last.then_inc(S["hgT_psum"], 1)
            pe.wait_ge(S["o_evac"], 4)
            merge(1, 2)
            pe.wait_ge(S["kT_ready"], 2)
            pe.wait_ge(S["bd_ready"], 1)

            def outputs(h):
                pe.wait_ge(S["st_ready"], h + 1)
                if h:
                    pe.wait_ge(S["ho_evac"], 2 * h)
                for half in range(2):
                    lo = half * P
                    mm(bank[7][:, lo:lo + P], hg_v[:, half, h * P:h * P + P], hg_bd[:, 2 * h + half, :], start=True, stop=False)
                    for b in range(8 * half, 8 * half + 8):
                        if b:
                            last = mm(bank[7][:, b * BLK:b * BLK + BLK], state[:, b - 1, :], q_inter[:, h * SEQ + b * BLK:h * SEQ + b * BLK + BLK],
                                      start=False, stop=b % 8 == 7)
                last.then_inc(S["ho_psum"], 1)

            for h in range(HEADS):
                for half in range(2):
                    n = 2 * h + half
                    pe.wait_ge(S["vx_ready"], n + 1)
                    for i in range(2):
                        u = 2 * n + i
                        if u >= 3:
                            pe.wait_ge(S["u_used"], u - 2)
                        mm(bank[4 + u % 3][:, :], hg_kT[:, n, :], v_exp[n % 2][:, 4 * i:4 * i + 4, :].rearrange("p a b -> p (a b)"), start=True, stop=True)\
                            .then_inc(S["u_psum"], 1)
                outputs(h)
                pe.wait_ge(S["ho_evac"], 2 * h + 1)
                mm(bank[3][:, 0:SEQ], ones_128[:, :], hg_sq, start=True, stop=True).then_inc(S["hss_psum"], 1)
            pe.wait_ge(S["yA_ready"], HEADS)
            merge(0, 3)
            pe.wait_ge(S["merge_done"], 4)
            for i in range(4):
                w = chunk(("wo", i))
                for kk in range(2):
                    k = 2 * i + kk
                    for half in range(2):
                        for dh in range(2):
                            last = mm(bank[4 + 2 * half + dh][:, :], acc[:, k, half * P:half * P + P], w[:, kk, 512 * dh:512 * dh + 512],
                                      start=k == 0, stop=k == KD - 1)
                last.then_inc(S["chunk_used"], 1)
            pe.wait_ge(S["h_ready"], 2)
            for r in range(4):
                for kk in range(2):
                    for half in range(2):
                        k = 2 * r + kk
                        last = nc.tensor.transpose(bank[r][:, kk * SEQ + half * P:kk * SEQ + half * P + P], h_tok[:, half, k * P:k * P + P], ident[:, :])
                last.then_inc(S["hT_psum"], 1)
            pe.wait_ge(S["hT_act"], 4)
            pe.wait_ge(S["rw_in"], 16)
            for half in range(2):
                for k in range(KD):
                    last = mm(bank[4][:, half * NE:half * NE + NE], hT[:, k, half * P:half * P + P], rw[:, k, :], start=k == 0, stop=k == KD - 1)
            last.then_inc(S["logit_psum"], 1)
            pe.wait_ge(S["route_ready"], 1)
            mm(bank[4][:, 0:NE], earlier[:, :], member[:, 0, :], start=True, stop=True)
            mm(bank[4][:, NE:2 * NE], earlier[:, :], member[:, 1, :], start=True, stop=False)
            mm(bank[4][:, NE:2 * NE], ones[:, :], member[:, 0, :], start=False, stop=True)
            mm(bank[4][:, 2 * NE:3 * NE], ones[:, :], member[:, 0, :], start=True, stop=False)
            mm(bank[4][:, 2 * NE:3 * NE], ones[:, :], member[:, 1, :], start=False, stop=True).then_inc(S["rank_psum"], 1)
            for half in range(2):
                last = nc.tensor.transpose(bank[6][0:NE, half * P:half * P + P], wfull[:, half, 0:NE], ident[:, :])
            last.then_inc(S["wT_psum"], 1)

            def gather(g, u):
                pe.wait_ge(S["sel_ready"], g + 1)
                for i in range(2):
                    for ct in range(2):
                        mm(bank[2 * u + i][64 * ct:64 * ct + 64, :], esel, b1_all[:, i * FF + ct * 512:i * FF + ct * 512 + 512], start=True, stop=False)
                for k in range(KD):
                    for half in range(2):
                        last = mm(bank[5][:, k * CAP:k * CAP + CAP], h_tok[:, half, k * P:k * P + P], sel[:, half, :], start=half == 0, stop=half == 1)
                last.then_inc(S["xg_psum"], 1)

            def expert(n, u, g, gather_next=None):
                pe.wait_ge(S["xg_ready"], g + 1)
                for c in range(8):
                    pe.wait_ge(landed[c], (n + 1) * 16 + 16 * uses[c])
                    w = expert_slot(c)
                    for i in range(2):
                        for ct in range(2):
                            last = mm(bank[2 * u + i][64 * ct:64 * ct + 64, :], xg[:, c, :], w[:, i * FF + ct * 512:i * FF + ct * 512 + 512], start=False, stop=c == 7)
                    last.then_inc(S["expert_chunk_used"], 1)
                if gather_next is not None:
                    pe.wait_ge(S["b2_used"], 1)
                    gather(gather_next, 1 - u)
                pe.wait_ge(S["act_ready"], n + 1)
                for j in range(4):
                    last = nc.tensor.transpose(bank[6][:, j * P:j * P + P], g1[:, j * P:j * P + P], ident[:, :])
                last.then_inc(S["at_psum"], 1)
                pe.wait_ge(S["at_ready"], n + 1)
                for c in range(8, 12):
                    pe.wait_ge(landed[c], (n + 1) * 16 + 16 * uses[c])
                    w = expert_slot(c)
                    for kk in range(2):
                        r = 2 * (c - 8) + kk
                        fh, j = r // 4, r % 4
                        for dh in range(2):
                            last = mm(bank[4][64 * dh:64 * dh + 64, :], actT[:, j, 64 * fh:64 * fh + 64], w[:, kk, 512 * dh:512 * dh + 512], start=r == 0, stop=r == 7)
                    last.then_inc(S["expert_chunk_used"], 1)

            def weights(rows_):
                for half in range(2):
                    last = nc.tensor.transpose(bank[7][0:rows_, half * P:half * P + P], wsel[:, half, 0:rows_], ident[:, :])
                last.then_inc(S["wselT_psum"], 1)

            def combine(m_, n, rows_):
                pe.wait_ge(S["wselT_ready"], m_ + 1)
                pe.wait_ge(S["ypair_act"], n)
                pe.wait_ge(S["ypair_vec"], n)
                for i in range(4):
                    half, dh = i // 2, i % 2
                    if i >= 2:
                        pe.wait_ge(S["comb_used"], m_ * 4 + i - 1)
                    mm(bank[6 + i % 2][:, :], wselT[0:rows_, half, :], y_pair[0:rows_, 512 * dh:512 * dh + 512], start=True, stop=True).then_inc(S["comb_psum"], 1)
                pe.wait_ge(S["comb_used"], m_ * 4 + 4)

            pe.wait_ge(S["b_in"], 32)
            gather(0, 0)
            pe.wait_ge(S["wT_ready"], 1)
            for half in range(2):
                for dh in range(2):
                    last = mm(bank[(2, 3, 6, 7)[2 * half + dh]][:, :], wTd[:, half, :], b2_all[:, 512 * dh:512 * dh + 512], start=True, stop=True)
            last.then_inc(S["b2_psum"], 1)
            with pe.Fori(0, NPAIR) as p:
                expert(p * 2, 0, p * 2, p * 2 + 1)
                weights(P)
                expert(p * 2 + 1, 1, p * 2 + 1, p * 2 + 2)
                combine(p, p * 2 + 2, P)
            pe.wait_ge(S["items_ready"], 1)
            n_items = pe.value_load(item_e[0:1, NITEM:NITEM + 1], min_val=0, max_val=NITEM)
            with pe.If(n_items > 0):
                with pe.Fori(0, n_items) as j:
                    gather(j + NE + 1, 1)
                    weights(CAP)
                    expert(j + NE, 1, j + NE + 1)
                    combine(j + NPAIR, j + NE + 1, CAP)

        @block.vector
        def _(dve):
            V = nc.vector
            vc = [0]
            base = [0]
            tail = [False]
            fc = [0]

            def link(ins):
                if tail[0]:
                    fc[0] += 1
                    ins.then_inc(S["f_chain"], 1)
                    dve.wait_ge(S["f_chain"], fc[0])
                    return
                vc[0] += 1
                ins.then_inc(S["v_chain"], 1)
                dve.wait_ge(S["v_chain"], base[0] + vc[0])

            def inverse_root(dst, src, eps, nth):
                link(V.tensor_scalar(dst, src, eps, None, ALU.add))
                V.reciprocal(dst, dst).then_inc(S["rs_req"], 1)
                dve.wait_ge(S["rs_ready"], nth)

            def sm(lo, n=16):
                return small[:, lo:lo + n]

            dve.wait_ge(S["iota_ready"], 1)
            V.tensor_copy(iota[:, :], iota_i[:, :]).then_inc(S["iota_read"], 1)
            dve.wait_ge(S["iota_read"], 1)
            dve.wait_ge(S["dt_in"], 16)
            V.tensor_copy(small[0:S5T, 64:192].rearrange("p (a b) -> p a b", a=2), small[0:S5T, 0:2].unsqueeze(2).to_broadcast([S5T, 2, 64])).then_inc(S["dt_rows"], 1)
            dve.wait_ge(S["const_ready"], NCONST)
            link(V.memset(lx[:, :, 0:3], 0.0))
            link(V.memset(b_exp, 0.0))
            for r in (0, 2):
                dve.wait_ge(S["xT_psum"], r + 1)
                V.tensor_copy(xT[:, 2 * r:2 * r + 2, :].rearrange("p a b -> p (a b)"), bank[3 + r][:, :]).then_inc(S["xT_vec"], 1)
            dve.wait_ge(S["vec_psum"], 1)
            link(V.tensor_copy(sm(16), bank[7][:, P:P + S5T]))
            V.tensor_copy(vec[:, :], bank[7][:, 0:NVEC]).then_inc(S["vec_ready"], 1)
            dve.wait_ge(S["vec_ready"], 1)
            V.tensor_copy(small[:, 500:501], small[:, 16:17]).then_inc(S["dt_exp"], 1)
            V.scalar_tensor_tensor(sm(360, 4), v_("apar", 0, 4), -1.0, v_("apar", 0, 4), ALU.mult, ALU.max).then_inc(S["absa_ready"], 1)
            V.tensor_tensor(sm(400, 4), v_("lb", 0, 4), v_("lb", 0, 4), ALU.subtract).then_inc(S["lbe_req"], 1)
            dve.wait_ge(S["s5_small"], 1)
            link(V.tensor_tensor(sm(48), v_("a_re", 0, 16), sm(32), ALU.mult))
            link(V.tensor_tensor(sm(64), v_("a_im", 0, 16), sm(32), ALU.mult))
            V.tensor_copy(small[:, 501:502], small[:, 48:49]).then_inc(S["s5_mag"], 1)
            link(V.tensor_scalar(sm(96), sm(64), INV2PI, MAGIC, ALU.mult, ALU.add))
            link(V.tensor_scalar(sm(96), sm(96), MAGIC, None, ALU.subtract))
            for c in (C1, C2, C3):
                link(V.scalar_tensor_tensor(sm(64), sm(96), -c, sm(64), ALU.mult, ALU.add))
            link(V.tensor_scalar(sm(176), sm(64), INV2PI, None, ALU.mult))
            link(V.tensor_scalar(sm(144), sm(64), PI_LOW, -PI_LOW, ALU.min, ALU.max))
            link(V.scalar_tensor_tensor(sm(160), sm(144), -1.0, sm(144), ALU.mult, ALU.min))
            V.tensor_scalar(sm(160), sm(160), float(np.pi / 2), None, ALU.add).then_inc(S["s5_theta"], 1)
            dve.wait_ge(S["expa_ready"], 1)
            z, s_, s2, po = sm(364, 4), sm(368, 4), sm(372, 4), sm(388, 4)
            link(V.tensor_scalar(s_, z, 2.0, None, ALU.add))
            link(V.reciprocal(s_, s_))
            link(V.tensor_tensor(s_, s_, z, ALU.mult))
            link(V.tensor_tensor(s2, s_, s_, ALU.mult))
            link(V.tensor_scalar(po, s2, 1.0 / 17, 1.0 / 15, ALU.mult, ALU.add))
            for d_ in (13, 11, 9, 7, 5, 3, 1):
                link(V.tensor_tensor(po, po, s2, ALU.mult))
                link(V.tensor_scalar(po, po, 1.0 / d_, None, ALU.add))
            link(V.tensor_tensor(po, po, s_, ALU.mult))
            link(V.tensor_scalar(s_, v_("apar", 0, 4), 0.0, None, ALU.max))
            link(V.scalar_tensor_tensor(po, po, 2.0, s_, ALU.mult, ALU.add))
            link(V.tensor_scalar(sm(376, 4), po, -8.0, None, ALU.mult))
            link(V.tensor_scalar(sm(380, 4), po, 8.0, None, ALU.mult))
            V.tensor_scalar(sm(384, 4), po, -16.0, None, ALU.mult).then_inc(S["sp_ready"], 1)
            dve.wait_ge(S["lbe_ready"], 1)
            link(V.reciprocal(sm(408, 4), sm(404, 4)))
            link(V.tensor_tensor(sm(408, 4), sm(408, 4), sm(404, 4), ALU.mult))
            link(V.tensor_tensor(sm(412, 4), sm(408, 4), sm(408, 4), ALU.subtract))
            link(V.tensor_scalar(sm(416, 4), sm(412, 4), -1.0, 1.0, ALU.mult, ALU.add))
            dve.wait_ge(S["proj_evac"], 2)
            for i in range(4):
                link(V.tensor_scalar(xc[:, i, :], lx[:, i, 3:3 + SEQ], v_("convw", 12 + i), v_("convb", i), ALU.mult, ALU.add))
                for tap in range(3):
                    ins = V.scalar_tensor_tensor(xc[:, i, :], lx[:, i, tap:tap + SEQ], v_("convw", 4 * tap + i), xc[:, i, :], ALU.mult, ALU.add)
                    if tap < 2:
                        link(ins)
                ins.then_inc(S["xc_ready"], 1)
            dve.wait_ge(S["s5_trig0"], 1)
            dve.wait_ge(S["s5_small"], 2)
            sn, cs, mag = sm(112), sm(128), sm(80)
            re, im = v_("a_re", 0, 16), v_("a_im", 0, 16)
            nr, li, den, tq = sm(208), sm(224), sm(240), sm(256)
            cr, ci = sm(272), sm(288)
            link(V.tensor_tensor(nr, mag, cs, ALU.mult))
            link(V.tensor_scalar(nr, nr, -1.0, None, ALU.add))
            link(V.tensor_tensor(li, mag, sn, ALU.mult))
            link(V.tensor_tensor(den, re, re, ALU.mult))
            link(V.tensor_tensor(tq, im, im, ALU.mult))
            link(V.tensor_tensor(den, den, tq, ALU.add))
            link(V.reciprocal(den, den))
            link(V.tensor_tensor(cr, nr, re, ALU.mult))
            link(V.tensor_tensor(tq, li, im, ALU.mult))
            link(V.tensor_tensor(cr, cr, tq, ALU.add))
            link(V.tensor_tensor(cr, cr, den, ALU.mult))
            link(V.tensor_tensor(ci, li, re, ALU.mult))
            link(V.tensor_tensor(tq, nr, im, ALU.mult))
            link(V.tensor_tensor(ci, ci, tq, ALU.subtract))
            link(V.tensor_tensor(ci, ci, den, ALU.mult))
            dve.wait_ge(S["s5_in"], 64)
            b4 = [s_raw[:, i, :].rearrange("p (a b) -> p a b", a=16) for i in range(2)]
            u1 = t1.rearrange("p a b -> p (a b)")[:, 0:256].rearrange("p (a b) -> p a b", a=16)
            u2 = t2.rearrange("p a b -> p (a b)")[:, 0:256].rearrange("p (a b) -> p a b", a=16)

            def wide(v):
                return v.unsqueeze(2).to_broadcast([P, 16, 16])

            for i, (ca, cb, op) in enumerate(((cr, ci, ALU.subtract), (ci, cr, ALU.add))):
                link(V.tensor_tensor(u1, b4[0], wide(ca), ALU.mult))
                link(V.tensor_tensor(u2, b4[1], wide(cb), ALU.mult))
                for g2_ in range(2):
                    p0 = 64 * g2_
                    link(V.tensor_tensor(b_exp[p0:p0 + 64, i, :, 16 * g2_:16 * g2_ + 16], u1[p0:p0 + 64], u2[p0:p0 + 64], op))
            link(V.tensor_reduce(oddmask[:, 0:1], blockmask[:, :].rearrange("p (a b) -> p b a", b=2)[:, 0, :], X, ALU.add))
            link(V.tensor_reduce(oddmask[:, 1:2], blockmask[:, :].rearrange("p (a b) -> p b a", b=2)[:, 1, :], X, ALU.add))
            for i in range(2):
                craw = s_raw[:, 2 + i, :].rearrange("p (a b) -> p a b", a=4)
                for half in range(2):
                    ins = V.tensor_scalar(c_exp[:, i, :, 64 * half:64 * half + 64], craw, oddmask[:, half:half + 1], None, ALU.mult)
                    if (i, half) != (1, 1):
                        link(ins)
            ins.then_inc(S["exp_ready"], 1)

            def phases(q):
                s, c = sinT[q % 2], cosT[q % 2]
                for j in range(4):
                    ins = V.tensor_scalar(c[:, j, :], iota[:, :], small[:, 176 + 4 * q + j:177 + 4 * q + j], MAGIC, ALU.mult, ALU.add)
                link(ins)
                cf = c.rearrange("p a b -> p (a b)")
                sf = s.rearrange("p a b -> p (a b)")
                link(V.tensor_scalar(cf, cf, MAGIC, None, ALU.subtract))
                for j in range(4):
                    ins = V.scalar_tensor_tensor(s[:, j, :], iota[:, :], small[:, 176 + 4 * q + j:177 + 4 * q + j], c[:, j, :], ALU.mult, ALU.subtract)
                link(ins)
                V.scalar_tensor_tensor(cf, sf, -1.0, sf, ALU.mult, ALU.max).then_inc(S["f_ready"], 1)

            phases(0)
            phases(1)
            flat = "p a b -> p (a b)"
            dve.wait_ge(S["gate_act"], 8)
            link(V.tensor_tensor(lr_i.rearrange(flat), lr_i.rearrange(flat), xc.rearrange(flat), ALU.mult))
            dve.wait_ge(S["lru_exp"], 8)
            link(V.scalar_tensor_tensor(lr_t, lx[:, :, 0:SEQ], 1.0, lr_t, ALU.add, ALU.mult))
            V.tensor_scalar(lr_t.rearrange(flat), lr_t.rearrange(flat), 0.0, None, ALU.max).then_inc(S["lru_b2"], 1)
            dve.wait_ge(S["lru_sqrt"], 1)
            dve.wait_ge(S["lru_exp"], 12)
            link(V.tensor_tensor(lr_i.rearrange(flat), lr_i.rearrange(flat), lr_t.rearrange(flat), ALU.mult))
            for i in range(4):
                link(V.tensor_tensor_scan(xc[:, i, :], lr_r[:, i, :], lr_i[:, i, :], 0.0, ALU.mult, ALU.add))
            dve.wait_ge(S["proj_evac"], 6)
            V.tensor_tensor(yT[:, 3].rearrange(flat), xc.rearrange(flat), lr_g.rearrange(flat), ALU.mult).then_inc(S["yD_ready"], 1)

            for h in range(8):
                q = h // 2
                dve.wait_ge(S["bu_psum"], h + 1)
                dve.wait_ge(S["trig_ready"], 2 * q + 2)
                lo = 2 * (h % 2)
                s, c = sinT[q % 2][:, lo:lo + 2, :], cosT[q % 2][:, lo:lo + 2, :]
                bu = banks[:, 3 + 2 * (h % 2):5 + 2 * (h % 2), :]
                br, bi = bu[:, :, 0:SEQ], bu[:, :, SEQ:]
                a, b, zrf, zif = t1, t2, zr, zi
                link(V.tensor_tensor(a, br, c, ALU.mult))
                link(V.tensor_tensor(b, bi, s, ALU.mult))
                link(V.tensor_tensor(a, a, b, ALU.add))
                for j in range(2):
                    ti = 2 * h + j
                    link(V.tensor_tensor_scan(zr[:, j, :], small[:, 80 + ti:81 + ti].to_broadcast([P, SEQ]), t1[:, j, :], 0.0, ALU.mult, ALU.add))
                link(V.tensor_tensor(a, bi, c, ALU.mult))
                link(V.tensor_tensor(b, br, s, ALU.mult))
                V.tensor_tensor(a, a, b, ALU.subtract).then_inc(S["bu_free"], 1)
                dve.wait_ge(S["bu_free"], h + 1)
                for j in range(2):
                    ti = 2 * h + j
                    link(V.tensor_tensor_scan(zi[:, j, :], small[:, 80 + ti:81 + ti].to_broadcast([P, SEQ]), t1[:, j, :], 0.0, ALU.mult, ALU.add))
                if h >= 2:
                    dve.wait_ge(S["x_used"], h - 1)
                xrf, xif = xr[h % 2], xi[h % 2]
                link(V.tensor_tensor(a, zrf, c, ALU.mult))
                link(V.tensor_tensor(b, zif, s, ALU.mult))
                link(V.tensor_tensor(xrf, a, b, ALU.subtract))
                link(V.tensor_tensor(a, zif, c, ALU.mult))
                link(V.tensor_tensor(b, zrf, s, ALU.mult))
                V.tensor_tensor(xif, a, b, ALU.add).then_inc(S["x_ready"], 1)
                dve.wait_ge(S["x_ready"], h + 1)
                if h in (1, 3):
                    phases(q + 2)
                if h % 2:
                    dve.wait_ge(S["x_used"], h + 1)
                    V.scalar_tensor_tensor(s_out[:, q, :], su[:, q, :], v_("dskip", q), bank[7][:, 0:SEQ], ALU.mult, ALU.add).then_inc(S["y_evac"], 1)
            dve.wait_ge(S["pos_in"], 32)
            link(V.tensor_copy(ang, pos_i[:, :]))
            link(V.tensor_scalar(ang, ang, inv_freq[:, 0:1], None, ALU.mult))
            link(V.tensor_scalar(ang2, ang, INV2PI, MAGIC, ALU.mult, ALU.add))
            link(V.tensor_scalar(ang2, ang2, MAGIC, None, ALU.subtract))
            for c in (C1, C2, C3):
                link(V.scalar_tensor_tensor(ang, ang2, -c, ang, ALU.mult, ALU.add))
            link(V.tensor_scalar(ang, ang, PI_LOW, -PI_LOW, ALU.min, ALU.max))
            link(V.scalar_tensor_tensor(ang2, ang, -1.0, ang, ALU.mult, ALU.min))
            V.tensor_scalar(ang2, ang2, float(np.pi / 2), None, ALU.add).then_inc(S["cos_req"], 1)
            dve.wait_ge(S["glu_gate"], 4)
            V.tensor_tensor(yT[:, 2].rearrange(flat), yT[:, 2].rearrange(flat), s_out.rearrange(flat), ALU.mult).then_inc(S["yC_ready"], 1)

            dve.wait_ge(S["yC_ready"], 1)
            link(V.tensor_copy(cq.rearrange(flat), cq_s.rearrange(flat)))
            dve.wait_ge(S["proj_evac"], PROJ.index(("ckv", 0)) + 1)
            link(V.tensor_tensor(sq[:, 0:2, :].rearrange(flat), cq.rearrange(flat), cq.rearrange(flat), ALU.mult))
            V.tensor_tensor(sq[:, 2, :], ckv, ckv, ALU.mult).then_inc(S["sq_ready"], 1)
            dve.wait_ge(S["ss_psum"], 1)
            inverse_root(rst.rearrange(flat), bank[5][:, :], RMS_EPS, 1)
            for i in range(2):
                link(V.scalar_tensor_tensor(cq[:, i, :], cq[:, i, :], v_("qnorm", i), rst[:, 0, :], ALU.mult, ALU.mult))
            V.scalar_tensor_tensor(ckv, ckv, v_("kvnorm", 0), rst[:, 1, :], ALU.mult, ALU.mult).then_inc(S["norm_ready"], 1)
            dve.wait_ge(S["chunk_used"], STREAM.index(("wq", 0)) + 1)
            dve.wait_ge(S["cos_ready"], 2)
            x1, x2 = (bank[3 + i][:, :].rearrange("p (a b) -> p a b", a=2) for i in range(2))
            cb = cos_p.unsqueeze(1).to_broadcast([P, 2, SEQ])
            sb_ = sin_p.unsqueeze(1).to_broadcast([P, 2, SEQ])
            link(V.tensor_tensor(tA, x1, cb, ALU.mult))
            link(V.tensor_tensor(tB, x2, sb_, ALU.mult))
            link(V.tensor_tensor(rp1, tA, tB, ALU.subtract))
            link(V.tensor_tensor(tA, x2, cb, ALU.mult))
            link(V.tensor_tensor(tB, x1, sb_, ALU.mult))
            link(V.tensor_tensor(rp2, tA, tB, ALU.add))
            for qm, rp in ((qm1, rp1), (qm2, rp2)):
                for h in range(HEADS):
                    ins = V.tensor_scalar(qm[:, h, :], rp[:, 0, :], headmask[:, h:h + 1], None, ALU.mult)
                    if not (rp is rp2 and h == HEADS - 1):
                        link(ins)
            ins.then_inc(S["mla_masked"], 1)

            def attend(n):
                if n < 8:
                    qt = n % 2
                    nk = P * (qt + 1)
                    b = bank[3 + n % 2]
                    dve.wait_ge(S["s_psum"], n + 1)
                    link(V.memset(b[0:CHUNK, nk - CHUNK:nk], MASK_VALUE))
                    link(V.tensor_reduce(small[:, 208 + n % 2:209 + n % 2], b[:, 0:nk], X, ALU.max))
                    V.tensor_scalar(small[:, 192 + n:193 + n], small[:, 208 + n % 2:209 + n % 2], -SM, None, ALU.mult).then_inc(S["smax_ready"], 1)
                if n >= 1:
                    i = n - 1
                    nk = P * (i % 2 + 1)
                    dve.wait_ge(S["sexp_ready"], i + 1)
                    link(V.reciprocal(small[:, 210 + i % 2:211 + i % 2], small[:, 200 + i:201 + i]))
                    V.tensor_scalar(probs[i % 2][:, 0:nk], probs[i % 2][:, 0:nk], small[:, 210 + i % 2:211 + i % 2], None, ALU.mult).then_inc(S["p_norm"], 1)

            for n in range(9):
                attend(n)
            mg = [0]

            def merge(br):
                for j in range(4):
                    u = mg[0]
                    mg[0] += 1
                    if j % 2 == 0:
                        dve.wait_ge(S["merge_psum"], u // 2 + 1)
                    else:
                        dve.wait_ge(S["chunk_used"], STREAM.index(("wb", br, j // 2)) + 1)
                    gate = merge_gate[:, 8 * br + 2 * j:8 * br + 2 * j + 2, :].rearrange(flat)
                    dst = acc[:, 2 * j:2 * j + 2, :].rearrange(flat)
                    V.tensor_tensor(dst if u < 4 else m_tmp, bank[2][:, :], gate, ALU.mult).then_inc(S["merge_used"], 1)
                    dve.wait_ge(S["merge_used"], u + 1)
                    if u >= 4:
                        link(V.tensor_tensor(dst, dst, m_tmp, ALU.add))
                V.tensor_copy(small[:, 502:503], acc[:, 7, 255:256]).then_inc(S["merge_done"], 1)

            def hv(v, t):
                return v.rearrange("p (a b) -> p a b", b=BLK)[:, :, t:t + 1]

            dve.wait_ge(S["proj_evac"], PROJ.index(("hq", 1)) + 1)
            for h in range(HEADS):
                f, k = hg_f[:, h * SEQ:(h + 1) * SEQ], hg_k[:, h * SEQ:(h + 1) * SEQ]
                V.tensor_scalar(k, k, small[:, 416 + h:417 + h], None, ALU.mult)
                link(V.tensor_scalar(f, f, small[:, 416 + h:417 + h], small[:, 412 + h:413 + h], ALU.mult, ALU.add))
            link(V.tensor_scalar(hg_f, hg_f, F_MIN, None, ALU.max))
            link(V.memset(prod[0], 0.0))
            link(V.memset(prod[1], 0.0))

            def grow_step(t):
                if t == 0:
                    link(V.tensor_copy(decay, hv(hg_f, 0)))
                else:
                    link(V.tensor_tensor(decay, decay, hv(hg_f, t), ALU.mult))
                    V.tensor_tensor(grow[:, :, 0:t], grow[:, :, 0:t], hv(hg_f, t).to_broadcast([P, HB, t]), ALU.mult)
                link(V.tensor_copy(grow[:, :, t:t + 1], hv(hg_k, t)))
                link(V.tensor_tensor(hv(q_inter, t), decay, hv(hg_q, t), ALU.mult))
                if t >= 2:
                    dve.wait_ge(S["p_used"], t - 1)
                V.tensor_tensor(prod[t % 2][:, :, 0:t + 1], grow[:, :, 0:t + 1], hv(hg_q, t).to_broadcast([P, HB, t + 1]), ALU.mult).then_inc(S["p_ready"], 1)

            grow_step(0)
            grow_step(1)
            merge(3)
            merge(2)
            for t in range(2, BLK):
                grow_step(t)
            dve.wait_ge(S["p_ready"], BLK)
            V.tensor_copy(small[:, 503:504], grow[:, 0, 0:1]).then_inc(S["g_ready"], 1)
            dve.wait_ge(S["p_used"], BLK)
            for n in range(8):
                ins = V.tensor_tensor(hg_bd[:, n, :].rearrange("p (a b) -> p a b", a=8),
                                      bank[3][:, n * BLK:n * BLK + BLK].unsqueeze(1).to_broadcast([P, 8, BLK]),
                                      blockmask[:, :].unsqueeze(2).to_broadcast([P, 8, BLK]), ALU.mult)
            ins.then_inc(S["bd_ready"], 1)
            merge(1)

            for h in range(HEADS):
                if h:
                    dve.wait_ge(S["ho_psum"], h)
                for b in range(NBLK):
                    u = 4 * h + b // 4
                    if b % 4 == 0:
                        dve.wait_ge(S["u_psum"], u + 1)
                    ub = bank[4 + u % 3][:, (b % 4) * P:(b % 4 + 1) * P]
                    if b == 0:
                        ins = V.tensor_copy(state[:, 0, :], ub)
                    else:
                        ins = V.scalar_tensor_tensor(state[:, b, :], state[:, b - 1, :], decay[:, NBLK * h + b, :], ub, ALU.mult, ALU.add)
                    if b % 4 == 3:
                        ins.then_inc(S["u_used"], 1)
                        dve.wait_ge(S["u_used"], u + 1)
                    else:
                        link(ins)
                V.tensor_copy(small[:, 504:505], state[:, 15, 0:1]).then_inc(S["st_ready"], 1)
                dve.wait_ge(S["hss_psum"], h + 1)
                dve.wait_ge(S["ho_evac"], 2 * h + 2)
                inverse_root(hg_rs, bank[3][:, 0:SEQ], RMS_EPS, 2 + h)
                link(V.scalar_tensor_tensor(hg_rs, hg_rs, v_("hnorm", h), hg_o, ALU.mult, ALU.mult))
                V.tensor_tensor(yT[:, 0, h, :], hg_rs, hg_g[:, h * SEQ:(h + 1) * SEQ], ALU.mult).then_inc(S["yA_ready"], 1)
            dve.wait_ge(S["yA_ready"], HEADS)
            merge(0)
            V.memset(wTd, 0.0)
            V.memset(b2_all, 0.0)
            V.memset(b1_all, 0.0).then_inc(S["b_clear"], 1)

            def norm(half, dst, src, nth):
                st_ = small[:, 300:312].rearrange("p (a b) -> p a b", a=2)
                for dh in range(2):
                    link(V.bn_stats(st_[:, dh, :], src[:, half, 512 * dh:512 * dh + 512]))
                link(V.bn_aggr(small[:, 312:314], st_))
                inverse_root(small[:, 314:315], small[:, 313:314], LN_EPS, nth)
                link(V.tensor_scalar(src[:, half, :], src[:, half, :], small[:, 312:313], small[:, 314:315], ALU.subtract, ALU.mult))
                link(V.tensor_tensor(src[:, half, :], src[:, half, :], ln_w, ALU.mult))
                return V.tensor_tensor(dst[:, half, :], src[:, half, :], ln_b, ALU.add)

            dve.wait_ge(S["xres_in"], 16)
            dve.wait_ge(S["ln_in"], 32)
            dve.wait_ge(S["chunk_used"], len(STREAM))
            for half in range(2):
                for dh in range(2):
                    link(V.scalar_tensor_tensor(x_res[:, half, 512 * dh:512 * dh + 512], x_res[:, half, 512 * dh:512 * dh + 512], ALPHA,
                                                bank[4 + 2 * half + dh][:, :], ALU.mult, ALU.add))
                norm(half, h_tok, x_res, 6 + half).then_inc(S["h_ready"], 1)
            dve.wait_ge(S["h_ready"], 2)
            dve.wait_ge(S["logit_psum"], 1)
            dve.wait_ge(S["rb_in"], 16)
            for half in range(2):
                link(V.tensor_tensor(logits[:, half, :], bank[4][:, half * NE:half * NE + NE], rb, ALU.add))
                link(V.max(top[:, half, :], logits[:, half, :]))
                link(V.max_index(top_i[:, half, :], top[:, half, :], logits[:, half, :]))
                ins = V.tensor_scalar(small[:, 232 + half:233 + half], top[:, half, 0:1], -1.0, None, ALU.mult)
                if half == 0:
                    link(ins)
            ins.then_inc(S["topexp_req"], 1)
            link(V.tensor_copy(sm(320, 16).rearrange("p (a b) -> p a b", a=2), top_i[:, :, :]))
            link(V.memset(wfull, 0.0))
            link(V.memset(rank, -1.0))
            link(V.memset(member, 0.0))
            dve.wait_ge(S["topexp_ready"], 2)
            link(V.reciprocal(small[:, 238:240], small[:, 236:238]))
            for half in range(2):
                link(V.tensor_scalar(small[:, 216 + 8 * half:220 + 8 * half], small[:, 216 + 8 * half:220 + 8 * half], small[:, 238 + half:239 + half], None, ALU.mult))
                for j in range(TOPK):
                    place = small[:, 320 + 8 * half + j:321 + 8 * half + j]
                    link(V.tensor_scalar(oneh, iota[:, 0:NE], place, None, ALU.is_equal))
                    link(V.tensor_tensor(member[:, half, :], member[:, half, :], oneh, ALU.add))
                    link(V.scalar_tensor_tensor(wfull[:, half, 0:NE], oneh, small[:, 216 + 8 * half + j:217 + 8 * half + j], wfull[:, half, 0:NE], ALU.mult, ALU.add))
            V.tensor_copy(small[:, 506:507], wfull[:, 1, 31:32]).then_inc(S["route_ready"], 1)
            dve.wait_ge(S["rank_psum"], 1)
            rk_ = rank[:, :, 0:NE]
            link(V.scalar_tensor_tensor(rk_, bank[4][:, 0:2 * NE].rearrange("p (a b) -> p a b", a=2), 1.0, member, ALU.add, ALU.mult))
            link(V.tensor_scalar(rk_, rk_, -1.0, None, ALU.add))

            def select(g, u, e, off=None):
                for half in range(2):
                    rk = rank[:, half, bass.ds(e, 1)]
                    w = wfull[:, half, bass.ds(e, 1)]
                    if off is None:
                        V.tensor_scalar(sel[:, half, :], iota[:, 0:CAP], rk, None, ALU.is_equal)
                        link(V.tensor_scalar(wsel[:, half, u * CAP:(u + 1) * CAP], iota[:, 0:CAP], rk, w, ALU.is_equal, ALU.mult))
                    else:
                        link(V.tensor_scalar(sel[:, half, :], iota[:, 0:CAP], off, rk, ALU.add, ALU.is_equal))
                        link(V.tensor_scalar(wsel[:, half, 0:CAP], sel[:, half, :], w, None, ALU.mult))
                V.tensor_scalar(esel, ones[:, 0:CAP], ident[:, bass.ds(e, 1)], None, ALU.mult).then_inc(S["sel_ready"], 1)

            select(0, 0, 0)
            dve.wait_ge(S["b2_psum"], 1)
            for half in range(2):
                for dh in range(2):
                    link(V.scalar_tensor_tensor(y_acc[:, half, 512 * dh:512 * dh + 512], h_tok[:, half, 512 * dh:512 * dh + 512], ALPHA,
                                                bank[(2, 3, 6, 7)[2 * half + dh]][:, :], ALU.mult, ALU.add))
            V.tensor_copy(small[:, 508:509], y_acc[:, 1, 0:1]).then_inc(S["b2_used"], 1)
            code = cand[:, 2, :].rearrange("p (a b) -> p a b", b=3)
            for b in range(3):
                link(V.tensor_scalar(cand[:, 0, :].rearrange("p (a b) -> p a b", b=3)[:, :, b:b + 1], bank[4][:, 2 * NE:3 * NE].unsqueeze(2),
                                     float(CAP * (b + 1)), None, ALU.is_gt))
            link(V.tensor_tensor_scan(cand[:, 1, :], ones[:, 0:96], cand[:, 0, :], 0.0, ALU.mult, ALU.add))
            link(V.tensor_copy(small[:, 507:508], cand[:, 1, 95:96]))
            link(V.tensor_tensor(cand[:, 1, :], cand[:, 1, :], cand[:, 0, :], ALU.mult))
            for dst, expert_code in ((item_ef, True), (item_off, False)):
                for b in range(3):
                    link(V.tensor_scalar(code[:, :, b:b + 1], iota[:, 0:NE].unsqueeze(2), 1.0 if expert_code else 0.0,
                                         0.0 if expert_code else float(CAP * (b + 1)), ALU.mult, ALU.add))
                link(V.tensor_scalar(small[:, 340:356], iota[:, 0:NITEM], 1.0, None, ALU.add))
                link(V.tensor_tensor(cmp, cand[:, 1, :].unsqueeze(1).to_broadcast([P, NITEM, 96]),
                                     small[:, 340:356].unsqueeze(2).to_broadcast([P, NITEM, 96]), ALU.is_equal))
                link(V.tensor_tensor(cmp, cmp, cand[:, 2, :].unsqueeze(1).to_broadcast([P, NITEM, 96]), ALU.mult))
                link(V.tensor_reduce(dst, cmp, X, ALU.add))
            link(V.tensor_copy(item_e[0:1, 0:NITEM], item_ef[0:1, :]))
            V.tensor_copy(item_e[0:1, NITEM:NITEM + 1], small[0:1, 507:508]).then_inc(S["items_ready"], 1)
            dve.wait_ge(S["items_ready"], 1)

            before = vc[0]

            def swiglu(n, u, hb):
                dve.wait_ge(S["expert_chunk_used"], n * R2S + 8)
                V.tensor_scalar(g1, bank[2 * hb][:, :], LIMIT, None, ALU.min).then_inc(S["gmin_ready"], 1)
                link(V.tensor_scalar(g2, bank[2 * hb + 1][:, :], LIMIT, -LIMIT, ALU.min, ALU.max))
                dve.wait_ge(S["sig_ready"], n + 1)
                link(V.scalar_tensor_tensor(g2, g2, 1.0, g1, ALU.add, ALU.mult))
                V.tensor_tensor(g1, g2, g3, ALU.mult).then_inc(S["act_ready"], 1)
                dve.wait_ge(S["expert_chunk_used"], n * R2S + R2S)
                V.tensor_copy(y_pair[64 * u:64 * u + 64, 512:1024], bank[4][64:128, :]).then_inc(S["ypair_vec"], 1)

            def combine(m_):
                for i in range(4):
                    half, dh = i // 2, i % 2
                    dst = y_acc[:, half, 512 * dh:512 * dh + 512]
                    dve.wait_ge(S["comb_psum"], m_ * 4 + i + 1)
                    V.tensor_tensor(dst, dst, bank[6 + i % 2][:, :], ALU.add).then_inc(S["comb_used"], 1)

            with dve.Fori(0, NPAIR) as p:
                base[0] = p * 8
                dve.wait_ge(S["xg_psum"], p * 2 + 1)
                select(p * 2 + 1, 1, p * 2 + 1)
                swiglu(p * 2, 0, 0)
                dve.wait_ge(S["xg_psum"], p * 2 + 2)
                dve.wait_ge(S["wselT_psum"], p + 1)
                select(p * 2 + 2, 0, p * 2 + 2)
                swiglu(p * 2 + 1, 1, 1)
                combine(p)
            per_pair = vc[0] - before
            assert per_pair == 8, per_pair
            n_items = dve.value_load(item_e[0:1, NITEM:NITEM + 1], min_val=0, max_val=NITEM)
            before = vc[0]
            with dve.If(n_items > 0):
                with dve.Fori(0, n_items) as j:
                    base[0] = j * 6 + (NPAIR - 1) * 8
                    e = dve.value_load(item_e[0:1, bass.ds(j, 1)], min_val=0, max_val=NE - 1)
                    select(j + NE + 1, 0, e, item_off[:, bass.ds(j, 1)])
                    swiglu(j + NE, 0, 1)
                    combine(j + NPAIR)
            assert vc[0] - before == 6, vc[0] - before
            dve.wait_ge(S["ln2_in"], 32)
            tail[0] = True

            for half in range(2):
                st_ = small[:, 300:312].rearrange("p (a b) -> p a b", a=2)
                src = y_acc
                for dh in range(2):
                    link(V.bn_stats(st_[:, dh, :], src[:, half, 512 * dh:512 * dh + 512]))
                link(V.bn_aggr(small[:, 312:314], st_))
                inverse_root(small[:, 314:315], small[:, 313:314], LN_EPS, 8 + half)
                link(V.tensor_scalar(src[:, half, :], src[:, half, :], small[:, 312:313], small[:, 314:315], ALU.subtract, ALU.mult))
                link(V.tensor_tensor(src[:, half, :], src[:, half, :], ln_w, ALU.mult))
                ins = V.tensor_tensor(src[:, half, :], src[:, half, :], ln_b, ALU.add)
                if half == 0:
                    link(ins)
            ins.then_inc(S["out_ready"], 1)


SHAPES = {
    "x": None, "positions": None, "w_in": (1024, 8128), "b_gate": (32, 128), "hgrn_lb_logits": (4, 128), "hgrn_norm_w": (4, 128),
    "mla_q_norm_w": (2, 128), "mla_wq_b": (256, 768), "mla_kv_norm_w": (1, 128), "mla_wkv_b": (128, 1024),
    "s5_a_re": (16, 128), "s5_a_im": (16, 128), "s5_log_dt": (16, 2), "s5_b_re": (2048, 16), "s5_b_im": (2048, 16),
    "s5_c_re": (512, 64), "s5_c_im": (512, 64), "s5_d": (4, 128), "s5_w_glu": (512, 512), "s5_b_glu": (4, 128),
    "lru_conv_w": (16, 128), "lru_conv_b": (4, 128), "lru_wa": (8, 64, 64), "lru_ba": (4, 128), "lru_wx": (8, 64, 64), "lru_bx": (4, 128),
    "lru_a_param": (4, 128), "w_branch": (4, 512, 1024), "w_out": (1024, 1024), "ln1_w": (1, 1024), "ln1_b": (1, 1024),
    "ln2_w": (1, 1024), "ln2_b": (1, 1024), "router_w": (1024, 32), "router_b": (1, 32),
    "moe_w1": (32, 1024, 2048), "moe_b1": (32, 2048), "moe_w2": (32, 1024, 1024), "moe_b2": (32, 1024),
}


def kernel(**inputs):
    import numpy as _np
    import concourse.bacc as _bacc
    from concourse import mybir as _mybir
    from concourse.bass_utils import run_bass_kernel_spmd as _run

    nc = _bacc.Bacc("TRN2", target_bir_lowering=False, num_devices=1)
    arrays, aps = {}, {}
    for name, shape in SHAPES.items():
        a = _np.ascontiguousarray(inputs[name])
        if shape is not None:
            a = a.reshape(shape)
        arrays["in_" + name] = a
    freq = _np.float32(10000.0) ** (-_np.arange(0, ROPE, 2, dtype=_np.float32) / _np.float32(ROPE))
    arrays["in_inv_freq"] = _np.ascontiguousarray(_np.tile(freq, HEADS).reshape(P, 1).astype(_np.float32))
    for name, a in arrays.items():
        aps[name[3:]] = nc.dram_tensor(name, a.shape, _mybir.dt.from_np(a.dtype), kind="ExternalInput").ap()
    out = nc.dram_tensor("out", (1, SEQ, D), F32, kind="ExternalOutput").ap()
    encoder_layer(nc, aps, out)
    r = _run(nc, [arrays], core_ids=[0])
    return r.results[0]["out"]
```

```python
from contextlib import ExitStack

import numpy as np

import concourse.bass as bass
from concourse import mybir

ALU = mybir.AluOpType
ACT = mybir.ActivationFunctionType
F32 = mybir.dt.float32
I32 = mybir.dt.int32
U32 = mybir.dt.uint32
X = mybir.AxisListType.X

P = 128
SEQ = 256
D = 1024
KD = D // P
TH = SEQ // P
HEADS = 4
BLK = 16
NBLK = SEQ // BLK
HB = HEADS * NBLK
Q_RANK, KV_RANK, NOPE, ROPE, VD = 256, 128, 128, 64, 128
QK = NOPE + ROPE
R2 = ROPE // 2
CHUNK = 64
MASK_VALUE = -1e30
SM = float(QK) ** -0.5
S5T = 16
NBR = 4
BW = 512
NE = 32
TOPK = 4
FF = 1024
CAP = 64
NITEM = SEQ * TOPK // CAP
ALPHA = 2.0 ** 0.25
LN_EPS, RMS_EPS = 1e-5, 1e-6
F_MIN = 1e-30
LIMIT, SWA = 7.0, 1.702
TWO_PI = 2.0 * np.pi
INV2PI = float(np.float32(1.0 / TWO_PI))
MAGIC = 12582912.0
C1 = 6.28125
C2 = float(np.float32(TWO_PI - C1))
C3 = float(TWO_PI - C1 - np.float64(np.float32(TWO_PI - C1)))
PI_LOW = 3.1415925
TWO_PI_LOW = 6.2831850

HQ, HF, HI, HG, CQ, CKV, SU, LX, LG, GL = 0, 512, 1024, 1536, 2048, 2304, 2496, 3008, 3520, 4032
CW = 256
SLOT = 2048
R1 = 8
R2S = 12

VR = {}
_at = 0
for _name, _n in (("a_re", 16), ("a_im", 16), ("hnorm", 4), ("qnorm", 2), ("kvnorm", 1), ("dskip", 4), ("bglu", 4),
                  ("convw", 16), ("convb", 4), ("ba", 4), ("bx", 4), ("apar", 4), ("lb", 4), ("bgate", 32)):
    VR[_name] = _at
    _at += _n
NVEC = _at


def weight_stream():
    s = [("lx", 0), ("lx", 1), ("su", 0), ("su", 1), ("lg", 0), ("lg", 1), ("cq", 0)]
    for h in range(8):
        s += [("gl", 2 * h), ("gl", 2 * h + 1)]
    s += [("ckv", 0), ("hf", 0), ("wglu", 0), ("wq", 0), ("wkv", 0)]
    s += [("hf", 1), ("hq", 0), ("hq", 1), ("hi", 0), ("hi", 1), ("hg", 0), ("hg", 1)]
    for br in (3, 2, 1, 0):
        s += [("wb", br, 0), ("wb", br, 1)]
    s += [("wo", i) for i in range(4)]
    return s


COL = {"lx": LX, "lg": LG, "su": SU, "cq": CQ, "ckv": CKV, "gl": GL, "hf": HF, "hq": HQ, "hi": HI, "hg": HG}
STREAM = weight_stream()
PROJ = [c for c in STREAM if c[0] in COL]
NPAIR = NE // 2
AHEAD = NPAIR // 2
MIX_BANK = ((0, 1), (5, 6))
HT_BANK = ((2, 3), (5, 7))
U_BANK = (0, 1, 5, 6)


def encoder_layer(nc, A, out, dbg=None):
    with ExitStack() as ctx:
        def sb(name, shape, dt=F32):
            return ctx.enter_context(nc.sbuf_tensor(name, shape, dt))

        def sem(name):
            return ctx.enter_context(nc.semaphore(name))

        banks = ctx.enter_context(nc.psum_tensor("banks", [P, 8, 512], F32))
        bank = [banks[:, i, :] for i in range(8)]

        ring = sb("ring", [P, R2S * SLOT])
        merge_gate = ring[:, R1 * SLOT:].rearrange("p (c t) -> p c t", t=SEQ)
        ident = sb("ident", [P, P])
        ones = sb("ones", [P, P])
        ones_128 = sb("ones_128", [P, P])
        ones_256 = sb("ones_256", [P, P])
        earlier = sb("earlier", [P, P])
        blockmask = sb("blockmask", [P, 8])
        headmask = sb("headmask", [P, HEADS])
        oddmask = sb("oddmask", [P, 2])
        half_pi = sb("half_pi", [P, 1])
        iota_i = sb("iota_i", [P, SEQ], I32)
        iota = sb("iota", [P, SEQ])
        vec = sb("vec", [P, NVEC])
        small = sb("small", [P, 512])
        acc = sb("acc", [P, KD, SEQ])
        yT = sb("yT", [P, NBR, HEADS, SEQ])
        xT = sb("xT", [P, KD, SEQ])
        ARENA = 16912
        arena = sb("arena", [P, ARENA])

        def at(off, *shape):
            n = int(np.prod(shape))
            assert off + n <= ARENA, (off, shape, ARENA)
            v = arena[:, off:off + n]
            if len(shape) == 1:
                return v
            names = "abcd"[:len(shape)]
            return v.rearrange(f"p ({' '.join(names)}) -> p {' '.join(names)}", **dict(zip(names[1:], shape[1:])))

        class At:
            def __init__(self, base):
                self.o = base

            def __call__(self, *shape):
                v = at(self.o, *shape)
                self.o += int(np.prod(shape))
                return v

        m = At(0)
        su = m(4, SEQ)
        s_raw = m(4, 256)
        b_exp = m(2, 16, 32)
        c_exp = m(2, 4, 128)
        bT = m(2, 4, 128)
        cT = m(2, 4, 128)
        sinT, cosT = [None, None], [None, None]
        for i in range(2):
            sinT[i], cosT[i] = m(4, SEQ), m(4, SEQ)
        t1, t2 = m(2, SEQ), m(2, SEQ)
        s5_end = m.o
        xr = [at(1024, 2, SEQ), at(2048, 2, SEQ)]
        xi = [at(1536, 2, SEQ), at(2560, 2, SEQ)]
        zr, zi = at(3072, 2, SEQ), at(3584, 2, SEQ)
        s_out = yT[:, 1]
        lx = m(4, SEQ + 4)
        xc = m(4, SEQ)
        lr_r = m(4, SEQ)
        lr_i = m(4, SEQ)
        lr_t = m(4, SEQ)
        lr_g = yT[:, 3]
        cq_s = m(2, SEQ)
        m = At(0)
        hg_f, hg_q, hg_k = m(4 * SEQ), m(4 * SEQ), m(4 * SEQ)
        grow = m(HB, BLK)
        decay = m(HB, 1)
        prod = [m(HB, BLK), m(HB, BLK)]
        q_inter = m(4 * SEQ)
        hg_kT = hg_f.rearrange("p (a b) -> p a b", a=8)
        hg_bd = hg_q.rearrange("p (a b) -> p a b", a=8)
        second = m.o
        v_exp = [m(8, P), m(8, P)] + [v.rearrange("p a b -> p (a b)").rearrange("p (a b) -> p a b", a=8) for v in prod]
        state = [m(NBLK, P), m(NBLK, P)]
        hg_rs = [m(SEQ), m(SEQ)]
        m_tmp = m(512)
        hg_v, hg_g = m(2, 512), m(4 * SEQ)
        hg_o, hg_sq = ([hg_k[:, (2 * i + j) * SEQ:(2 * i + j + 1) * SEQ] for j in range(2)] for i in range(2))
        m = At(second)
        cq = m(2, SEQ)
        ckv = m(SEQ)
        sq = m(3, SEQ)
        rst = m(2, SEQ)
        qn = m(4, SEQ)
        kn = m(4, SEQ)
        vv = m(2, 512)
        rp1, rp2 = m(2, SEQ), m(2, SEQ)
        tA, tB = m(2, SEQ), m(2, SEQ)
        wa = sb("wa", [P, 4, P])
        wx = sb("wx", [P, 4, P])
        cos_p, sin_p = wa[:, 0:2, :].rearrange("p a b -> p (a b)"), wa[:, 2:4, :].rearrange("p a b -> p (a b)")
        ang = wx[:, 0:2, :].rearrange("p a b -> p (a b)")
        ang2 = wx[:, 2:4, :].rearrange("p a b -> p (a b)")
        qm1 = acc[:, 0:4, :]
        qm2 = acc[:, 4:8, :]
        probs = [rst[:, i, :] for i in range(2)]
        probsT = [sq.rearrange("p a b -> p (a b)")[:, i * SEQ:(i + 1) * SEQ].rearrange("p (a b) -> p a b", a=2) for i in range(2)]
        rows = sb("rows", [P, P])
        inv_freq = sb("inv_freq", [P, 1])
        pos_i = iota_i
        x_tok = acc[:, :, :].rearrange("p (h k) t -> p h (k t)", h=2)
        m = At(0)
        ALT = 5
        alt = [yT[:, 0:2].rearrange("p a b c -> p (a b c)"), yT[:, 2:4].rearrange("p a b c -> p (a b c)"),
               acc[:, :, :].rearrange("p a b -> p (a b)"), xT[:, :, :].rearrange("p a b -> p (a b)")]
        alt.append(at(4 * D, 2 * D))
        h_tok = m(2, D)
        y_acc = m(2, D)
        assert m.o == 4 * D
        ln_w, ln_b = m(D), m(D)
        b1_all = m(2 * FF)
        xg = m(KD, CAP)
        g1, g2, g3 = m(512), m(512), m(512)
        actT = m(4, P)
        y_pair = m(D)
        wselT = m(2, P)
        hT = xT
        sel = m(2, CAP)
        wsel = m(2, P)
        esel = m(CAP)
        logits = m(2, NE)
        wfull, rank = m(2, NE + 1), m(2, NE + 1)
        member = m(2, NE)
        top = m(2, 8)
        b2_all = m(D)
        cmp = m(NITEM, 96)
        oneh = cmp.rearrange("p a b -> p (a b)")[:, 0:2 * TOPK * NE].rearrange("p (a b) -> p a b", b=NE)
        wTd = m(2, P)
        rb = m(NE)
        rw = m(KD, NE)
        item_off = m(NITEM)
        item_ef = m(NITEM)
        cand = m(3, 96)
        top_i = sb("top_i", [P, 2, 8], U32)
        item_e = sb("item_e", [1, 32], I32)
        x_res = y_acc

        landed = [sem(f"landed{i}") for i in range(R2S)]
        alt_landed = [sem(f"alt_landed{i}") for i in range(ALT)]
        names = """chunk_used const_ready iota_ready iota_read x_in vec_in dt_in s5_in lru_in pos_in xT_psum xT_vec vec_psum vec_ready
            dt_rows dt_exp s5_small s5_mag s5_theta s5_trig0 exp_ready prep_psum prep_evac f_ready trig_ready bu_psum bu_free x_ready x_used
            y_evac gelu_ready glu_psum glu_gate yC_ready proj_evac xc_ready gate_psum gate_act absa_ready expa_ready sp_ready
            lru_exp lru_b2 lru_sqrt yD_ready cos_req cos_ready sq_ready ss_psum norm_ready mla_psum mla_evac mla_masked
            s_psum smax_ready sexp_ready p_norm pT_psum pT_ready o_psum o_evac lbe_req lbe_ready g_ready p_ready p_used hgT_psum kT_ready bd_ready
            vx_ready u_psum u_used st_ready ho_psum ho_evac hss_psum yA_ready merge_psum merge_used acc_ready xres_in ln_in h_ready
            hT_psum hT_act rw_in logit_psum rs_req rs_ready rb_in b_in b_clear topexp_req topexp_ready route_ready rank_psum wT_psum wT_ready b2_psum b2_used
            esel_ready sel_ready member_ready mix_psum prod_clear xg_psum xg_ready expert_chunk_used gmin_ready sig_ready act_ready at_psum at_ready ypair_vec ypair_act
            wselT_psum wselT_ready comb_psum comb_used ln2_in out_ready out_sent v_chain f_chain a_chain g_chain items_ready
            """.split()
        S = {n: sem(n) for n in names}

        def v_(name, i=0, n=1):
            return vec[:, VR[name] + i:VR[name] + i + n]

        slot_of = {c: i % R1 for i, c in enumerate(STREAM)}
        uses = [0] * R2S
        need = {}
        for i, c in enumerate(STREAM):
            uses[i % R1] += 1
            need[c] = 16 * uses[i % R1]
        last_in_slot = [max(i for i in range(len(STREAM)) if i % R1 == s) for s in range(R1)]

        def slot(s, *shape):
            n = int(np.prod(shape))
            v = ring[:, s * SLOT:s * SLOT + n]
            names = "abcd"[:len(shape)]
            return v.rearrange(f"p ({' '.join(names)}) -> p {' '.join(names)}", **dict(zip(names[1:], shape[1:])))

        w_in = A["w_in"].rearrange("(k p) n -> p k n", p=P)
        w1 = A["moe_w1"]
        w2 = A["moe_w2"]

        def chunk_source(c):
            if c[0] in COL:
                lo = COL[c[0]] + CW * c[1]
                w = 192 if c[0] == "ckv" else CW
                return (KD, w), w_in[:, :, lo:lo + w]
            if c[0] == "wglu":
                return (4, 512), A["s5_w_glu"].rearrange("(k p) n -> p k n", p=P)
            if c[0] == "wq":
                return (2, 768), A["mla_wq_b"].rearrange("(k p) n -> p k n", p=P)
            if c[0] == "wkv":
                return (1, 1024), A["mla_wkv_b"].rearrange("(k p) n -> p k n", p=P)
            if c[0] == "wb":
                return (4, 512), A["w_branch"][c[1]].rearrange("(k p) n -> p k n", p=P)[:, :, 512 * c[2]:512 * c[2] + 512]
            return (2, D), A["w_out"][256 * c[1]:256 * c[1] + 256, :].rearrange("(k p) n -> p k n", p=P)

        block = ctx.enter_context(nc.Block())

        def expert_source(e, c):
            if c < 8:
                return w1[e, P * c:P * c + P, :]
            return w2[e, 256 * (c - 8):256 * (c - 8) + 256, :].rearrange("(k p) n -> p k n", p=P)

        def expert_slot(c, odd=0):
            if odd and c < ALT:
                return alt[c]
            return slot(c, SLOT) if c < 8 else slot(c, 2, D)

        def landed_of(c, odd=0):
            return alt_landed[c] if odd and c < ALT else landed[c]

        def landed_count(c, n, odd):
            if c >= ALT:
                return (n + 1) * 16 + 16 * uses[c]
            if odd:
                return (n + 1) * 8
            return n * 8 + 16 + 16 * uses[c]

        @block.sync
        def _(sp):
            sp.dma_start(x_tok, A["x"][0].rearrange("(h p) n -> p h n", p=P)).then_inc(S["x_in"], 16)
            for i, c in enumerate(STREAM):
                if i == 2:
                    sp.wait_ge(S["vec_in"], 16 * 14)
                if i >= R1:
                    sp.wait_ge(S["chunk_used"], i - R1 + 1)
                shape, src = chunk_source(c)
                sp.dma_start(slot(i % R1, *shape), src).then_inc(landed[i % R1], 16)
            early = sorted(range(R1), key=lambda c: last_in_slot[c])
            early, late = early[:4], early[4:]
            for c in early + list(range(R1, R2S)) + late:
                if c < R1:
                    sp.wait_ge(S["chunk_used"], last_in_slot[c] + 1)
                elif c == R1:
                    sp.wait_ge(S["acc_ready"], 4)
                sp.dma_start(expert_slot(c), expert_source(0, c)).then_inc(landed[c], 16)

            for c in range(ALT):
                if c == 0:
                    sp.wait_ge(S["chunk_used"], len(STREAM))
                elif c == 3:
                    sp.wait_ge(S["logit_psum"], 1)
                elif c == 4:
                    sp.wait_ge(S["h_ready"], 2)
                sp.dma_start(expert_slot(c, 1), expert_source(1, c)).then_inc(landed_of(c, 1), 16)

            def load(e, odd, c, passes):
                sp.wait_ge(S["expert_chunk_used"], (passes - 1) * R2S + c + 1)
                sp.dma_start(expert_slot(c, odd), expert_source(e, c)).then_inc(landed_of(c, odd), 16)

            def first_chunks(n, odd):
                for c in range(ALT):
                    load(n + 2, odd, c, n + 1)

            def other_chunks(n, odd):
                for c in range(ALT, R2S):
                    load(n + 1, 1 - odd, c, n + 1)

            with sp.Fori(0, AHEAD) as p:
                for odd in range(2):
                    first_chunks(p * 2 + odd, odd)
                    other_chunks(p * 2 + odd, odd)
            with sp.Fori(AHEAD, NPAIR - 1) as p:
                for odd in range(2):
                    other_chunks(p * 2 + odd, odd)
                    first_chunks(p * 2 + odd, odd)
            other_chunks(NE - 2, 0)
            sp.wait_ge(S["expert_chunk_used"], (NE - 1) * R2S + ALT)
            sp.dma_start(ln_w, A["ln2_w"].to_broadcast([P, D])).then_inc(S["ln2_in"], 16)
            sp.dma_start(ln_b, A["ln2_b"].to_broadcast([P, D])).then_inc(S["ln2_in"], 16)
            sp.wait_ge(S["items_ready"], 1)
            n_items = sp.value_load(item_e[0:1, NITEM:NITEM + 1], min_val=0, max_val=NITEM)
            with sp.If(n_items > 0):
                with sp.Fori(0, n_items) as j:
                    e = sp.value_load(item_e[0:1, bass.ds(j, 1)], min_val=0, max_val=NE - 1)
                    for c in range(R2S):
                        sp.wait_ge(S["expert_chunk_used"], (j + NE - 1) * R2S + c + 1)
                        sp.dma_start(expert_slot(c), expert_source(e, c)).then_inc(landed[c], 16)
            for half in range(2):
                sp.wait_ge(S["out_ready"], half + 1)
                sp.dma_start(out[0][half * P:half * P + P, :], y_acc[:, half, :]).then_inc(S["out_sent"], 16)
            sp.wait_ge(S["out_sent"], 32)

        @block.gpsimd
        def _(pool):
            g = [0]

            def link(ins):
                g[0] += 1
                ins.then_inc(S["g_chain"], 1)
                pool.wait_ge(S["g_chain"], g[0])

            link(nc.gpsimd.memset(ident[:, :], 0.0))
            link(nc.gpsimd.affine_select(out=ident[:, :], in_=ident[:, :], compare_op=ALU.not_equal, fill=1.0,
                                         base=0, pattern=[[-1, P]], channel_multiplier=1))
            nc.gpsimd.memset(ones[:, :], 1.0).then_inc(S["const_ready"], 1)
            nc.gpsimd.memset(ones_128[:, :], 1.0 / 128).then_inc(S["const_ready"], 1)
            nc.gpsimd.memset(ones_256[:, :], 1.0 / 256).then_inc(S["const_ready"], 1)
            nc.gpsimd.memset(half_pi[:, :], float(np.pi / 2)).then_inc(S["const_ready"], 1)
            nc.gpsimd.iota(iota_i[:, :], pattern=[[1, SEQ]], base=0, channel_multiplier=0).then_inc(S["iota_ready"], 1)
            nc.gpsimd.memset(wa[:, :, :], 0.0).then_inc(S["const_ready"], 1)
            nc.gpsimd.memset(wx[:, :, :], 0.0).then_inc(S["const_ready"], 1)
            link(nc.gpsimd.memset(blockmask[:, :], 1.0))
            link(nc.gpsimd.affine_select(out=blockmask[:, :], in_=blockmask[:, :], compare_op=ALU.is_ge, fill=0.0,
                                         base=0, pattern=[[-16, 8]], channel_multiplier=1))
            link(nc.gpsimd.affine_select(out=blockmask[:, :], in_=blockmask[:, :], compare_op=ALU.is_ge, fill=0.0,
                                         base=15, pattern=[[16, 8]], channel_multiplier=-1))
            link(nc.gpsimd.memset(headmask[:, :], 1.0))
            link(nc.gpsimd.affine_select(out=headmask[:, :], in_=headmask[:, :], compare_op=ALU.is_ge, fill=0.0,
                                         base=0, pattern=[[-32, HEADS]], channel_multiplier=1))
            link(nc.gpsimd.affine_select(out=headmask[:, :], in_=headmask[:, :], compare_op=ALU.is_ge, fill=0.0,
                                         base=31, pattern=[[32, HEADS]], channel_multiplier=-1))
            link(nc.gpsimd.memset(earlier[:, :], 1.0))
            nc.gpsimd.affine_select(out=earlier[:, :], in_=earlier[:, :], compare_op=ALU.is_gt, fill=0.0,
                                    base=0, pattern=[[1, P]], channel_multiplier=-1).then_inc(S["const_ready"], 1)
            pool.wait_ge(S["x_used"], 8)
            pool.wait_ge(S["x_ready"], 8)
            for i in range(2):
                nc.gpsimd.memset(prod[i], 0.0).then_inc(S["prod_clear"], 1)
            pool.wait_ge(S["proj_evac"], PROJ.index(("hi", 1)) + 1)
            pool.wait_ge(S["o_evac"], 4)
            for n in range(8):
                h, half = n // 2, n % 2
                if n == 2:
                    pool.wait_ge(S["p_used"], BLK)
                if n >= 4:
                    pool.wait_ge(S["u_psum"], 2 * (n - 3))
                nc.gpsimd.tensor_tensor(v_exp[n % 4], hg_v[:, half, h * P:h * P + P].unsqueeze(1).to_broadcast([P, 8, P]),
                                        blockmask[:, :].unsqueeze(2).to_broadcast([P, 8, P]), ALU.mult).then_inc(S["vx_ready"], 1)

        NCONST = 7

        @block.scalar
        def _(act):
            ac = [0]

            def link(ins):
                ac[0] += 1
                ins.then_inc(S["a_chain"], 1)
                act.wait_ge(S["a_chain"], ac[0])

            nvec = 0
            for name, src in (("a_re", "s5_a_re"), ("a_im", "s5_a_im"), ("hnorm", "hgrn_norm_w"), ("qnorm", "mla_q_norm_w"),
                              ("kvnorm", "mla_kv_norm_w"), ("dskip", "s5_d"), ("bglu", "s5_b_glu"), ("convw", "lru_conv_w"),
                              ("convb", "lru_conv_b"), ("ba", "lru_ba"), ("bx", "lru_bx"), ("apar", "lru_a_param"),
                              ("lb", "hgrn_lb_logits"), ("bgate", "b_gate")):
                n = A[src].shape[0]
                act.dma_start(rows[VR[name]:VR[name] + n, :], A[src]).then_inc(S["vec_in"], 16)
                nvec += 1
            assert nvec == 14
            act.dma_start(inv_freq[:, :], A["inv_freq"]).then_inc(S["pos_in"], 16)
            act.dma_start(small[0:S5T, 0:2], A["s5_log_dt"]).then_inc(S["dt_in"], 16)
            proj_n = [0]

            def projected(c):
                i = proj_n[0]
                assert PROJ[i] == c, (PROJ[i], c)
                proj_n[0] += 1
                act.wait_ge(S["chunk_used"], STREAM.index(c) + 1)
                return bank[i % 2]

            def evac_gate(n):
                b = projected(("gl", n))
                for j in range(2):
                    ins = nc.scalar.activation(merge_gate[:, 2 * n + j, :], b[:, j * SEQ:(j + 1) * SEQ], ACT.Sigmoid,
                                               bias=v_("bgate", 2 * n + j))
                ins.then_inc(S["proj_evac"], 1)

            act.wait_ge(S["const_ready"], 6)
            for half in range(2):
                p0 = 64 * half
                for tile_, src in ((wa, "lru_wa"), (wx, "lru_wx")):
                    act.dma_start(tile_[p0:p0 + 64, :, p0:p0 + 64], A[src].rearrange("(i h) r c -> h r i c", h=2)[half]).then_inc(S["lru_in"], 16)
            act.dma_start(s_raw[:, 0, :].rearrange("p (a b) -> p a b", a=16), A["s5_b_re"].rearrange("(j q) c -> q j c", q=P)).then_inc(S["s5_in"], 16)
            act.dma_start(s_raw[:, 1, :].rearrange("p (a b) -> p a b", a=16), A["s5_b_im"].rearrange("(j q) c -> q j c", q=P)).then_inc(S["s5_in"], 16)
            act.dma_start(s_raw[:, 2, :].rearrange("p (a b) -> p a b", a=4), A["s5_c_re"].rearrange("(j q) c -> q j c", q=P)).then_inc(S["s5_in"], 16)
            act.dma_start(s_raw[:, 3, :].rearrange("p (a b) -> p a b", a=4), A["s5_c_im"].rearrange("(j q) c -> q j c", q=P)).then_inc(S["s5_in"], 16)

            act.wait_ge(S["iota_read"], 1)
            act.dma_start(pos_i[:, :], A["positions"].to_broadcast([P, SEQ])).then_inc(S["pos_in"], 16)
            for i in range(2):
                b = projected(("lx", i))
                nc.scalar.activation(lx[:, 2 * i:2 * i + 2, 3:3 + SEQ], b[:, :].rearrange("p (a b) -> p a b", a=2), ACT.Copy)\
                    .then_inc(S["proj_evac"], 1)
            act.wait_ge(S["dt_exp"], 1)
            nc.scalar.activation(small[:, 32:48], small[:, 16:32], ACT.Exp).then_inc(S["s5_small"], 1)
            act.wait_ge(S["s5_mag"], 1)
            nc.scalar.activation(small[:, 80:96], small[:, 48:64], ACT.Exp).then_inc(S["s5_small"], 1)
            act.wait_ge(S["absa_ready"], 1)
            nc.scalar.activation(small[:, 364:368], small[:, 360:364], ACT.Exp, scale=-1.0).then_inc(S["expa_ready"], 1)
            act.wait_ge(S["lbe_req"], 1)
            nc.scalar.activation(small[:, 404:408], small[:, 400:404], ACT.Exp).then_inc(S["lbe_ready"], 1)
            act.wait_ge(S["s5_theta"], 1)
            nc.scalar.activation(small[:, 112:144], small[:, 144:176], ACT.Sin).then_inc(S["s5_trig0"], 1)
            for i in range(2):
                b = projected(("su", i))
                nc.scalar.activation(su[:, 2 * i:2 * i + 2, :].rearrange("p a b -> p (a b)"), b[:, :], ACT.Copy).then_inc(S["proj_evac"], 1)
            for i in range(4):
                act.wait_ge(S["gate_psum"], i + 1)
                nc.scalar.activation(lr_r[:, i, :], bank[3 + i][:, 0:SEQ], ACT.Sigmoid, bias=v_("ba", i)).then_inc(S["gate_act"], 1)
                nc.scalar.activation(lr_i[:, i, :], bank[3 + i][:, SEQ:], ACT.Sigmoid, bias=v_("bx", i)).then_inc(S["gate_act"], 1)
            for i in range(2):
                b = projected(("lg", i))
                nc.scalar.activation(lr_g[:, 2 * i:2 * i + 2, :].rearrange("p a b -> p (a b)"), b[:, :], ACT.Gelu_apprx_tanh).then_inc(S["proj_evac"], 1)
            b = projected(("cq", 0))
            nc.scalar.activation(cq_s.rearrange("p a b -> p (a b)"), b[:, :], ACT.Copy).then_inc(S["proj_evac"], 1)
            for i in range(4):
                act.wait_ge(S["prep_psum"], i + 1)
                dst = (bT[:, 0], bT[:, 1], cT[:, 0], cT[:, 1])[i]
                nc.scalar.activation(dst.rearrange("p a b -> p (a b)"), bank[3 + i][:, :], ACT.Copy, scale=-1.0 if i == 3 else 1.0)\
                    .then_inc(S["prep_evac"], 1)

            def trig(q):
                act.wait_ge(S["f_ready"], q + 1)
                s, c = sinT[q % 2].rearrange("p a b -> p (a b)"), cosT[q % 2].rearrange("p a b -> p (a b)")
                nc.scalar.activation(s, s, ACT.Sin, scale=TWO_PI_LOW).then_inc(S["trig_ready"], 1)
                nc.scalar.activation(c, c, ACT.Sin, scale=-TWO_PI_LOW, bias=half_pi[:, 0:1]).then_inc(S["trig_ready"], 1)

            trig(0)
            trig(1)
            act.wait_ge(S["sp_ready"], 1)
            act.wait_ge(S["gate_act"], 8)
            for i in range(4):
                nc.scalar.activation(lr_t[:, i, :], lr_r[:, i, :], ACT.Tanh, scale=small[:, 380 + i:381 + i]).then_inc(S["lru_exp"], 1)
                nc.scalar.activation(lx[:, i, 0:SEQ], lr_r[:, i, :], ACT.Exp, scale=small[:, 384 + i:385 + i]).then_inc(S["lru_exp"], 1)
            act.wait_ge(S["lru_exp"], 8)
            for i in range(4):
                nc.scalar.activation(lr_r[:, i, :], lr_r[:, i, :], ACT.Exp, scale=small[:, 376 + i:377 + i]).then_inc(S["lru_exp"], 1)
            act.wait_ge(S["lru_b2"], 1)
            nc.scalar.activation(lr_t.rearrange("p a b -> p (a b)"), lr_t.rearrange("p a b -> p (a b)"), ACT.Sqrt).then_inc(S["lru_sqrt"], 1)
            for h in range(8):
                if h in (4, 6):
                    trig(h // 2)
                evac_gate(2 * h)
                evac_gate(2 * h + 1)

            def root(v, nth):
                act.wait_ge(S["rs_req"], nth)
                nc.scalar.activation(v, v, ACT.Sqrt).then_inc(S["rs_ready"], 1)

            def evac_decay(i):
                b = projected(("hf", i))
                nc.scalar.activation(hg_f[:, 512 * i:512 * i + 512], b[:, :], ACT.Sigmoid)
                nc.scalar.activation(hg_k[:, 512 * i:512 * i + 512], b[:, :], ACT.Sigmoid, scale=-1.0).then_inc(S["proj_evac"], 1)

            act.wait_ge(S["y_evac"], 4)
            nc.scalar.activation(s_out.rearrange("p a b -> p (a b)"), s_out.rearrange("p a b -> p (a b)"), ACT.Gelu_apprx_tanh).then_inc(S["gelu_ready"], 1)
            b = projected(("ckv", 0))
            act.wait_ge(S["yD_ready"], 1)
            nc.scalar.activation(ckv, b[:, 0:SEQ], ACT.Copy).then_inc(S["proj_evac"], 1)
            evac_decay(0)
            root(rst.rearrange("p a b -> p (a b)"), 1)
            for i in range(4):
                if i == 0:
                    act.wait_ge(S["glu_psum"], 1)
                if i == 2:
                    act.wait_ge(S["chunk_used"], STREAM.index(("wglu", 0)) + 1)
                nc.scalar.activation(yT[:, 2, i, :], bank[5 + i // 2][:, (i % 2) * SEQ:(i % 2 + 1) * SEQ], ACT.Sigmoid, bias=v_("bglu", i))\
                    .then_inc(S["glu_gate"], 1)
            act.wait_ge(S["cos_req"], 1)
            nc.scalar.activation(sin_p, ang, ACT.Sin).then_inc(S["cos_ready"], 1)
            nc.scalar.activation(cos_p, ang2, ACT.Sin).then_inc(S["cos_ready"], 1)
            for n in range(6):
                if n < 5:
                    act.wait_ge(S["mla_psum"], n + 1)
                else:
                    act.wait_ge(S["chunk_used"], STREAM.index(("wkv", 0)) + 1)
                dst = (qn[:, 0:2], qn[:, 2:4], kn[:, 0:2], kn[:, 2:4], vv[:, 0], vv[:, 1])[n]
                if n < 4:
                    dst = dst.rearrange("p a b -> p (a b)")
                nc.scalar.activation(dst, bank[(6, 7, 5, 6, 7, 5)[n]][:, :], ACT.Copy).then_inc(S["mla_evac"], 1)
            evac_decay(1)
            for i in range(2):
                b = projected(("hq", i))
                nc.scalar.activation(hg_q[:, 512 * i:512 * i + 512], b[:, :], ACT.Silu).then_inc(S["proj_evac"], 1)
            act.wait_ge(S["yC_ready"], 1)
            for n in range(8 + 2):
                if n < 8:
                    nk = P * (n % 2 + 1)
                    act.wait_ge(S["smax_ready"], n + 1)
                    if n >= 2:
                        act.wait_ge(S["pT_psum"], n - 1)
                    nc.scalar.activation(probs[n % 2][:, 0:nk], bank[3 + n % 2][:, 0:nk], ACT.Exp, bias=small[:, 192 + n:193 + n], scale=SM,
                                         accum_out=small[:, 200 + n:201 + n]).then_inc(S["sexp_ready"], 1)
                if n >= 1 and n - 1 < 8:
                    i = n - 1
                    act.wait_ge(S["pT_psum"], i + 1)
                    nk = i % 2 + 1
                    nc.scalar.activation(probsT[i % 2][:, 0:nk, :].rearrange("p a b -> p (a b)"), bank[5 + i % 2][:, 0:nk * P], ACT.Copy).then_inc(S["pT_ready"], 1)
                if n >= 2 and n % 2 == 1:
                    h = (n - 3) // 2
                    act.wait_ge(S["o_psum"], h + 1)
                    nc.scalar.activation(yT[:, 1, h, :], bank[7][:, 0:SEQ], ACT.Copy).then_inc(S["o_evac"], 1)
                if n in (1, 3):
                    i = n // 2
                    b = projected(("hi", i))
                    for half in range(2):
                        ins = nc.scalar.activation(hg_v[:, half, 256 * i:256 * i + 256], b[:, half * 256:half * 256 + 256], ACT.Copy)
                    ins.then_inc(S["proj_evac"], 1)
                if n in (5, 7):
                    i = n // 2 - 2
                    b = projected(("hg", i))
                    nc.scalar.activation(hg_g[:, 512 * i:512 * i + 512], b[:, :], ACT.Silu).then_inc(S["proj_evac"], 1)
            for i in range(2):
                act.wait_ge(S["hgT_psum"], i + 1)
                nc.scalar.activation(hg_kT[:, 4 * i:4 * i + 4, :].rearrange("p a b -> p (a b)"), bank[5 + i][:, :], ACT.Copy).then_inc(S["kT_ready"], 1)
            for h in range(HEADS):
                act.wait_ge(S["ho_psum"], h + 1)
                b = bank[(7, 2)[h % 2]]
                nc.scalar.activation(hg_sq[h % 2], b[:, 0:SEQ], ACT.Square).then_inc(S["ho_evac"], 1)
                nc.scalar.activation(hg_o[h % 2], b[:, 0:SEQ], ACT.Copy).then_inc(S["ho_evac"], 1)
                root(hg_rs[h % 2], 2 + h)
            assert proj_n[0] == len(PROJ)

            act.wait_ge(S["yA_ready"], HEADS)
            act.dma_start(x_res, A["x"][0].rearrange("(h p) n -> p h n", p=P)).then_inc(S["xres_in"], 16)
            act.dma_start(ln_w, A["ln1_w"].to_broadcast([P, D])).then_inc(S["ln_in"], 16)
            act.dma_start(ln_b, A["ln1_b"].to_broadcast([P, D])).then_inc(S["ln_in"], 16)
            act.dma_start(rb, A["router_b"].to_broadcast([P, NE])).then_inc(S["rb_in"], 16)
            act.dma_start(rw, A["router_w"].rearrange("(k p) n -> p k n", p=P)).then_inc(S["rw_in"], 16)
            act.wait_ge(S["b_clear"], 1)
            act.dma_start(b1_all[0:NE, :], A["moe_b1"]).then_inc(S["b_in"], 16)
            act.dma_start(b2_all[0:NE, :], A["moe_b2"]).then_inc(S["b_in"], 16)
            root(small[:, 314:315], 6)
            for r in range(4):
                half, kq = r // 2, r % 2
                if r == 2:
                    root(small[:, 314:315], 7)
                act.wait_ge(S["hT_psum"], r + 1)
                nc.scalar.activation(hT[:, 4 * kq:4 * kq + 4, half * P:half * P + P], bank[HT_BANK[half][kq]][:, :].rearrange("p (a b) -> p a b", a=4), ACT.Copy)\
                    .then_inc(S["hT_act"], 1)
            act.wait_ge(S["topexp_req"], 1)
            for half in range(2):
                nc.scalar.activation(small[:, 216 + 4 * half:220 + 4 * half], top[:, half, 0:TOPK], ACT.Exp, bias=small[:, 232 + half:233 + half],
                                     accum_out=small[:, 236 + half:237 + half]).then_inc(S["topexp_ready"], 1)
            act.wait_ge(S["wT_psum"], 1)
            nc.scalar.activation(wTd[0:NE].rearrange("p a b -> p (a b)"), bank[6][0:NE, 0:2 * P], ACT.Copy).then_inc(S["wT_ready"], 1)

            def gathered(g):
                act.wait_ge(S["xg_psum"], g + 1)
                nc.scalar.activation(xg.rearrange("p a b -> p (a b)"), bank[5][:, :], ACT.Copy).then_inc(S["xg_ready"], 1)

            def expert(n, u, gather_next=None):
                act.wait_ge(S["gmin_ready"], n + 1)
                nc.scalar.activation(g3, g1, ACT.Sigmoid, scale=SWA).then_inc(S["sig_ready"], 1)
                act.wait_ge(S["at_psum"], n + 1)
                nc.scalar.activation(actT.rearrange("p a b -> p (a b)"), bank[6][:, :], ACT.Copy).then_inc(S["at_ready"], 1)
                if gather_next is not None:
                    gathered(gather_next)
                act.wait_ge(S["expert_chunk_used"], n * R2S + R2S)
                nc.scalar.activation(y_pair[64 * u:64 * u + 64, 0:512], bank[4][0:64, :], ACT.Copy).then_inc(S["ypair_act"], 1)

            def weights(m_):
                act.wait_ge(S["wselT_psum"], m_ + 1)
                nc.scalar.activation(wselT.rearrange("p a b -> p (a b)"), bank[7][:, 0:256], ACT.Copy).then_inc(S["wselT_ready"], 1)

            gathered(0)
            with act.Fori(0, NPAIR) as p:
                expert(p * 2, 0, p * 2 + 1)
                weights(p)
                expert(p * 2 + 1, 1, p * 2 + 2)
            act.wait_ge(S["items_ready"], 1)
            n_items = act.value_load(item_e[0:1, NITEM:NITEM + 1], min_val=0, max_val=NITEM)
            with act.If(n_items > 0):
                with act.Fori(0, n_items) as j:
                    gathered(j + NE + 1)
                    weights(j + NPAIR)
                    expert(j + NE, 0)
            for half in range(2):
                root(small[:, 314:315], 8 + half)

        @block.tensor
        def _(pe):
            mm = nc.tensor.matmul
            st = [0]
            pj = [0]

            def chunk(c):
                i = st[0]
                assert STREAM[i] == c, (STREAM[i], c)
                st[0] += 1
                pe.wait_ge(landed[i % R1], need[c])
                shape, _ = chunk_source(c)
                return slot(i % R1, *shape)

            open_slot = [None]

            def proj(c, parts=(0, 1)):
                if parts[0] == 0:
                    open_slot[0] = chunk(c)
                    pj[0] += 1
                w = open_slot[0]
                i = pj[0] - 1
                if i >= 2 and parts[0] == 0:
                    pe.wait_ge(S["proj_evac"], i - 1)
                b = bank[i % 2]
                for j in parts:
                    if c[0] == "hi":
                        for k in range(KD):
                            last = mm(b[:, j * CW:j * CW + CW], xT[:, k, j * P:j * P + P], w[:, k, :], start=k == 0, stop=k == KD - 1)
                    elif c[0] == "ckv" and j == 0:
                        for k in range(KD):
                            last = mm(b[:, 0:SEQ], w[:, k, 0:P], xT[:, k, :], start=k == 0, stop=k == KD - 1)
                    elif c[0] == "ckv":
                        pe.wait_ge(S["bu_free"], 8)
                        for half in range(2):
                            for k in range(KD):
                                for h in range(HEADS):
                                    last = mm(bank[3 + half][32 * h:32 * h + 32, SEQ:], w[:, k, P + R2 * half:P + R2 * half + R2], xT[:, k, :],
                                              start=k == 0, stop=k == KD - 1)
                    else:
                        for k in range(KD):
                            last = mm(b[:, j * SEQ:(j + 1) * SEQ], w[:, k, j * P:j * P + P], xT[:, k, :], start=k == 0, stop=k == KD - 1)
                if parts[-1] == 1:
                    last.then_inc(S["chunk_used"], 1)

            def merge(br, j, u):
                if j % 2 == 0:
                    open_slot[0] = chunk(("wb", br, j // 2))
                w = open_slot[0]
                if u >= 2:
                    pe.wait_ge(S["merge_used"], u - 1)
                for i in range(2):
                    for k in range(4):
                        c = 2 * (j % 2) + i
                        last = mm(bank[3 + u % 2][:, i * SEQ:(i + 1) * SEQ], w[:, k, c * P:(c + 1) * P], yT[:, br, k, :], start=k == 0, stop=k == 3)
                last.then_inc(S["merge_psum"] if j % 2 == 0 else S["chunk_used"], 1)

            pe.wait_ge(S["const_ready"], NCONST)
            pe.wait_ge(S["x_in"], 16)
            for r in range(4):
                for kk in range(2):
                    for half in range(2):
                        k = 2 * r + kk
                        last = nc.tensor.transpose(bank[3 + r][:, kk * SEQ + half * P:kk * SEQ + half * P + P], x_tok[:, half, k * P:k * P + P], ident[:, :])
                last.then_inc(S["xT_psum"], 1)
            pe.wait_ge(S["xT_vec"], 4)
            proj(("lx", 0))
            pe.wait_ge(S["vec_in"], 16 * 14)
            nc.tensor.transpose(bank[7][:, 0:NVEC], rows[0:NVEC, :], ident[0:NVEC, 0:NVEC])
            pe.wait_ge(S["dt_rows"], 1)
            nc.tensor.transpose(bank[7][:, P:P + S5T], small[0:S5T, 64:192], ident[0:S5T, 0:S5T]).then_inc(S["vec_psum"], 1)
            proj(("lx", 1))
            proj(("su", 0))
            proj(("su", 1))
            pe.wait_ge(S["lru_in"], 16 * 4)
            for i in range(4):
                pe.wait_ge(S["xc_ready"], i + 1)
                mm(bank[3 + i][:, 0:SEQ], wa[:, i, :], xc[:, i, :], start=True, stop=True)
                mm(bank[3 + i][:, SEQ:], wx[:, i, :], xc[:, i, :], start=True, stop=True).then_inc(S["gate_psum"], 1)
            proj(("lg", 0))
            proj(("lg", 1))
            proj(("cq", 0))
            pe.wait_ge(S["exp_ready"], 1)
            pe.wait_ge(S["gate_act"], 8)
            for i in range(4):
                for q in range(4):
                    src = b_exp[:, i, 4 * q:4 * q + 4, :].rearrange("p a b -> p (a b)") if i < 2 else c_exp[:, i - 2, q, :]
                    last = nc.tensor.transpose(bank[3 + i][:, q * P:q * P + P], src, ident[:, :])
                last.then_inc(S["prep_psum"], 1)
            pe.wait_ge(S["prep_evac"], 4)
            pe.wait_ge(S["proj_evac"], 4)

            def drive(h):
                if h >= 2:
                    pe.wait_ge(S["bu_free"], h - 1)
                for i in range(2):
                    for j in (2 * h, 2 * h + 1):
                        q, r = j // 4, 32 * (j % 4)
                        last = mm(bank[3 + 2 * (h % 2) + j % 2][:, i * SEQ:(i + 1) * SEQ], bT[r:r + 32, i, q, :], su[r:r + 32, q, :],
                                  start=True, stop=True, tile_position=(r, 0))
                last.then_inc(S["bu_psum"], 1)

            def read_out(h):
                pe.wait_ge(S["x_ready"], h + 1)
                q = h // 2
                if h % 2 == 0 and q >= 1:
                    pe.wait_ge(S["y_evac"], q)
                for i, xs in ((0, xr), (1, xi)):
                    for j in (2 * h, 2 * h + 1):
                        r = 32 * (j % 4)
                        last = mm(bank[7][r:r + 32, 0:SEQ], cT[:, i, q, r:r + 32], xs[h % 2][:, j % 2, :], start=i == 0, stop=i == 1)
                last.then_inc(S["x_used"], 1)

            drive(0)
            for h in range(8):
                proj(("gl", 2 * h))
                if h < 7:
                    drive(h + 1)
                proj(("gl", 2 * h + 1))
                if h:
                    read_out(h - 1)
            proj(("ckv", 0))
            read_out(7)
            proj(("hf", 0))
            pe.wait_ge(S["sq_ready"], 1)
            mm(bank[7][:, 0:SEQ], ones_256[:, :], sq[:, 0, :], start=True, stop=False)
            mm(bank[7][:, 0:SEQ], ones_256[:, :], sq[:, 1, :], start=False, stop=True)
            mm(bank[7][:, SEQ:], ones_128[:, :], sq[:, 2, :], start=True, stop=True).then_inc(S["ss_psum"], 1)
            w = chunk(("wglu", 0))
            pe.wait_ge(S["gelu_ready"], 1)
            for j in range(4):
                for k in range(4):
                    last = mm(bank[5 + j // 2][:, (j % 2) * SEQ:(j % 2 + 1) * SEQ], w[:, k, j * P:j * P + P], s_out[:, k, :], start=k == 0, stop=k == 3)
                if j == 1:
                    last.then_inc(S["glu_psum"], 1)
            last.then_inc(S["chunk_used"], 1)
            wq = chunk(("wq", 0))
            pe.wait_ge(S["norm_ready"], 1)
            pe.wait_ge(S["glu_gate"], 4)
            for h in range(HEADS):
                for k in range(2):
                    last = mm(bank[6 + h // 2][:, (h % 2) * SEQ:(h % 2 + 1) * SEQ], wq[:, k, h * QK:h * QK + NOPE], cq[:, k, :], start=k == 0, stop=k == 1)
                if h % 2:
                    last.then_inc(S["mla_psum"], 1)
            for half in range(2):
                for h in range(HEADS):
                    for k in range(2):
                        lo = h * QK + NOPE + R2 * half
                        last = mm(bank[3 + half][32 * h:32 * h + 32, 0:SEQ], wq[:, k, lo:lo + R2], cq[:, k, :], start=k == 0, stop=k == 1)
            last.then_inc(S["chunk_used"], 1)
            wkv = chunk(("wkv", 0))
            for h in range(HEADS):
                if h == 2:
                    pe.wait_ge(S["mla_evac"], 1)
                last = mm(bank[5 + h // 2][:, (h % 2) * SEQ:(h % 2 + 1) * SEQ], wkv[:, 0, h * 256:h * 256 + NOPE], ckv, start=True, stop=True)
                if h % 2:
                    last.then_inc(S["mla_psum"], 1)
            wv = wkv[:, 0, :].rearrange("p (h c) -> p h c", h=HEADS)[:, :, NOPE:]
            for half in range(2):
                pe.wait_ge(S["mla_evac"], 2 + half)
                mm(bank[7 - 2 * half][:, :].rearrange("p (a b) -> p a b", a=HEADS), ckv[:, half * P:half * P + P], wv, start=True, stop=True)\
                    .then_inc(S["chunk_used"] if half else S["mla_psum"], 1)
            for c in (("hf", 1), ("hq", 0), ("hq", 1)):
                proj(c)
            pe.wait_ge(S["mla_evac"], 6)
            pe.wait_ge(S["mla_masked"], 1)

            def block_scores(t):
                pe.wait_ge(S["p_ready"], t + 1)
                for n in range(8):
                    last = mm(bank[2][:, n * BLK + t:n * BLK + t + 1], prod[t % 2][:, 8 * n:8 * n + 8, :].rearrange("p a b -> p (a b)"), ones[:, 0:1], start=True, stop=True)
                last.then_inc(S["p_used"], 1)

            filler = [(("hi", 0), 0), (("hi", 0), 1), (("hi", 1), 0), (("hi", 1), 1), (("hg", 0), 0), (("hg", 0), 1), (("hg", 1), 0), (("hg", 1), 1)]
            for n in range(8 + 2):
                if n < 8:
                    h, qt = n // 2, n % 2
                    nk = P * (qt + 1)
                    if n >= 2:
                        pe.wait_ge(S["sexp_ready"], n - 1)
                    b = bank[3 + n % 2]
                    mm(b[:, 0:nk], qn[:, h, qt * P:qt * P + P], kn[:, h, 0:nk], start=True, stop=False)
                    mm(b[:, 0:nk], qm1[:, h, qt * P:qt * P + P], rp1[:, 1, 0:nk], start=False, stop=False)
                    mm(b[:, 0:nk], qm2[:, h, qt * P:qt * P + P], rp2[:, 1, 0:nk], start=False, stop=True).then_inc(S["s_psum"], 1)
                if 1 <= n <= 8:
                    i = n - 1
                    pe.wait_ge(S["p_norm"], i + 1)
                    if i >= 2:
                        pe.wait_ge(S["pT_ready"], i - 1)
                    for kt in range(i % 2 + 1):
                        last = nc.tensor.transpose(bank[5 + i % 2][:, kt * P:kt * P + P], probs[i % 2][:, kt * P:kt * P + P], ident[:, :])
                    last.then_inc(S["pT_psum"], 1)
                if n >= 2:
                    i = n - 2
                    h, qt = i // 2, i % 2
                    pe.wait_ge(S["pT_ready"], i + 1)
                    if qt == 0 and h >= 1:
                        pe.wait_ge(S["o_evac"], h)
                    for kt in range(qt + 1):
                        last = mm(bank[7][:, qt * P:qt * P + P], vv[:, kt, h * VD:h * VD + VD], probsT[i % 2][:, kt, :], start=kt == 0, stop=kt == qt)
                    if qt:
                        last.then_inc(S["o_psum"], 1)
                if n < len(filler):
                    c, part = filler[n]
                    proj(c, (part,))
                if n >= 1:
                    block_scores(n - 1)
            pe.wait_ge(S["yD_ready"], 1)
            pe.wait_ge(S["yC_ready"], 1)
            for u in range(8):
                merge(3 - u // 4, u % 4, u)
                if 9 + u < BLK:
                    block_scores(9 + u)
            pe.wait_ge(S["g_ready"], 1)
            for n in range(8):
                last = nc.tensor.transpose(bank[5 + n // 4][:, (n % 4) * P:(n % 4 + 1) * P], grow[:, 8 * n:8 * n + 8, :].rearrange("p a b -> p (a b)"), ident[:, :])
                if n % 4 == 3:
                    last.then_inc(S["hgT_psum"], 1)
            pe.wait_ge(S["o_evac"], 4)
            merge(1, 0, 8)
            merge(1, 1, 9)
            pe.wait_ge(S["kT_ready"], 2)
            pe.wait_ge(S["bd_ready"], 1)
            pe.wait_ge(S["proj_evac"], len(PROJ))

            def updates(h):
                for half in range(2):
                    n = 2 * h + half
                    pe.wait_ge(S["vx_ready"], n + 1)
                    for i in range(2):
                        u = 2 * n + i
                        if u >= 4:
                            pe.wait_ge(S["u_used"], u - 3)
                        mm(bank[U_BANK[u % 4]][:, :], hg_kT[:, n, :], v_exp[n % 4][:, 4 * i:4 * i + 4, :].rearrange("p a b -> p (a b)"), start=True, stop=True)\
                            .then_inc(S["u_psum"], 1)

            def outputs(h):
                b = bank[(7, 2)[h % 2]]
                pe.wait_ge(S["st_ready"], h + 1)
                if h >= 2:
                    pe.wait_ge(S["yA_ready"], h - 1)
                for half in range(2):
                    lo = half * P
                    mm(b[:, lo:lo + P], hg_v[:, half, h * P:h * P + P], hg_bd[:, 2 * h + half, :], start=True, stop=False)
                    for t in range(8 * half, 8 * half + 8):
                        if t:
                            last = mm(b[:, t * BLK:t * BLK + BLK], state[h % 2][:, t - 1, :], q_inter[:, h * SEQ + t * BLK:h * SEQ + t * BLK + BLK],
                                      start=False, stop=t % 8 == 7)
                last.then_inc(S["ho_psum"], 1)

            def squares(h):
                pe.wait_ge(S["ho_evac"], 2 * h + 2)
                mm(bank[(7, 2)[h % 2]][:, SEQ:], ones_128[:, :], hg_sq[h % 2], start=True, stop=True).then_inc(S["hss_psum"], 1)

            updates(0)
            updates(1)
            for h in range(HEADS):
                outputs(h)
                if h + 2 < HEADS:
                    updates(h + 2)
                elif h == 2:
                    merge(1, 2, 10)
                squares(h)
            merge(1, 3, 11)
            pe.wait_ge(S["yA_ready"], HEADS)
            for j in range(4):
                merge(0, j, 12 + j)
            wo = [chunk(("wo", i)) for i in range(4)]
            for half in range(2):
                for k in range(KD):
                    if half == 0 and k % 2 == 0:
                        pe.wait_ge(S["acc_ready"], k // 2 + 1)
                    for dh in range(2):
                        last = mm(bank[MIX_BANK[half][dh]][:, :], acc[:, k, half * P:half * P + P], wo[k // 2][:, k % 2, 512 * dh:512 * dh + 512],
                                  start=k == 0, stop=k == KD - 1)
                    if half and k % 2:
                        last.then_inc(S["chunk_used"], 1)
                if half == 0:
                    last.then_inc(S["mix_psum"], 1)
            def bias(g, u):
                pe.wait_ge(S["esel_ready"], g + 1)
                for i in range(2):
                    for ct in range(2):
                        mm(bank[2 * u + i][64 * ct:64 * ct + 64, :], esel, b1_all[:, i * FF + ct * 512:i * FF + ct * 512 + 512], start=True, stop=False)

            pe.wait_ge(S["rw_in"], 16)
            for half in range(2):
                if half:
                    pe.wait_ge(S["b_in"], 32)
                    bias(0, 0)
                pe.wait_ge(S["h_ready"], half + 1)
                for k in range(KD):
                    last = nc.tensor.transpose(bank[HT_BANK[half][k // 4]][:, (k % 4) * P:(k % 4 + 1) * P], h_tok[:, half, k * P:k * P + P], ident[:, :])
                    if k % 4 == 3:
                        last.then_inc(S["hT_psum"], 1)
                for k in range(KD):
                    if k % 4 == 0:
                        pe.wait_ge(S["hT_act"], 2 * half + 1 + k // 4)
                    last = mm(bank[4][:, half * NE:half * NE + NE], hT[:, k, half * P:half * P + P], rw[:, k, :], start=k == 0, stop=k == KD - 1)
            last.then_inc(S["logit_psum"], 1)

            def gather(g):
                pe.wait_ge(S["sel_ready"], g + 1)
                for k in range(KD):
                    for half in range(2):
                        last = mm(bank[5][:, k * CAP:k * CAP + CAP], h_tok[:, half, k * P:k * P + P], sel[:, half, :], start=half == 0, stop=half == 1)
                last.then_inc(S["xg_psum"], 1)

            pe.wait_ge(S["member_ready"], 1)
            mm(bank[4][:, 0:NE], earlier[:, :], member[:, 0, :], start=True, stop=True)
            mm(bank[4][:, NE:2 * NE], earlier[:, :], member[:, 1, :], start=True, stop=False)
            mm(bank[4][:, NE:2 * NE], ones[:, :], member[:, 0, :], start=False, stop=True)
            mm(bank[4][:, 2 * NE:3 * NE], ones[:, :], member[:, 0, :], start=True, stop=False)
            mm(bank[4][:, 2 * NE:3 * NE], ones[:, :], member[:, 1, :], start=False, stop=True).then_inc(S["rank_psum"], 1)
            pe.wait_ge(S["route_ready"], 1)
            for half in range(2):
                last = nc.tensor.transpose(bank[6][0:NE, half * P:half * P + P], wfull[:, half, 0:NE], ident[:, :])
            last.then_inc(S["wT_psum"], 1)

            def expert(n, u, g, gather_next=None, item=None):
                odd = 0 if item is not None else u
                pe.wait_ge(S["xg_ready"], g + 1)
                for c in range(8):
                    if item is not None and c < ALT:
                        pe.wait_ge(landed[c], item * 16 + (NPAIR + 1) * 16 + 16 * uses[c])
                    else:
                        pe.wait_ge(landed_of(c, odd), landed_count(c, n, odd))
                    w = expert_slot(c, odd)
                    for i in range(2):
                        for ct in range(2):
                            last = mm(bank[2 * u + i][64 * ct:64 * ct + 64, :], xg[:, c, :], w[:, i * FF + ct * 512:i * FF + ct * 512 + 512], start=False, stop=c == 7)
                    last.then_inc(S["expert_chunk_used"], 1)
                if gather_next is not None:
                    pe.wait_ge(S["b2_used"], 1)
                    bias(gather_next, 1 - u)
                    gather(gather_next)
                pe.wait_ge(S["act_ready"], n + 1)
                for j in range(4):
                    last = nc.tensor.transpose(bank[6][:, j * P:j * P + P], g1[:, j * P:j * P + P], ident[:, :])
                last.then_inc(S["at_psum"], 1)
                pe.wait_ge(S["at_ready"], n + 1)
                for c in range(8, 12):
                    pe.wait_ge(landed[c], landed_count(c, n, odd))
                    w = expert_slot(c)
                    for kk in range(2):
                        r = 2 * (c - 8) + kk
                        fh, j = r // 4, r % 4
                        for dh in range(2):
                            last = mm(bank[4][64 * dh:64 * dh + 64, :], actT[:, j, 64 * fh:64 * fh + 64], w[:, kk, 512 * dh:512 * dh + 512], start=r == 0, stop=r == 7)
                    last.then_inc(S["expert_chunk_used"], 1)

            def weights(rows_):
                for half in range(2):
                    last = nc.tensor.transpose(bank[7][0:rows_, half * P:half * P + P], wsel[:, half, 0:rows_], ident[:, :])
                last.then_inc(S["wselT_psum"], 1)

            def combine(m_, n, rows_):
                pe.wait_ge(S["wselT_ready"], m_ + 1)
                pe.wait_ge(S["ypair_act"], n)
                pe.wait_ge(S["ypair_vec"], n)
                for i in range(4):
                    half, dh = i // 2, i % 2
                    if i >= 2:
                        pe.wait_ge(S["comb_used"], m_ * 4 + i - 1)
                    mm(bank[6 + i % 2][:, :], wselT[0:rows_, half, :], y_pair[0:rows_, 512 * dh:512 * dh + 512], start=True, stop=True).then_inc(S["comb_psum"], 1)
                pe.wait_ge(S["comb_used"], m_ * 4 + 4)

            gather(0)
            pe.wait_ge(S["wT_ready"], 1)
            for half in range(2):
                for dh in range(2):
                    last = mm(bank[(2, 3, 6, 7)[2 * half + dh]][:, :], wTd[:, half, :], b2_all[:, 512 * dh:512 * dh + 512], start=True, stop=True)
            last.then_inc(S["b2_psum"], 1)
            with pe.Fori(0, NPAIR) as p:
                expert(p * 2, 0, p * 2, p * 2 + 1)
                weights(P)
                expert(p * 2 + 1, 1, p * 2 + 1, p * 2 + 2)
                combine(p, p * 2 + 2, P)
            pe.wait_ge(S["items_ready"], 1)
            n_items = pe.value_load(item_e[0:1, NITEM:NITEM + 1], min_val=0, max_val=NITEM)
            with pe.If(n_items > 0):
                with pe.Fori(0, n_items) as j:
                    bias(j + NE + 1, 1)
                    gather(j + NE + 1)
                    weights(CAP)
                    expert(j + NE, 1, j + NE + 1, item=j)
                    combine(j + NPAIR, j + NE + 1, CAP)

        @block.vector
        def _(dve):
            V = nc.vector
            vc = [0]
            base = [0]
            tail = [False]
            fc = [0]

            def link(ins):
                if tail[0]:
                    fc[0] += 1
                    ins.then_inc(S["f_chain"], 1)
                    dve.wait_ge(S["f_chain"], fc[0])
                    return
                vc[0] += 1
                ins.then_inc(S["v_chain"], 1)
                dve.wait_ge(S["v_chain"], base[0] + vc[0])

            def inverse_root(dst, src, eps, nth):
                link(V.tensor_scalar(dst, src, eps, None, ALU.add))
                V.reciprocal(dst, dst).then_inc(S["rs_req"], 1)
                dve.wait_ge(S["rs_ready"], nth)

            def sm(lo, n=16):
                return small[:, lo:lo + n]

            dve.wait_ge(S["iota_ready"], 1)
            V.tensor_copy(iota[:, :], iota_i[:, :]).then_inc(S["iota_read"], 1)
            dve.wait_ge(S["iota_read"], 1)
            dve.wait_ge(S["const_ready"], NCONST)
            link(V.memset(lx[:, :, 0:3], 0.0))
            link(V.memset(b_exp, 0.0))
            for r in range(4):
                dve.wait_ge(S["xT_psum"], r + 1)
                V.tensor_copy(xT[:, 2 * r:2 * r + 2, :].rearrange("p a b -> p (a b)"), bank[3 + r][:, :]).then_inc(S["xT_vec"], 1)
            dve.wait_ge(S["dt_in"], 16)
            V.tensor_copy(small[0:S5T, 64:192].rearrange("p (a b) -> p a b", a=2), small[0:S5T, 0:2].unsqueeze(2).to_broadcast([S5T, 2, 64])).then_inc(S["dt_rows"], 1)
            dve.wait_ge(S["vec_psum"], 1)
            link(V.tensor_copy(sm(16), bank[7][:, P:P + S5T]))
            V.tensor_copy(vec[:, :], bank[7][:, 0:NVEC]).then_inc(S["vec_ready"], 1)
            dve.wait_ge(S["vec_ready"], 1)
            V.tensor_copy(small[:, 500:501], small[:, 16:17]).then_inc(S["dt_exp"], 1)
            V.scalar_tensor_tensor(sm(360, 4), v_("apar", 0, 4), -1.0, v_("apar", 0, 4), ALU.mult, ALU.max).then_inc(S["absa_ready"], 1)
            V.tensor_tensor(sm(400, 4), v_("lb", 0, 4), v_("lb", 0, 4), ALU.subtract).then_inc(S["lbe_req"], 1)
            dve.wait_ge(S["s5_small"], 1)
            link(V.tensor_tensor(sm(48), v_("a_re", 0, 16), sm(32), ALU.mult))
            link(V.tensor_tensor(sm(64), v_("a_im", 0, 16), sm(32), ALU.mult))
            V.tensor_copy(small[:, 501:502], small[:, 48:49]).then_inc(S["s5_mag"], 1)
            link(V.tensor_scalar(sm(96), sm(64), INV2PI, MAGIC, ALU.mult, ALU.add))
            link(V.tensor_scalar(sm(96), sm(96), MAGIC, None, ALU.subtract))
            for c in (C1, C2, C3):
                link(V.scalar_tensor_tensor(sm(64), sm(96), -c, sm(64), ALU.mult, ALU.add))
            link(V.tensor_scalar(sm(176), sm(64), INV2PI, None, ALU.mult))
            link(V.tensor_scalar(sm(144), sm(64), PI_LOW, -PI_LOW, ALU.min, ALU.max))
            link(V.scalar_tensor_tensor(sm(160), sm(144), -1.0, sm(144), ALU.mult, ALU.min))
            V.tensor_scalar(sm(160), sm(160), float(np.pi / 2), None, ALU.add).then_inc(S["s5_theta"], 1)
            dve.wait_ge(S["expa_ready"], 1)
            z, s_, s2, po = sm(364, 4), sm(368, 4), sm(372, 4), sm(388, 4)
            link(V.tensor_scalar(s_, z, 2.0, None, ALU.add))
            link(V.reciprocal(s_, s_))
            link(V.tensor_tensor(s_, s_, z, ALU.mult))
            link(V.tensor_tensor(s2, s_, s_, ALU.mult))
            link(V.tensor_scalar(po, s2, 1.0 / 17, 1.0 / 15, ALU.mult, ALU.add))
            for d_ in (13, 11, 9, 7, 5, 3, 1):
                link(V.tensor_tensor(po, po, s2, ALU.mult))
                link(V.tensor_scalar(po, po, 1.0 / d_, None, ALU.add))
            link(V.tensor_tensor(po, po, s_, ALU.mult))
            link(V.tensor_scalar(s_, v_("apar", 0, 4), 0.0, None, ALU.max))
            link(V.scalar_tensor_tensor(po, po, 2.0, s_, ALU.mult, ALU.add))
            link(V.tensor_scalar(sm(376, 4), po, -8.0, None, ALU.mult))
            link(V.tensor_scalar(sm(380, 4), po, 8.0, None, ALU.mult))
            V.tensor_scalar(sm(384, 4), po, -16.0, None, ALU.mult).then_inc(S["sp_ready"], 1)
            dve.wait_ge(S["lbe_ready"], 1)
            link(V.reciprocal(sm(408, 4), sm(404, 4)))
            link(V.tensor_tensor(sm(408, 4), sm(408, 4), sm(404, 4), ALU.mult))
            link(V.tensor_tensor(sm(412, 4), sm(408, 4), sm(408, 4), ALU.subtract))
            link(V.tensor_scalar(sm(416, 4), sm(412, 4), -1.0, 1.0, ALU.mult, ALU.add))
            dve.wait_ge(S["proj_evac"], 2)
            for i in range(4):
                link(V.tensor_scalar(xc[:, i, :], lx[:, i, 3:3 + SEQ], v_("convw", 12 + i), v_("convb", i), ALU.mult, ALU.add))
                for tap in range(3):
                    ins = V.scalar_tensor_tensor(xc[:, i, :], lx[:, i, tap:tap + SEQ], v_("convw", 4 * tap + i), xc[:, i, :], ALU.mult, ALU.add)
                    if tap < 2:
                        link(ins)
                ins.then_inc(S["xc_ready"], 1)
            dve.wait_ge(S["s5_trig0"], 1)
            dve.wait_ge(S["s5_small"], 2)
            sn, cs, mag = sm(112), sm(128), sm(80)
            re, im = v_("a_re", 0, 16), v_("a_im", 0, 16)
            nr, li, den, tq = sm(208), sm(224), sm(240), sm(256)
            cr, ci = sm(272), sm(288)
            link(V.tensor_tensor(nr, mag, cs, ALU.mult))
            link(V.tensor_scalar(nr, nr, -1.0, None, ALU.add))
            link(V.tensor_tensor(li, mag, sn, ALU.mult))
            link(V.tensor_tensor(den, re, re, ALU.mult))
            link(V.tensor_tensor(tq, im, im, ALU.mult))
            link(V.tensor_tensor(den, den, tq, ALU.add))
            link(V.reciprocal(den, den))
            link(V.tensor_tensor(cr, nr, re, ALU.mult))
            link(V.tensor_tensor(tq, li, im, ALU.mult))
            link(V.tensor_tensor(cr, cr, tq, ALU.add))
            link(V.tensor_tensor(cr, cr, den, ALU.mult))
            link(V.tensor_tensor(ci, li, re, ALU.mult))
            link(V.tensor_tensor(tq, nr, im, ALU.mult))
            link(V.tensor_tensor(ci, ci, tq, ALU.subtract))
            link(V.tensor_tensor(ci, ci, den, ALU.mult))
            dve.wait_ge(S["s5_in"], 64)
            b4 = [s_raw[:, i, :].rearrange("p (a b) -> p a b", a=16) for i in range(2)]
            u1 = t1.rearrange("p a b -> p (a b)")[:, 0:256].rearrange("p (a b) -> p a b", a=16)
            u2 = t2.rearrange("p a b -> p (a b)")[:, 0:256].rearrange("p (a b) -> p a b", a=16)

            def wide(v):
                return v.unsqueeze(2).to_broadcast([P, 16, 16])

            for i, (ca, cb, op) in enumerate(((cr, ci, ALU.subtract), (ci, cr, ALU.add))):
                link(V.tensor_tensor(u1, b4[0], wide(ca), ALU.mult))
                link(V.tensor_tensor(u2, b4[1], wide(cb), ALU.mult))
                for g2_ in range(2):
                    p0 = 64 * g2_
                    link(V.tensor_tensor(b_exp[p0:p0 + 64, i, :, 16 * g2_:16 * g2_ + 16], u1[p0:p0 + 64], u2[p0:p0 + 64], op))
            link(V.tensor_reduce(oddmask[:, 0:1], blockmask[:, :].rearrange("p (a b) -> p b a", b=2)[:, 0, :], X, ALU.add))
            link(V.tensor_reduce(oddmask[:, 1:2], blockmask[:, :].rearrange("p (a b) -> p b a", b=2)[:, 1, :], X, ALU.add))
            for i in range(2):
                craw = s_raw[:, 2 + i, :].rearrange("p (a b) -> p a b", a=4)
                for half in range(2):
                    ins = V.tensor_scalar(c_exp[:, i, :, 64 * half:64 * half + 64], craw, oddmask[:, half:half + 1], None, ALU.mult)
                    if (i, half) != (1, 1):
                        link(ins)
            ins.then_inc(S["exp_ready"], 1)

            def phases(q):
                s, c = sinT[q % 2], cosT[q % 2]
                for j in range(4):
                    ins = V.tensor_scalar(c[:, j, :], iota[:, :], small[:, 176 + 4 * q + j:177 + 4 * q + j], MAGIC, ALU.mult, ALU.add)
                link(ins)
                cf = c.rearrange("p a b -> p (a b)")
                sf = s.rearrange("p a b -> p (a b)")
                link(V.tensor_scalar(cf, cf, MAGIC, None, ALU.subtract))
                for j in range(4):
                    ins = V.scalar_tensor_tensor(s[:, j, :], iota[:, :], small[:, 176 + 4 * q + j:177 + 4 * q + j], c[:, j, :], ALU.mult, ALU.subtract)
                link(ins)
                V.scalar_tensor_tensor(cf, sf, -1.0, sf, ALU.mult, ALU.max).then_inc(S["f_ready"], 1)

            phases(0)
            phases(1)
            flat = "p a b -> p (a b)"
            dve.wait_ge(S["gate_act"], 8)
            link(V.tensor_tensor(lr_i.rearrange(flat), lr_i.rearrange(flat), xc.rearrange(flat), ALU.mult))
            dve.wait_ge(S["lru_exp"], 8)
            link(V.scalar_tensor_tensor(lr_t, lx[:, :, 0:SEQ], 1.0, lr_t, ALU.add, ALU.mult))
            V.tensor_scalar(lr_t.rearrange(flat), lr_t.rearrange(flat), 0.0, None, ALU.max).then_inc(S["lru_b2"], 1)
            dve.wait_ge(S["lru_sqrt"], 1)
            dve.wait_ge(S["lru_exp"], 12)
            link(V.tensor_tensor(lr_i.rearrange(flat), lr_i.rearrange(flat), lr_t.rearrange(flat), ALU.mult))
            for i in range(4):
                link(V.tensor_tensor_scan(xc[:, i, :], lr_r[:, i, :], lr_i[:, i, :], 0.0, ALU.mult, ALU.add))
            dve.wait_ge(S["proj_evac"], 6)
            V.tensor_tensor(yT[:, 3].rearrange(flat), xc.rearrange(flat), lr_g.rearrange(flat), ALU.mult).then_inc(S["yD_ready"], 1)

            def y_out(q):
                dve.wait_ge(S["x_used"], 2 * q + 2)
                V.scalar_tensor_tensor(s_out[:, q, :], su[:, q, :], v_("dskip", q), bank[7][:, 0:SEQ], ALU.mult, ALU.add).then_inc(S["y_evac"], 1)

            for h in range(8):
                q = h // 2
                dve.wait_ge(S["bu_psum"], h + 1)
                dve.wait_ge(S["trig_ready"], 2 * q + 2)
                lo = 2 * (h % 2)
                s, c = sinT[q % 2][:, lo:lo + 2, :], cosT[q % 2][:, lo:lo + 2, :]
                bu = banks[:, 3 + 2 * (h % 2):5 + 2 * (h % 2), :]
                br, bi = bu[:, :, 0:SEQ], bu[:, :, SEQ:]
                a, b, zrf, zif = t1, t2, zr, zi
                link(V.tensor_tensor(a, br, c, ALU.mult))
                link(V.tensor_tensor(b, bi, s, ALU.mult))
                link(V.tensor_tensor(a, a, b, ALU.add))
                for j in range(2):
                    ti = 2 * h + j
                    link(V.tensor_tensor_scan(zr[:, j, :], small[:, 80 + ti:81 + ti].to_broadcast([P, SEQ]), t1[:, j, :], 0.0, ALU.mult, ALU.add))
                link(V.tensor_tensor(a, bi, c, ALU.mult))
                link(V.tensor_tensor(b, br, s, ALU.mult))
                V.tensor_tensor(a, a, b, ALU.subtract).then_inc(S["bu_free"], 1)
                dve.wait_ge(S["bu_free"], h + 1)
                for j in range(2):
                    ti = 2 * h + j
                    link(V.tensor_tensor_scan(zi[:, j, :], small[:, 80 + ti:81 + ti].to_broadcast([P, SEQ]), t1[:, j, :], 0.0, ALU.mult, ALU.add))
                if h % 2 == 1 and h >= 3:
                    y_out(q - 1)
                if h >= 2:
                    dve.wait_ge(S["x_used"], h - 1)
                xrf, xif = xr[h % 2], xi[h % 2]
                link(V.tensor_tensor(a, zrf, c, ALU.mult))
                link(V.tensor_tensor(b, zif, s, ALU.mult))
                link(V.tensor_tensor(xrf, a, b, ALU.subtract))
                link(V.tensor_tensor(a, zif, c, ALU.mult))
                link(V.tensor_tensor(b, zrf, s, ALU.mult))
                V.tensor_tensor(xif, a, b, ALU.add).then_inc(S["x_ready"], 1)
                dve.wait_ge(S["x_ready"], h + 1)
                if h in (1, 3):
                    phases(q + 2)
            y_out(3)
            link(V.tensor_copy(cq.rearrange(flat), cq_s.rearrange(flat)))
            link(V.tensor_tensor(sq[:, 0:2, :].rearrange(flat), cq.rearrange(flat), cq.rearrange(flat), ALU.mult))
            dve.wait_ge(S["proj_evac"], PROJ.index(("ckv", 0)) + 1)
            V.tensor_tensor(sq[:, 2, :], ckv, ckv, ALU.mult).then_inc(S["sq_ready"], 1)
            dve.wait_ge(S["pos_in"], 32)
            link(V.tensor_copy(ang, pos_i[:, :]))
            link(V.tensor_scalar(ang, ang, inv_freq[:, 0:1], None, ALU.mult))
            link(V.tensor_scalar(ang2, ang, INV2PI, MAGIC, ALU.mult, ALU.add))
            link(V.tensor_scalar(ang2, ang2, MAGIC, None, ALU.subtract))
            for c in (C1, C2, C3):
                link(V.scalar_tensor_tensor(ang, ang2, -c, ang, ALU.mult, ALU.add))
            link(V.tensor_scalar(ang, ang, PI_LOW, -PI_LOW, ALU.min, ALU.max))
            link(V.scalar_tensor_tensor(ang2, ang, -1.0, ang, ALU.mult, ALU.min))
            V.tensor_scalar(ang2, ang2, float(np.pi / 2), None, ALU.add).then_inc(S["cos_req"], 1)
            dve.wait_ge(S["ss_psum"], 1)
            inverse_root(rst.rearrange(flat), bank[7][:, :], RMS_EPS, 1)
            for i in range(2):
                link(V.scalar_tensor_tensor(cq[:, i, :], cq[:, i, :], v_("qnorm", i), rst[:, 0, :], ALU.mult, ALU.mult))
            V.scalar_tensor_tensor(ckv, ckv, v_("kvnorm", 0), rst[:, 1, :], ALU.mult, ALU.mult).then_inc(S["norm_ready"], 1)

            def decays(i):
                dve.wait_ge(S["proj_evac"], PROJ.index(("hf", i)) + 1)
                for h in (2 * i, 2 * i + 1):
                    f, k = hg_f[:, h * SEQ:(h + 1) * SEQ], hg_k[:, h * SEQ:(h + 1) * SEQ]
                    V.tensor_scalar(k, k, small[:, 416 + h:417 + h], None, ALU.mult)
                    link(V.tensor_scalar(f, f, small[:, 416 + h:417 + h], small[:, 412 + h:413 + h], ALU.mult, ALU.add))
                f = hg_f[:, 512 * i:512 * i + 512]
                link(V.tensor_scalar(f, f, F_MIN, None, ALU.max))

            decays(0)
            dve.wait_ge(S["glu_gate"], 4)
            V.tensor_tensor(yT[:, 2].rearrange(flat), yT[:, 2].rearrange(flat), s_out.rearrange(flat), ALU.mult).then_inc(S["yC_ready"], 1)
            dve.wait_ge(S["chunk_used"], STREAM.index(("wq", 0)) + 1)
            dve.wait_ge(S["cos_ready"], 2)
            x1, x2 = (bank[3 + i][:, :].rearrange("p (a b) -> p a b", a=2) for i in range(2))
            cb = cos_p.unsqueeze(1).to_broadcast([P, 2, SEQ])
            sb_ = sin_p.unsqueeze(1).to_broadcast([P, 2, SEQ])
            link(V.tensor_tensor(tA, x1, cb, ALU.mult))
            link(V.tensor_tensor(tB, x2, sb_, ALU.mult))
            link(V.tensor_tensor(rp1, tA, tB, ALU.subtract))
            link(V.tensor_tensor(tA, x2, cb, ALU.mult))
            link(V.tensor_tensor(tB, x1, sb_, ALU.mult))
            link(V.tensor_tensor(rp2, tA, tB, ALU.add))
            for qm, rp in ((qm1, rp1), (qm2, rp2)):
                for h in range(HEADS):
                    ins = V.tensor_scalar(qm[:, h, :], rp[:, 0, :], headmask[:, h:h + 1], None, ALU.mult)
                    if not (rp is rp2 and h == HEADS - 1):
                        link(ins)
            ins.then_inc(S["mla_masked"], 1)

            def attend(n):
                if n >= 1:
                    i = n - 1
                    nk = P * (i % 2 + 1)
                    dve.wait_ge(S["sexp_ready"], i + 1)
                    link(V.reciprocal(small[:, 210 + i % 2:211 + i % 2], small[:, 200 + i:201 + i]))
                    V.tensor_scalar(probs[i % 2][:, 0:nk], probs[i % 2][:, 0:nk], small[:, 210 + i % 2:211 + i % 2], None, ALU.mult).then_inc(S["p_norm"], 1)
                if n < 8:
                    qt = n % 2
                    nk = P * (qt + 1)
                    b = bank[3 + n % 2]
                    dve.wait_ge(S["s_psum"], n + 1)
                    link(V.memset(b[0:CHUNK, nk - CHUNK:nk], MASK_VALUE))
                    link(V.tensor_reduce(small[:, 208 + n % 2:209 + n % 2], b[:, 0:nk], X, ALU.max))
                    V.tensor_scalar(small[:, 192 + n:193 + n], small[:, 208 + n % 2:209 + n % 2], -SM, None, ALU.mult).then_inc(S["smax_ready"], 1)

            decays(1)
            mg = [0]

            def merge(br, j):
                u = mg[0]
                mg[0] += 1
                if j % 2 == 0:
                    dve.wait_ge(S["merge_psum"], u // 2 + 1)
                else:
                    dve.wait_ge(S["chunk_used"], STREAM.index(("wb", br, j // 2)) + 1)
                gate = merge_gate[:, 8 * br + 2 * j:8 * br + 2 * j + 2, :].rearrange(flat)
                dst = acc[:, 2 * j:2 * j + 2, :].rearrange(flat)
                V.tensor_tensor(dst if u < 4 else m_tmp, bank[3 + u % 2][:, :], gate, ALU.mult).then_inc(S["merge_used"], 1)
                dve.wait_ge(S["merge_used"], u + 1)
                if u >= 4:
                    ins = V.tensor_tensor(dst, dst, m_tmp, ALU.add)
                    if u >= 12:
                        ins.then_inc(S["acc_ready"], 1)
                        dve.wait_ge(S["acc_ready"], u - 11)
                    else:
                        link(ins)

            def hv(v, t):
                return v.rearrange("p (a b) -> p a b", b=BLK)[:, :, t:t + 1]

            def finish_scores():
                dve.wait_ge(S["p_ready"], BLK)
                V.tensor_copy(small[:, 503:504], grow[:, 0, 0:1]).then_inc(S["g_ready"], 1)

            def grow_step(t):
                if t == 0:
                    link(V.tensor_copy(decay, hv(hg_f, 0)))
                else:
                    link(V.tensor_tensor(decay, decay, hv(hg_f, t), ALU.mult))
                    V.tensor_tensor(grow[:, :, 0:t], grow[:, :, 0:t], hv(hg_f, t).to_broadcast([P, HB, t]), ALU.mult)
                link(V.tensor_copy(grow[:, :, t:t + 1], hv(hg_k, t)))
                link(V.tensor_tensor(hv(q_inter, t), decay, hv(hg_q, t), ALU.mult))
                if t >= 2:
                    dve.wait_ge(S["p_used"], t - 1)
                V.tensor_tensor(prod[t % 2][:, :, 0:t + 1], grow[:, :, 0:t + 1], hv(hg_q, t).to_broadcast([P, HB, t + 1]), ALU.mult).then_inc(S["p_ready"], 1)

            dve.wait_ge(S["proj_evac"], PROJ.index(("hq", 1)) + 1)
            dve.wait_ge(S["prod_clear"], 2)
            for n in range(9):
                attend(n)
                grow_step(n)
            for u in range(8):
                if 9 + u < BLK:
                    grow_step(9 + u)
                if 9 + u == BLK:
                    finish_scores()
                merge(3 - u // 4, u % 4)
            dve.wait_ge(S["p_used"], BLK)
            for n in range(8):
                ins = V.tensor_tensor(hg_bd[:, n, :].rearrange("p (a b) -> p a b", a=8),
                                      bank[2][:, n * BLK:n * BLK + BLK].unsqueeze(1).to_broadcast([P, 8, BLK]),
                                      blockmask[:, :].unsqueeze(2).to_broadcast([P, 8, BLK]), ALU.mult)
            ins.then_inc(S["bd_ready"], 1)
            merge(1, 0)
            merge(1, 1)

            def states(h):
                st_ = state[h % 2]
                if h >= 2:
                    dve.wait_ge(S["ho_psum"], h - 1)
                for b in range(NBLK):
                    u = 4 * h + b // 4
                    if b % 4 == 0:
                        dve.wait_ge(S["u_psum"], u + 1)
                    ub = bank[U_BANK[u % 4]][:, (b % 4) * P:(b % 4 + 1) * P]
                    if b == 0:
                        ins = V.tensor_copy(st_[:, 0, :], ub)
                    else:
                        ins = V.scalar_tensor_tensor(st_[:, b, :], st_[:, b - 1, :], decay[:, NBLK * h + b, :], ub, ALU.mult, ALU.add)
                    if b % 4 == 3:
                        ins.then_inc(S["u_used"], 1)
                        dve.wait_ge(S["u_used"], u + 1)
                    else:
                        link(ins)
                V.tensor_copy(small[:, 504:505], st_[:, 15, 0:1]).then_inc(S["st_ready"], 1)

            def finish(h):
                dve.wait_ge(S["hss_psum"], h + 1)
                rs = hg_rs[h % 2]
                inverse_root(rs, bank[(7, 2)[h % 2]][:, SEQ:], RMS_EPS, 2 + h)
                link(V.scalar_tensor_tensor(rs, rs, v_("hnorm", h), hg_o[h % 2], ALU.mult, ALU.mult))
                V.tensor_tensor(yT[:, 0, h, :], rs, hg_g[:, h * SEQ:(h + 1) * SEQ], ALU.mult).then_inc(S["yA_ready"], 1)

            states(0)
            states(1)
            for h in range(HEADS):
                if h + 2 < HEADS:
                    states(h + 2)
                elif h == 2:
                    merge(1, 2)
                finish(h)
            dve.wait_ge(S["yA_ready"], HEADS)
            merge(1, 3)
            for j in range(4):
                merge(0, j)
            V.memset(wTd, 0.0)
            V.memset(b2_all, 0.0)
            V.memset(b1_all, 0.0).then_inc(S["b_clear"], 1)
            link(V.memset(rank, -1.0))
            V.tensor_scalar(esel, ones[:, 0:CAP], ident[:, 0:1], None, ALU.mult).then_inc(S["esel_ready"], 1)

            def norm(half, dst, src, nth):
                st_ = small[:, 300:312].rearrange("p (a b) -> p a b", a=2)
                for dh in range(2):
                    link(V.bn_stats(st_[:, dh, :], src[:, half, 512 * dh:512 * dh + 512]))
                link(V.bn_aggr(small[:, 312:314], st_))
                inverse_root(small[:, 314:315], small[:, 313:314], LN_EPS, nth)
                link(V.tensor_scalar(src[:, half, :], src[:, half, :], small[:, 312:313], small[:, 314:315], ALU.subtract, ALU.mult))
                link(V.tensor_tensor(src[:, half, :], src[:, half, :], ln_w, ALU.mult))
                return V.tensor_tensor(dst[:, half, :], src[:, half, :], ln_b, ALU.add)

            dve.wait_ge(S["xres_in"], 16)
            dve.wait_ge(S["ln_in"], 32)
            for half in range(2):
                if half:
                    dve.wait_ge(S["chunk_used"], len(STREAM))
                else:
                    dve.wait_ge(S["mix_psum"], 1)
                for dh in range(2):
                    link(V.scalar_tensor_tensor(x_res[:, half, 512 * dh:512 * dh + 512], x_res[:, half, 512 * dh:512 * dh + 512], ALPHA,
                                                bank[MIX_BANK[half][dh]][:, :], ALU.mult, ALU.add))
                norm(half, h_tok, x_res, 6 + half).then_inc(S["h_ready"], 1)
            dve.wait_ge(S["h_ready"], 2)
            dve.wait_ge(S["logit_psum"], 1)
            dve.wait_ge(S["rb_in"], 16)
            for half in range(2):
                link(V.tensor_tensor(logits[:, half, :], bank[4][:, half * NE:half * NE + NE], rb, ALU.add))
                link(V.max(top[:, half, :], logits[:, half, :]))
                link(V.max_index(top_i[:, half, :], top[:, half, :], logits[:, half, :]))
                ins = V.tensor_scalar(small[:, 232 + half:233 + half], top[:, half, 0:1], -1.0, None, ALU.mult)
                if half == 0:
                    link(ins)
            ins.then_inc(S["topexp_req"], 1)
            link(V.tensor_copy(sm(320, 8).rearrange("p (a b) -> p a b", a=2), top_i[:, :, 0:TOPK]))
            link(V.tensor_tensor(oneh, iota[:, 0:NE].unsqueeze(1).to_broadcast([P, 2 * TOPK, NE]),
                                 sm(320, 8).unsqueeze(2).to_broadcast([P, 2 * TOPK, NE]), ALU.is_equal))
            chosen = [oneh[:, TOPK * half:TOPK * half + TOPK, :].rearrange("p j e -> p e j") for half in range(2)]
            for half in range(2):
                link(V.tensor_reduce(member[:, half, :], chosen[half], X, ALU.add))
            V.tensor_copy(small[:, 505:506], member[:, 1, 31:32]).then_inc(S["member_ready"], 1)
            dve.wait_ge(S["topexp_ready"], 2)
            link(V.reciprocal(small[:, 238:240], small[:, 236:238]))
            link(V.tensor_tensor(sm(216, 8).rearrange("p (a b) -> p a b", a=2), sm(216, 8).rearrange("p (a b) -> p a b", a=2),
                                 small[:, 238:240].unsqueeze(2).to_broadcast([P, 2, TOPK]), ALU.mult))
            link(V.tensor_tensor(oneh, oneh, sm(216, 8).unsqueeze(2).to_broadcast([P, 2 * TOPK, NE]), ALU.mult))
            for half in range(2):
                link(V.tensor_reduce(wfull[:, half, 0:NE], chosen[half], X, ALU.add))
            V.memset(wfull[:, :, NE:NE + 1], 0.0).then_inc(S["route_ready"], 1)
            dve.wait_ge(S["rank_psum"], 1)
            rk_ = rank[:, :, 0:NE]
            link(V.scalar_tensor_tensor(rk_, bank[4][:, 0:2 * NE].rearrange("p (a b) -> p a b", a=2), 1.0, member, ALU.add, ALU.mult))
            link(V.tensor_scalar(rk_, rk_, -1.0, None, ALU.add))

            def select(g, u, e, off=None, unit=True):
                if unit:
                    V.tensor_scalar(esel, ones[:, 0:CAP], ident[:, bass.ds(e, 1)], None, ALU.mult).then_inc(S["esel_ready"], 1)
                for half in range(2):
                    rk = rank[:, half, bass.ds(e, 1)]
                    w = wfull[:, half, bass.ds(e, 1)]
                    if off is None:
                        V.tensor_scalar(sel[:, half, :], iota[:, 0:CAP], rk, None, ALU.is_equal)
                        ins = V.tensor_scalar(wsel[:, half, u * CAP:(u + 1) * CAP], iota[:, 0:CAP], rk, w, ALU.is_equal, ALU.mult)
                    else:
                        link(V.tensor_scalar(sel[:, half, :], iota[:, 0:CAP], off, rk, ALU.add, ALU.is_equal))
                        ins = V.tensor_scalar(wsel[:, half, 0:CAP], sel[:, half, :], w, None, ALU.mult)
                ins.then_inc(S["sel_ready"], 1)

            dve.wait_ge(S["route_ready"], 1)
            select(0, 0, 0, unit=False)
            code = cand[:, 2, :].rearrange("p (a b) -> p a b", b=3)
            for b in range(3):
                link(V.tensor_scalar(cand[:, 0, :].rearrange("p (a b) -> p a b", b=3)[:, :, b:b + 1], bank[4][:, 2 * NE:3 * NE].unsqueeze(2),
                                     float(CAP * (b + 1)), None, ALU.is_gt))
            link(V.tensor_tensor_scan(cand[:, 1, :], ones[:, 0:96], cand[:, 0, :], 0.0, ALU.mult, ALU.add))
            link(V.tensor_copy(small[:, 507:508], cand[:, 1, 95:96]))
            link(V.tensor_tensor(cand[:, 1, :], cand[:, 1, :], cand[:, 0, :], ALU.mult))
            for dst, expert_code in ((item_ef, True), (item_off, False)):
                for b in range(3):
                    link(V.tensor_scalar(code[:, :, b:b + 1], iota[:, 0:NE].unsqueeze(2), 1.0 if expert_code else 0.0,
                                         0.0 if expert_code else float(CAP * (b + 1)), ALU.mult, ALU.add))
                link(V.tensor_scalar(small[:, 340:356], iota[:, 0:NITEM], 1.0, None, ALU.add))
                link(V.tensor_tensor(cmp, cand[:, 1, :].unsqueeze(1).to_broadcast([P, NITEM, 96]),
                                     small[:, 340:356].unsqueeze(2).to_broadcast([P, NITEM, 96]), ALU.is_equal))
                link(V.tensor_tensor(cmp, cmp, cand[:, 2, :].unsqueeze(1).to_broadcast([P, NITEM, 96]), ALU.mult))
                link(V.tensor_reduce(dst, cmp, X, ALU.add))
            link(V.tensor_copy(item_e[0:1, 0:NITEM], item_ef[0:1, :]))
            V.tensor_copy(item_e[0:1, NITEM:NITEM + 1], small[0:1, 507:508]).then_inc(S["items_ready"], 1)
            dve.wait_ge(S["b2_psum"], 1)
            for half in range(2):
                for dh in range(2):
                    link(V.scalar_tensor_tensor(y_acc[:, half, 512 * dh:512 * dh + 512], h_tok[:, half, 512 * dh:512 * dh + 512], ALPHA,
                                                bank[(2, 3, 6, 7)[2 * half + dh]][:, :], ALU.mult, ALU.add))
            V.tensor_copy(small[:, 508:509], y_acc[:, 1, 0:1]).then_inc(S["b2_used"], 1)
            dve.wait_ge(S["items_ready"], 1)

            before = vc[0]

            def swiglu(n, u, hb):
                dve.wait_ge(S["expert_chunk_used"], n * R2S + 8)
                V.tensor_scalar(g1, bank[2 * hb][:, :], LIMIT, None, ALU.min).then_inc(S["gmin_ready"], 1)
                link(V.tensor_scalar(g2, bank[2 * hb + 1][:, :], LIMIT, -LIMIT, ALU.min, ALU.max))
                dve.wait_ge(S["sig_ready"], n + 1)
                link(V.scalar_tensor_tensor(g2, g2, 1.0, g1, ALU.add, ALU.mult))
                V.tensor_tensor(g1, g2, g3, ALU.mult).then_inc(S["act_ready"], 1)
                dve.wait_ge(S["expert_chunk_used"], n * R2S + R2S)
                V.tensor_copy(y_pair[64 * u:64 * u + 64, 512:1024], bank[4][64:128, :]).then_inc(S["ypair_vec"], 1)

            def combine(m_):
                for i in range(4):
                    half, dh = i // 2, i % 2
                    dst = y_acc[:, half, 512 * dh:512 * dh + 512]
                    dve.wait_ge(S["comb_psum"], m_ * 4 + i + 1)
                    V.tensor_tensor(dst, dst, bank[6 + i % 2][:, :], ALU.add).then_inc(S["comb_used"], 1)

            with dve.Fori(0, NPAIR) as p:
                base[0] = p * 4
                dve.wait_ge(S["xg_psum"], p * 2 + 1)
                select(p * 2 + 1, 1, p * 2 + 1)
                swiglu(p * 2, 0, 0)
                dve.wait_ge(S["xg_psum"], p * 2 + 2)
                dve.wait_ge(S["wselT_psum"], p + 1)
                select(p * 2 + 2, 0, p * 2 + 2)
                swiglu(p * 2 + 1, 1, 1)
                combine(p)
            per_pair = vc[0] - before
            assert per_pair == 4, per_pair
            n_items = dve.value_load(item_e[0:1, NITEM:NITEM + 1], min_val=0, max_val=NITEM)
            before = vc[0]
            with dve.If(n_items > 0):
                with dve.Fori(0, n_items) as j:
                    base[0] = j * 4 + (NPAIR - 1) * 4
                    e = dve.value_load(item_e[0:1, bass.ds(j, 1)], min_val=0, max_val=NE - 1)
                    select(j + NE + 1, 0, e, item_off[:, bass.ds(j, 1)])
                    swiglu(j + NE, 0, 1)
                    combine(j + NPAIR)
            assert vc[0] - before == 4, vc[0] - before
            dve.wait_ge(S["ln2_in"], 32)
            tail[0] = True

            for half in range(2):
                st_ = small[:, 300:312].rearrange("p (a b) -> p a b", a=2)
                src = y_acc
                for dh in range(2):
                    link(V.bn_stats(st_[:, dh, :], src[:, half, 512 * dh:512 * dh + 512]))
                link(V.bn_aggr(small[:, 312:314], st_))
                inverse_root(small[:, 314:315], small[:, 313:314], LN_EPS, 8 + half)
                link(V.tensor_scalar(src[:, half, :], src[:, half, :], small[:, 312:313], small[:, 314:315], ALU.subtract, ALU.mult))
                link(V.tensor_tensor(src[:, half, :], src[:, half, :], ln_w, ALU.mult))
                ins = V.tensor_tensor(src[:, half, :], src[:, half, :], ln_b, ALU.add)
                ins.then_inc(S["out_ready"], 1)


SHAPES = {
    "x": None, "positions": None, "w_in": (1024, 8128), "b_gate": (32, 128), "hgrn_lb_logits": (4, 128), "hgrn_norm_w": (4, 128),
    "mla_q_norm_w": (2, 128), "mla_wq_b": (256, 768), "mla_kv_norm_w": (1, 128), "mla_wkv_b": (128, 1024),
    "s5_a_re": (16, 128), "s5_a_im": (16, 128), "s5_log_dt": (16, 2), "s5_b_re": (2048, 16), "s5_b_im": (2048, 16),
    "s5_c_re": (512, 64), "s5_c_im": (512, 64), "s5_d": (4, 128), "s5_w_glu": (512, 512), "s5_b_glu": (4, 128),
    "lru_conv_w": (16, 128), "lru_conv_b": (4, 128), "lru_wa": (8, 64, 64), "lru_ba": (4, 128), "lru_wx": (8, 64, 64), "lru_bx": (4, 128),
    "lru_a_param": (4, 128), "w_branch": (4, 512, 1024), "w_out": (1024, 1024), "ln1_w": (1, 1024), "ln1_b": (1, 1024),
    "ln2_w": (1, 1024), "ln2_b": (1, 1024), "router_w": (1024, 32), "router_b": (1, 32),
    "moe_w1": (32, 1024, 2048), "moe_b1": (32, 2048), "moe_w2": (32, 1024, 1024), "moe_b2": (32, 1024),
}


def kernel(**inputs):
    import numpy as _np
    import concourse.bacc as _bacc
    from concourse import mybir as _mybir
    from concourse.bass_utils import run_bass_kernel_spmd as _run

    nc = _bacc.Bacc("TRN2", target_bir_lowering=False, num_devices=1)
    arrays, aps = {}, {}
    for name, shape in SHAPES.items():
        a = _np.ascontiguousarray(inputs[name])
        if shape is not None:
            a = a.reshape(shape)
        arrays["in_" + name] = a
    freq = _np.float32(10000.0) ** (-_np.arange(0, ROPE, 2, dtype=_np.float32) / _np.float32(ROPE))
    arrays["in_inv_freq"] = _np.ascontiguousarray(_np.tile(freq, HEADS).reshape(P, 1).astype(_np.float32))
    for name, a in arrays.items():
        aps[name[3:]] = nc.dram_tensor(name, a.shape, _mybir.dt.from_np(a.dtype), kind="ExternalInput").ap()
    out = nc.dram_tensor("out", (1, SEQ, D), F32, kind="ExternalOutput").ap()
    encoder_layer(nc, aps, out)
    r = _run(nc, [arrays], core_ids=[0])
    return r.results[0]["out"]
```
